# Optimizing a Trainium2 kernel written in Bass

```python
import jax, jax.numpy as jnp
from jax import lax
import numpy as np

D_MODEL = 1024
BATCH = 1
SEQ = 1024
DEPTH = 1
DEC_BATCH = 8
DEC_SEQ = 8
PAST_LEN = 512
PAGE_SIZE = 128

CHUNK = 128
A_WIDTH = D_MODEL
A_GROUPS = 8
A_GROUP_DIM = A_WIDTH // A_GROUPS
HEAD_DIM = 64
HEADS_PER_GROUP = 4
DILATED_GROUPS = ((128, 1), (512, 4), (2048, 16))
N_ATTN_HEADS = HEADS_PER_GROUP * len(DILATED_GROUPS)
ATTN_WIDTH = N_ATTN_HEADS * HEAD_DIM
B_OUT = HEADS_PER_GROUP * HEAD_DIM
ROPE_DIM = HEAD_DIM // 4
ROPE_THETA = 500000.0
SCALE = HEAD_DIM ** -0.5
SPLIT_POINTS = (A_WIDTH, 2 * A_WIDTH, 2 * A_WIDTH + ATTN_WIDTH, 2 * A_WIDTH + 2 * ATTN_WIDTH,
                2 * A_WIDTH + 3 * ATTN_WIDTH, 2 * A_WIDTH + 3 * ATTN_WIDTH + D_MODEL)
IN_COLS = 2 * A_WIDTH + 3 * ATTN_WIDTH + 2 * D_MODEL
N_EXPERT_GROUPS = 4
EXPERTS_PER_GROUP = 8
N_EXPERTS = N_EXPERT_GROUPS * EXPERTS_PER_GROUP
TOP_K_INNER = 2
D_EXPERT = D_MODEL // 2
MOE_BLOCK = 128
EPS = 1e-6
NEG_INF = -1e30

kernel_name = 'hybrid_sgu_dilated_attn_hmoe_step'

def rmsnorm(x, g):
    xf = x.astype(jnp.float32)
    r = lax.rsqrt(jnp.mean(xf * xf, axis=-1, keepdims=True) + EPS)
    return (xf * r * g.astype(jnp.float32)).astype(x.dtype)

def rope(x, pos):
    half = ROPE_DIM // 2
    inv = jnp.float32(ROPE_THETA) ** (-jnp.arange(half, dtype=jnp.float32) * 2.0 / ROPE_DIM)
    ang = pos.astype(jnp.float32)[:, None] * inv[None, :]
    cos, sin = jnp.cos(ang)[:, None, :], jnp.sin(ang)[:, None, :]
    xr = x[..., :ROPE_DIM].astype(jnp.float32)
    x1, x2 = xr[..., :half], xr[..., half:]
    rot = jnp.concatenate([x1 * cos - x2 * sin, x2 * cos + x1 * sin], axis=-1).astype(x.dtype)
    return jnp.concatenate([rot, x[..., ROPE_DIM:]], axis=-1)

def mixer_inputs(x, norm_g, w_in):
    xn = rmsnorm(x, norm_g)
    z = jnp.einsum('bsd,dc->bsc', xn, w_in)
    u, v, q, k, va, ga, gb = jnp.split(z, SPLIT_POINTS, axis=-1)
    return jax.nn.gelu(u), jax.nn.gelu(v), q, k, va, ga, gb

def sgu(u, v, v_norm_g, w_s, b_s):
    b, s, _ = u.shape
    lc = min(s, CHUNK)
    vn = rmsnorm(v, v_norm_g)
    vc = vn.reshape(b, s // lc, lc, A_GROUPS, A_GROUP_DIM)
    wm = jnp.tril(w_s[:, :lc, :lc])
    f = jnp.einsum('gts,bnsgc->bntgc', wm, vc) + b_s[:, :lc].T[None, None, :, :, None]
    return u * f.reshape(b, s, A_WIDTH), vn

def attn_heads(q, k, va, q_g, k_g, pos):
    b, s, _ = q.shape
    shp = (b, s, N_ATTN_HEADS, HEAD_DIM)
    qh = rope(rmsnorm(q.reshape(shp), q_g), pos)
    kh = rope(rmsnorm(k.reshape(shp), k_g), pos)
    return qh, kh, va.reshape(shp)

def dilated_attn_prompt(q, k, v, window, dil):
    b, s, h, d = q.shape
    blk = window // dil
    n_sub = s // dil
    nb = -(-n_sub // blk)
    pad = nb * blk - n_sub

    def sub(a):
        a = a.reshape(b, n_sub, dil, h, d)
        return jnp.pad(a, ((0, 0), (0, pad), (0, 0), (0, 0), (0, 0)))

    def band(a):
        a = jnp.pad(sub(a), ((0, 0), (blk, 0), (0, 0), (0, 0), (0, 0))).reshape(b, nb + 1, blk, dil, h, d)
        return jnp.concatenate([a[:, :-1], a[:, 1:]], axis=2)

    qb = sub(q).reshape(b, nb, blk, dil, h, d)
    kb, vb = band(k), band(v)
    sc = jnp.einsum('bnqrhd,bnkrhd->bnrhqk', qb, kb).astype(jnp.float32) * SCALE
    qi = jnp.arange(blk)[:, None]
    kj = jnp.arange(2 * blk)[None, :]
    dist = qi + blk - kj
    key_sub = (jnp.arange(nb)[:, None, None] - 1) * blk + kj[None]
    valid = ((dist >= 0) & (dist <= blk))[None] & (key_sub >= 0)
    sc = jnp.where(valid[None, :, None, None], sc, NEG_INF)
    lse = jax.nn.logsumexp(sc, axis=-1)
    p = jnp.exp(sc - lse[..., None]).astype(v.dtype)
    o = jnp.einsum('bnrhqk,bnkrhd->bnqrhd', p, vb)
    o = o.reshape(b, nb * blk, dil, h, d)[:, :n_sub].reshape(b, s, h, d)
    lse = lse.transpose(0, 1, 4, 2, 3).reshape(b, nb * blk, dil, h)[:, :n_sub].reshape(b, s, h)
    return o, lse

def dilated_attn_sample(q, k_all, v_all, window, dil):
    t = q.shape[1]
    n_past = k_all.shape[1] - t
    n_keys = window // dil + 1
    idx = n_past + jnp.arange(t)[:, None] - dil * jnp.arange(n_keys)[None, :]
    valid = idx >= 0
    idx = jnp.maximum(idx, 0)
    kg, vg = k_all[:, idx], v_all[:, idx]
    sc = jnp.einsum('bthd,btnhd->bthn', q, kg).astype(jnp.float32) * SCALE
    sc = jnp.where(valid[None, :, None, :], sc, NEG_INF)
    lse = jax.nn.logsumexp(sc, axis=-1)
    p = jnp.exp(sc - lse[..., None]).astype(v_all.dtype)
    return jnp.einsum('bthn,btnhd->bthd', p, vg), lse

def combine_groups(outs, lses):
    alpha = jax.nn.softmax(jnp.stack(lses, axis=0), axis=0)
    o = jnp.sum(alpha[..., None] * jnp.stack(outs, axis=0).astype(jnp.float32), axis=0)
    b, s = o.shape[0], o.shape[1]
    return o.astype(outs[0].dtype).reshape(b, s, B_OUT)

def branch_merge(x, a_out, b_out, ga, gb, w_proj_a, w_proj_b, w_out):
    m = jax.nn.sigmoid(ga) * (a_out @ w_proj_a) + jax.nn.sigmoid(gb) * (b_out @ w_proj_b)
    return x + m @ w_out

def grouped_experts(xn, eid, wt, w_gate, w_up, w_down):
    n_tok, d = xn.shape
    n_asg = eid.shape[0]
    tok = jnp.arange(n_asg) // TOP_K_INNER
    order = jnp.argsort(eid)
    se, stok, sw = eid[order], tok[order], wt[order]
    counts = jax.ops.segment_sum(jnp.ones((n_asg,), jnp.int32), eid, num_segments=N_EXPERTS)
    start = jnp.cumsum(counts) - counts
    pcounts = (counts + MOE_BLOCK - 1) // MOE_BLOCK * MOE_BLOCK
    pend = jnp.cumsum(pcounts)
    pstart = pend - pcounts
    dest = pstart[se] + jnp.arange(n_asg) - start[se]
    n_blocks = -(-(n_asg + N_EXPERTS * (MOE_BLOCK - 1)) // MOE_BLOCK)
    n_slots = n_blocks * MOE_BLOCK
    slot_tok = jnp.zeros((n_slots,), jnp.int32).at[dest].set(stok)
    slot_w = jnp.zeros((n_slots,), jnp.float32).at[dest].set(sw)
    block_e = jnp.clip(jnp.searchsorted(pend, jnp.arange(n_blocks) * MOE_BLOCK, side='right'), 0, N_EXPERTS - 1)
    xb = xn[slot_tok].reshape(n_blocks, MOE_BLOCK, d)

    def expert_block(args):
        xblk, e = args
        hid = jax.nn.silu(xblk @ w_gate[e]) * (xblk @ w_up[e])
        return hid @ w_down[e]

    yb = lax.map(expert_block, (xb, block_e)).reshape(n_slots, d)
    yb = (yb.astype(jnp.float32) * slot_w[:, None]).astype(xn.dtype)
    return jax.ops.segment_sum(yb, slot_tok, num_segments=n_tok)

def channel_mix(h, norm_g, w_gr, b_gr, w_er, b_er, w_gate, w_up, w_down):
    b, s, d = h.shape
    xn = rmsnorm(h, norm_g).reshape(b * s, d)
    lg = (xn @ w_gr).astype(jnp.float32) + b_gr.astype(jnp.float32)
    grp = jnp.argmax(lg, axis=-1)
    p_grp = jnp.take_along_axis(jax.nn.softmax(lg, axis=-1), grp[:, None], axis=-1)[:, 0]
    le = jnp.einsum('td,dge->tge', xn, w_er).astype(jnp.float32) + b_er.astype(jnp.float32)
    le = jnp.take_along_axis(le, grp[:, None, None], axis=1)[:, 0]
    top_v, top_i = lax.top_k(le, TOP_K_INNER)
    wt = p_grp[:, None] * jax.nn.softmax(top_v, axis=-1)
    eid = grp[:, None] * EXPERTS_PER_GROUP + top_i
    y = grouped_experts(xn, eid.reshape(-1), wt.reshape(-1), w_gate, w_up, w_down)
    return h + y.reshape(b, s, d)

def setup_inputs(seed: int = 0) -> dict:
    key = jax.random.key(seed)
    ks = jax.random.split(key, 32)

    def nrm(k, shape, scale):
        return jax.random.normal(k, shape, jnp.float32) * scale

    def buf(k, w):
        return nrm(k, (DEPTH, DEC_BATCH, min(w, PAST_LEN), HEADS_PER_GROUP, HEAD_DIM), 1.0)

    return {
        'x_prompt': nrm(ks[0], (BATCH, SEQ, D_MODEL), 1.0),
        'x_sample': nrm(ks[1], (DEC_BATCH, DEC_SEQ, D_MODEL), 1.0),
        'cache_k_w128': buf(ks[2], 128),
        'cache_v_w128': buf(ks[3], 128),
        'cache_k_w512': buf(ks[4], 512),
        'cache_v_w512': buf(ks[5], 512),
        'cache_k_w2048': buf(ks[6], 2048),
        'cache_v_w2048': buf(ks[7], 2048),
        'norm1_g': 1.0 + nrm(ks[8], (DEPTH, D_MODEL), 0.05),
        'w_in': nrm(ks[9], (DEPTH, D_MODEL, IN_COLS), D_MODEL ** -0.5),
        'v_norm_g': 1.0 + nrm(ks[10], (DEPTH, A_WIDTH), 0.05),
        'w_spatial': nrm(ks[11], (DEPTH, A_GROUPS, CHUNK, CHUNK), CHUNK ** -0.5),
        'b_spatial': 1.0 + nrm(ks[12], (DEPTH, A_GROUPS, CHUNK), 0.1),
        'q_norm_g': 1.0 + nrm(ks[13], (DEPTH, HEAD_DIM), 0.05),
        'k_norm_g': 1.0 + nrm(ks[14], (DEPTH, HEAD_DIM), 0.05),
        'w_proj_a': nrm(ks[15], (DEPTH, A_WIDTH, D_MODEL), A_WIDTH ** -0.5),
        'w_proj_b': nrm(ks[16], (DEPTH, B_OUT, D_MODEL), B_OUT ** -0.5),
        'w_out': nrm(ks[17], (DEPTH, D_MODEL, D_MODEL), D_MODEL ** -0.5),
        'norm2_g': 1.0 + nrm(ks[18], (DEPTH, D_MODEL), 0.05),
        'w_group_router': nrm(ks[19], (DEPTH, D_MODEL, N_EXPERT_GROUPS), D_MODEL ** -0.5),
        'b_group_router': nrm(ks[20], (DEPTH, N_EXPERT_GROUPS), 0.01),
        'w_expert_router': nrm(ks[21], (DEPTH, D_MODEL, N_EXPERT_GROUPS, EXPERTS_PER_GROUP), D_MODEL ** -0.5),
        'b_expert_router': nrm(ks[22], (DEPTH, N_EXPERT_GROUPS, EXPERTS_PER_GROUP), 0.01),
        'w_gate': nrm(ks[23], (DEPTH, N_EXPERTS, D_MODEL, D_EXPERT), D_MODEL ** -0.5),
        'w_up': nrm(ks[24], (DEPTH, N_EXPERTS, D_MODEL, D_EXPERT), D_MODEL ** -0.5),
        'w_down': nrm(ks[25], (DEPTH, N_EXPERTS, D_EXPERT, D_MODEL), D_EXPERT ** -0.5),
    }

def reference(x_prompt, x_sample, cache_k_w128, cache_v_w128, cache_k_w512, cache_v_w512,
              cache_k_w2048, cache_v_w2048, norm1_g, w_in, v_norm_g, w_spatial, b_spatial,
              q_norm_g, k_norm_g, w_proj_a, w_proj_b, w_out, norm2_g, w_group_router,
              b_group_router, w_expert_router, b_expert_router, w_gate, w_up, w_down):
    cache_k = (cache_k_w128, cache_k_w512, cache_k_w2048)
    cache_v = (cache_v_w128, cache_v_w512, cache_v_w2048)
    n_g = len(DILATED_GROUPS)
    pk, pv = [[] for _ in range(n_g)], [[] for _ in range(n_g)]
    sk, sv = [[] for _ in range(n_g)], [[] for _ in range(n_g)]
    sgu_rows = []
    hp, hs = x_prompt, x_sample
    s_p, s_s = x_prompt.shape[1], x_sample.shape[1]
    pos_p = jnp.arange(s_p)
    pos_s = PAST_LEN + jnp.arange(s_s)
    for l in range(DEPTH):
        u, v, q, k, va, ga, gb = mixer_inputs(hp, norm1_g[l], w_in[l])
        a_out, _ = sgu(u, v, v_norm_g[l], w_spatial[l], b_spatial[l])
        qh, kh, vh = attn_heads(q, k, va, q_norm_g[l], k_norm_g[l], pos_p)
        outs, lses = [], []
        for g, (win, dil) in enumerate(DILATED_GROUPS):
            hsl = slice(g * HEADS_PER_GROUP, (g + 1) * HEADS_PER_GROUP)
            o, lse = dilated_attn_prompt(qh[:, :, hsl], kh[:, :, hsl], vh[:, :, hsl], win, dil)
            outs.append(o)
            lses.append(lse)
            keep = min(win, s_p)
            pk[g].append(kh[:, s_p - keep:, hsl])
            pv[g].append(vh[:, s_p - keep:, hsl])
        hp = branch_merge(hp, a_out, combine_groups(outs, lses), ga, gb, w_proj_a[l], w_proj_b[l], w_out[l])
        hp = channel_mix(hp, norm2_g[l], w_group_router[l], b_group_router[l], w_expert_router[l],
                         b_expert_router[l], w_gate[l], w_up[l], w_down[l])
        u, v, q, k, va, ga, gb = mixer_inputs(hs, norm1_g[l], w_in[l])
        a_out, vn_new = sgu(u, v, v_norm_g[l], w_spatial[l], b_spatial[l])
        sgu_rows.append(vn_new)
        qh, kh, vh = attn_heads(q, k, va, q_norm_g[l], k_norm_g[l], pos_s)
        outs, lses = [], []
        for g, (win, dil) in enumerate(DILATED_GROUPS):
            hsl = slice(g * HEADS_PER_GROUP, (g + 1) * HEADS_PER_GROUP)
            k_all = jnp.concatenate([cache_k[g][l].astype(kh.dtype), kh[:, :, hsl]], axis=1)
            v_all = jnp.concatenate([cache_v[g][l].astype(vh.dtype), vh[:, :, hsl]], axis=1)
            o, lse = dilated_attn_sample(qh[:, :, hsl], k_all, v_all, win, dil)
            outs.append(o)
            lses.append(lse)
            keep = min(win, k_all.shape[1])
            sk[g].append(k_all[:, k_all.shape[1] - keep:])
            sv[g].append(v_all[:, v_all.shape[1] - keep:])
        hs = branch_merge(hs, a_out, combine_groups(outs, lses), ga, gb, w_proj_a[l], w_proj_b[l], w_out[l])
        hs = channel_mix(hs, norm2_g[l], w_group_router[l], b_group_router[l], w_expert_router[l],
                         b_expert_router[l], w_gate[l], w_up[l], w_down[l])
    pk = [jnp.stack(a, axis=0) for a in pk]
    pv = [jnp.stack(a, axis=0) for a in pv]
    sk = [jnp.stack(a, axis=0) for a in sk]
    sv = [jnp.stack(a, axis=0) for a in sv]
    state_sgu_v_sample = jnp.stack(sgu_rows, axis=0)
    return (hp, hs, pk[0], pv[0], pk[1], pv[1], pk[2], pv[2],
            sk[0], sv[0], sk[1], sv[1], sk[2], sv[2], state_sgu_v_sample)


_drawn_inputs = setup_inputs


def setup_inputs(seed=0):
    import zlib

    import numpy as np

    out = dict(_drawn_inputs(seed))
    spreads = {}
    factors = {'q_norm_g': 5.563, 'b_group_router': 6.315, 'b_expert_router': 11.054}
    for name, (base, spread) in spreads.items():
        noise = np.random.default_rng([zlib.crc32(name.encode()), seed]).standard_normal(out[name].shape)
        drawn = base * np.exp(spread * noise) if base else spread * noise
        out[name] = __import__('jax').numpy.asarray(drawn.astype(out[name].dtype))
    for name, factor in factors.items():
        out[name] = (out[name] * factor).astype(out[name].dtype)
    return out
```

```python
from contextlib import ExitStack

import numpy as np
import concourse.bass as bass
from concourse import mybir

F32 = mybir.dt.float32
F32R = mybir.dt.float32r
BF16 = mybir.dt.bfloat16
I32 = mybir.dt.int32
ALU = mybir.AluOpType
ACT = mybir.ActivationFunctionType
AX = mybir.AxisListType

P = 128
D = 1024
KT = D // P
NPROMPT, NB, NS, PAST = 1024, 8, 8, 512
NSAMP = NB * NS
T = NPROMPT + NSAMP
NTILE = NPROMPT // P
TILES = NTILE + 1
ST = NTILE
HD, NH = 64, 4
GW = HD * NH
DIL = ((128, 1), (512, 4), (2048, 16))
NG = len(DIL)
KEEP = [min(w, NPROMPT) for w, _ in DIL]
PKEEP = [min(w, PAST) for w, _ in DIL]
SKEEP = [min(w, PAST + NS) for w, _ in DIL]
AG = 8
C_U, C_V, C_Q = 0, D, 2 * D
C_K, C_VA = C_Q + NG * GW, C_Q + 2 * NG * GW
C_GA = C_Q + 3 * NG * GW
C_GB = C_GA + D
WB = 256
NEG, EGE = 4, 8
NE = NEG * EGE
DE = D // 2
RW = NEG + NE
OVER = 16
SLOTB = NE + OVER
EPS = 1e-6
SCALE = HD ** -0.5
BIG = 1e30
SKT = [1, 4, 2]
SNK = [P * k + NS for k in SKT]
CHUNK = [(NSAMP, 512), (NSAMP + 512, 512), (0, NSAMP)]

(CI, CROPEC, CROPES, CBD, CREP, CTRIL, CCODE4, CCODE8, CE128, CTHR, CBLK, CVALID, CEPS, CONE, CEND) = np.cumsum(
    [0, P, TILES * 16, TILES * 16, NB, NSAMP, P, NEG, EGE, NE, 8, OVER, TILES, 1, P]).tolist()
(BI, BPO, BPAIR, BS0, BS1, BS2, BLT, BONE, BLS, BLI, BEND) = np.cumsum(
    [0, P, 2 * P, P, SNK[0], SNK[1], SNK[2], P, P, NE, NE]).tolist()


def col0(t):
    return 0 if t == ST else NSAMP + P * t


def constants():
    c = np.zeros((P, CEND), np.float32)
    p = np.arange(P)
    c[:, CI:CI + P] = np.eye(P)
    inv = np.float32(500000.0) ** (-np.arange(8, dtype=np.float32) * np.float32(2.0) / np.float32(16))
    for t in range(TILES):
        pos = (PAST + p % NS if t == ST else P * t + p).astype(np.float32)
        ang = (pos[:, None] * inv[None, :]).astype(np.float32)
        co, si = np.cos(ang), np.sin(ang)
        c[:, CROPEC + 16 * t:CROPEC + 16 * t + 16] = np.concatenate([co, co], 1)
        c[:, CROPES + 16 * t:CROPES + 16 * t + 16] = np.concatenate([si, -si], 1)
    c[:NSAMP, CBD:CBD + NB] = (p[:NSAMP, None] // NS == np.arange(NB)[None])
    c[:NS, CREP:CREP + NSAMP] = (p[:NS, None] == np.arange(NSAMP)[None] % NS)
    c[:, CTRIL:CTRIL + P] = (p[None, :] >= p[:, None])
    c[:, CCODE4:CCODE4 + NEG] = NEG - np.arange(NEG)
    c[:, CCODE8:CCODE8 + EGE] = EGE - np.arange(EGE)
    c[:, CE128:CE128 + NE] = P * np.arange(NE)
    c[:, CTHR:CTHR + 8] = P * (1 + np.arange(8)) + 0.5
    c[:, CBLK:CBLK + OVER] = np.arange(OVER) + 0.5
    c[:, CVALID:CVALID + TILES] = 1
    c[NSAMP:, CVALID + ST] = 0
    c[:, CEPS] = EPS
    c[:, CONE:CONE + P] = 1
    b = np.zeros((P, BEND), np.float32)
    b[:, BI:BI + P] = np.eye(P)
    b[:, BPO:BPO + P] = np.where(p[None, :] >= p[:, None], 0, -BIG)
    b[:, BPO + P:BPO + 2 * P] = np.where(p[None, :] <= p[:, None], 0, -BIG)
    same = p[None, :] // 64 == p[:, None] // 64
    b[:, BPAIR:BPAIR + P] = np.where(same & (p[None, :] <= p[:, None]), 0, -BIG)
    step = (p % 32) % NS
    for g, off in enumerate((BS0, BS1, BS2)):
        win, dil = DIL[g]
        nc_ = P * SKT[g]
        n = np.arange(nc_)
        key = (n // NS) * 16 + n % NS if g == 2 else n
        key = np.concatenate([key, PKEEP[g] + np.arange(NS)])
        dist = PKEEP[g] + step[:, None] - key[None, :]
        ok = (dist >= 0) & (dist <= win) & (dist % dil == 0)
        b[:, off:off + SNK[g]] = np.where(ok, 0, -BIG)
    b[:, BLT:BLT + P] = (p[:, None] < p[None, :])
    b[:, BONE:BONE + P] = 1
    e = np.arange(NE)
    b[:NE, BLS:BLS + NE] = e[:, None] < e[None, :]
    b[:NE, BLI:BLI + NE] = e[:, None] <= e[None, :]
    ids = np.zeros((P, TILES), np.int32)
    for t in range(TILES):
        ids[:, t] = col0(t) + p
    return {"c_f32": c, "c_bf16": b, "c_ids": ids}


class Steps:

    def __init__(self, eng, sem):
        self.eng, self.sem, self.n = eng, sem, 0

    def done(self, ins):
        ins.then_inc(self.sem, 1)
        self.n += 1
        return self.n

    def then_wait(self, ins):
        self.eng.wait_ge(self.sem, self.done(ins))


def build(nc, a, o):
    ctx = ExitStack()
    with ctx:
        _build(nc, ctx, a, o)


def _build(nc, ctx, a, o):
    def sb(name, shape, dt=F32):
        return ctx.enter_context(nc.sbuf_tensor(name, shape, dt))

    def sem(name):
        return ctx.enter_context(nc.semaphore(name))

    def dram(name, shape, dt=F32):
        return nc.dram_tensor(name, shape, dt).ap()

    a_d = dram("a_scratch", [AG, P, T])
    sg_d = dram("gate_scratch", [2, KT, P, T])
    v_d = dram("v_scratch", [T, NG * GW])
    ao_d = dram("attn_scratch", [T, NG, NH, HD + 2])
    xn_d = dram("xn2_scratch", [T, D])
    tok_d = dram("slot_token_scratch", [P * SLOTB, 1], I32)
    y_d = dram("expert_out_scratch", [SLOTB * P, D])

    cst = sb("cst", [P, CEND])
    cbf = sb("cbf", [P, BEND], BF16)
    ids = sb("ids", [P, TILES], I32)
    ident = cst[:, CI:CI + P]
    identb = cbf[:, BI:BI + P]
    eps = cst[:, CEPS:CEPS + 1]
    g1T = sb("g1T", [P, KT])
    qg = sb("qg", [P, 2, HD])

    NA = 50600
    ARENA = nc.sbuf_base
    arena = sb("arena", [P, NA])
    assert nc.sbuf_base - ARENA == 4 * NA
    parts = []

    class Lay:
        def __init__(self, at):
            self.at = at

        def take(self, *shape, dt=F32):
            n = int(np.prod(shape))
            parts.append(self.at)
            v = nc.alloc_sbuf_tensor_at(f"part{len(parts)}", [P, n], dt, offset=ARENA + 4 * self.at)[:, :]
            self.at += -(-n // 8) * 8
            assert self.at <= NA, self.at
            if len(shape) == 2:
                v = v.rearrange("p (a b) -> p a b", b=shape[1])
            elif len(shape) == 3:
                v = v.rearrange("p (a b c) -> p a b c", b=shape[1], c=shape[2])
            return v

    lay = Lay(0)
    xT = [lay.take(KT, T, dt=F32R), lay.take(KT, T, dt=F32R)]
    WSLOT = 10 * WB
    wraw = lay.take(WSLOT)
    whi = [lay.take(WSLOT, dt=F32R) for _ in range(2)]
    wlo = [lay.take(WSLOT, dt=F32R) for _ in range(2)]
    AFTER_W = lay.at
    l1 = Lay(AFTER_W)
    xin = [l1.take(D) for _ in range(2)]
    xs = [l1.take(D) for _ in range(2)]
    xfull = l1.take(KT, P)
    junk1 = l1.take(D)
    l2 = Lay(l1.at)
    vn = l2.take(TILES, D)
    l2b = Lay(AFTER_W)
    gvb = l2b.take(D)
    bsr = l2b.take(AG, P)
    junk2 = l2b.take(D)
    wsp = l2b.take(AG, P)
    wmT = l2b.take(AG, P)
    wmS = l2b.take(AG, NSAMP)
    assert l2b.at <= l1.at
    ug = [l2.take(512) for _ in range(3)]
    ast = [l2.take(512) for _ in range(3)]
    vst = [l2.take(GW) for _ in range(4)]
    zrow = Lay(NA - 512).take(512)
    assert l2.at <= NA - 512
    l3 = Lay(AFTER_W)
    qT = l3.take(6, NPROMPT)
    kT = l3.take(6, NPROMPT)
    qTs = l3.take(6, NSAMP)
    kTs = l3.take(6, NSAMP)
    AFTER_QK = l3.at
    qn = [l3.take(GW) for _ in range(4)]
    sq = [l3.take(GW) for _ in range(2)]
    rt = [[l3.take(NH, 16) for _ in range(2)] for _ in range(2)]
    sgs = [l3.take(512) for _ in range(4)]
    assert l3.at <= NA - 512
    la = Lay(AFTER_QK)
    vg = [la.take(2, GW) for _ in range(2)]
    Eb = [la.take(NH, 2 * P) for _ in range(2)]
    Pt = [la.take(NH * 2, P) for _ in range(2)]
    ob = [la.take(NH, HD + 2) for _ in range(4)]
    ls = Lay(0)
    kc = [ls.take(4, GW) for _ in range(2)]
    vc = [ls.take(4, GW) for _ in range(2)]
    KTs = [ls.take(2, 512) for _ in range(2)]
    Es = [ls.take(528) for _ in range(2)]
    PTs = [ls.take(5, P) for _ in range(2)]
    qpad = ls.take(6, 2 * NB, 32)
    vnew = ls.take(NB, NG * GW)
    osb = ls.take(NB * NG, HD + 2)
    assert ls.at <= AFTER_W
    lc = Lay(AFTER_QK)
    co = [lc.take(NG * NH, HD + 2) for _ in range(2)]
    cb = [lc.take(NG, GW) for _ in range(2)]
    cs = [lc.take(8, NH) for _ in range(2)]
    lm = Lay(AFTER_W)
    mT = lm.take(KT, T)
    bT = [lm.take(2, T, dt=F32R), lm.take(2, T, dt=F32R)]
    assert lm.at <= AFTER_QK
    lm2 = Lay(lc.at)
    sga = [lm2.take(512) for _ in range(2)]
    sgb = [lm2.take(512) for _ in range(2)]
    aT = xT
    lw = Lay(0)
    wo = [lw.take(KT, D, dt=F32R), lw.take(KT, D, dt=F32R)]
    assert lw.at <= 2 * KT * T
    AFTER_M = AFTER_W + KT * T
    lh = Lay(AFTER_M)
    hbuf = lh.take(TILES, D)
    AFTER_H = lh.at
    xr = [lh.take(D) for _ in range(2)]
    wr = lh.take(KT, RW)
    rbias = lh.take(RW)
    lh2 = Lay(2 * KT * T + WSLOT)
    mh = [lh2.take(KT, P, dt=F32R) for _ in range(2)]
    ml = [lh2.take(KT, P, dt=F32R) for _ in range(2)]
    x2 = [lh2.take(D) for _ in range(2)]
    x2T = [lh2.take(KT, P) for _ in range(2)]
    junk3 = lh2.take(D)
    g2b = lh2.take(D)
    assert lh2.at <= AFTER_W
    lgt = sb("lgt", [P, TILES, RW])
    slot = sb("slot", [P, TILES, 2], I32)
    wts = sb("wts", [P, TILES, 2])
    small = sb("small", [P, 8, TILES])
    tabs = sb("tabs", [P, SLOTB], I32)
    obe = sb("obe", [P, 24], I32)
    idxc = sb("idxc", [P, 1], I32)
    stat = sb("stat", [P, 8, NH])
    nm = sb("nm", [P, 2, NH])
    snm = sb("snm", [P, 2])
    lr = Lay(AFTER_W)
    R = {n: lr.take(TILES, w) for n, w in (
        ("m4", 1), ("d4", NEG), ("s4", 1), ("eq4", NEG), ("oh4", NEG), ("c4", 1), ("pg", 1),
        ("sel", EGE), ("t8", EGE), ("m1", 1), ("c8", 1), ("oh1", EGE), ("le2", EGE), ("m2", 1),
        ("oh2", EGE), ("ex", 1), ("dn", 1), ("E1", NE), ("E2", NE), ("A", NE), ("rank", NE),
        ("over", NE), ("pos", NE), ("pr", NE), ("sl", 2), ("rowf", 2), ("blkf", 2))}
    prod48 = lr.take(TILES * NEG, EGE)[:, :, :].rearrange("p (t g) e -> p t g e", g=NEG)
    Abf = lr.take(TILES * NE)[:, :].bitcast(BF16)[:, 0:TILES * NE].rearrange("p (a b) -> p a b", b=NE)
    cnt = lr.take(8)
    nbt = lr.take(8)
    nbb = lr.take(P).bitcast(BF16)[:, 0:P]
    ovl = lr.take(2, NE)
    obase = lr.take(NE)
    cmpo = lr.take(OVER, NE)
    obf = lr.take(24)
    rowi = lr.take(TILES * 2, dt=I32).rearrange("p (a b) -> p a b", b=2)
    blki = lr.take(TILES * 2, dt=I32).rearrange("p (a b) -> p a b", b=2)
    addr = lr.take(TILES * 2, dt=I32).rearrange("p (a b) -> p a b", b=2)
    assert lr.at <= AFTER_M
    NRAW, NSPL = 6, 3
    CW = 2048
    le_ = Lay(0)
    eraw = le_.take(NRAW, CW)
    ehi = le_.take(NSPL, CW, dt=F32R)
    elo = le_.take(NSPL, CW, dt=F32R)
    xg = le_.take(D)
    xgh = le_.take(KT, P, dt=F32R)
    xgl = le_.take(KT, P, dt=F32R)
    sil = le_.take(DE)
    hid = le_.take(DE)
    hTh = le_.take(4, P, dt=F32R)
    hTl = le_.take(4, P, dt=F32R)
    assert le_.at <= AFTER_W
    yb = Lay(AFTER_H).take(D)
    lf = Lay(0)
    y1 = [lf.take(D) for _ in range(2)]
    y2 = [lf.take(D) for _ in range(2)]
    yo = [lf.take(D) for _ in range(2)]

    ps = ctx.enter_context(nc.psum_tensor("ps", [P, 8, 512], F32))

    def bank(b, n=512):
        return ps[:, b, 0:n]

    def pair(b):
        return ps[:, b:b + 2, :].rearrange("p b (c n) -> p (b c) n", n=P)

    def flat(b):
        return ps[:, b:b + 2, :].rearrange("p b n -> p (b n)")

    S = {}

    def s(name):
        if name not in S:
            S[name] = sem(name)
        return S[name]

    blocks = [("v", C_V + WB * i) for i in range(4)] + [("va", C_VA + GW * g) for g in range(NG)]
    blocks += [("u", C_U + WB * i) for i in range(4)]
    blocks += [("q", C_Q + GW * g) for g in range(NG)] + [("k", C_K + GW * g) for g in range(NG)]
    blocks += [("ga", C_GA + WB * i) for i in range(4)] + [("gb", C_GB + WB * i) for i in range(4)]
    NWIN = len(blocks)
    assert NWIN == 25
    NPROJ = 4
    NSPLIT = NWIN + NPROJ + 4
    w_in_v = a["w_in"][0].rearrange("(k p) c -> p k c", p=P)
    wpa_v = a["w_proj_a"][0].rearrange("(k p) c -> p k c", p=P)
    wpb_v = a["w_proj_b"][0].rearrange("(k p) c -> p k c", p=P)
    wout_v = a["w_out"][0].rearrange("(k p) c -> p k c", p=P)

    def wslot(n):
        k = 10 if NWIN <= n < NWIN + NPROJ else KT
        if n >= NWIN + NPROJ:
            j = n - NWIN - NPROJ
            hi, lo = (w[:, :, WB * j:WB * (j + 1)] for w in wo)
        else:
            hi, lo = (w[n % 2][:, 0:k * WB].rearrange("p (k c) -> p k c", c=WB) for w in (whi, wlo))
        return wraw[:, 0:k * WB].rearrange("p (k c) -> p k c", c=WB), hi, lo

    units = []
    for n, (kind, _) in enumerate(blocks):
        if kind in ("v", "va", "q", "k"):
            units += [(n, t) for t in range(TILES)]
        else:
            units += [(n, ct, c) for ct in range(2) for c in range(3)]
    readers, freed = [], {"act": 0, "dve": 0}
    for un in units:
        eng_ = "dve" if blocks[un[0]][0] in ("q", "k") else "act"
        freed[eng_] += 1
        readers.append((eng_, freed[eng_]))
    freed_u0 = 7 * TILES
    freed_g0 = 7 * TILES + 3 * AG
    last_unit = {un[0]: i + 1 for i, un in enumerate(units)}


    def first_chunks():
        return [("gu", j, j, 0) for j in range(4)]

    def loop_chunks(b):
        return [("gu", j, j - 2, b) for j in range(4)] + [("down", j, 2 + j, b - 1) for j in range(2)]

    def last_chunks():
        return [("down", j, 4 + j, NE - 1) for j in range(2)]

    def over_chunks(expert):
        return [("gu", j, j, expert) for j in range(4)] + [("down", j, 4 + j, expert) for j in range(2)]

    def store_counts(n, ring, stores):
        seen, out = [0] * ring, []
        for i in range(n):
            seen[i % ring] += stores(i)
            out.append(list(seen))
        return out

    def kept(g, t):
        return t == ST or P * t >= NPROMPT - KEEP[g]

    vst_n = store_counts(NG * TILES, 4, lambda i: 1 + kept(i // TILES, i % TILES))
    kst = store_counts(2 * NG * TILES, 4, lambda i: int(i >= NG * TILES and kept(i // TILES - NG, i % TILES)))

    def value_rows(g, j):
        dil = DIL[g][1]
        if g == 0:
            lst = ([(lambda v, i=j - 1: v[P * i:P * i + P, :], 0)] if j else []) + [(lambda v, i=j: v[P * i:P * i + P, :], 1)]
        elif g == 1:
            r, n = j // 2, j % 2
            f = lambda v, i: v.rearrange("(n q r) c -> r n q c", r=dil, q=P)[r, i, :, :]
            lst = ([(lambda v: f(v, n - 1), 0)] if n else []) + [(lambda v: f(v, n), 1)]
        else:
            lst = [(lambda v, r=2 * j + i: v.rearrange("(q r) c -> r q c", r=dil)[r, :, :], 0) for i in range(2)]
        return lst

    def qcols(x, g, j, which):
        dil = DIL[g][1]
        if g == 0:
            i = j + which
            return x[:, P * i:P * i + P]
        if g == 1:
            r, n = j // 2, j % 2 + which
            return x[:, P * dil * n + r:P * dil * (n + 1):dil]
        raise AssertionError

    attn_n = store_counts(NG * NTILE, 4, lambda n: 2 if n // NTILE == 2 else 1)
    sattn_stores = NH * NG

    def nblk(n):
        g, j = divmod(n, NTILE)
        return 1 if g == 2 or (g == 0 and j == 0) or (g == 1 and j % 2 == 0) else 2

    def vg_count(n):
        return 16 * sum(len(value_rows(*divmod(m, NTILE))) for m in range(n % 2, n + 1, 2))

    def cache_count(n):
        return 16 * sum(2 * SKT[m // NB] for m in range(n % 2, n + 1, 2))

    def w_in_count(n):
        return 16 * (n + 1 + max(0, min(n - NWIN + 1, NPROJ)))

    def chunk_uses(off):
        return off // NRAW + 1

    block = ctx.enter_context(nc.Block())

    @block.sync
    def _(sp):
        dma = nc.sync.dma_start
        dma(cst[:, :], a["c_f32"]).then_inc(s("const_in"), 16)
        dma(g1T[:, :], a["norm1_g"][0].rearrange("(k p) -> p k", p=P), allow_slow_non_contiguous=True).then_inc(s("const_in"), 16)

        def load_x(dst, t):
            if t == ST:
                dma(dst[0:NSAMP, :], a["x_sample"].rearrange("b s d -> (b s) d")).then_inc(s(f"x_in{t % 2}"), 16)
                dma(dst[NSAMP:P, :], a["x_prompt"][0, 0:P - NSAMP, :]).then_inc(s(f"x_in{t % 2}"), 16)
            else:
                dma(dst[:, :], a["x_prompt"][0, P * t:P * t + P, :]).then_inc(s(f"x_in{t % 2}"), 16)

        def load_w(n):
            if n >= 1:
                sp.wait_ge(s("w_split"), n)
            raw = wslot(n)[0]
            if n < NWIN:
                c = blocks[n][1]
                dma(raw, w_in_v[:, :, c:c + WB]).then_inc(s("w_in"), 16)
            elif n < NWIN + NPROJ:
                c = WB * (n - NWIN)
                dma(raw[:, 0:KT, :], wpa_v[:, :, c:c + WB]).then_inc(s("w_in"), 16)
                dma(raw[:, KT:10, :], wpb_v[:, :, c:c + WB]).then_inc(s("w_in"), 16)
            else:
                c = WB * (n - NWIN - NPROJ)
                dma(raw, wout_v[:, :, c:c + WB]).then_inc(s("w_in"), 16)

        load_x(xin[0], 0)
        load_w(0)
        load_x(xin[1], 1)
        dma(ids[:, :], a["c_ids"]).then_inc(s("const2_in"), 16)
        for j, n in enumerate(("q_norm_g", "k_norm_g")):
            dma(qg[:, j, :], a[n][0].partition_broadcast(P)).then_inc(s("const2_in"), 16)
        for t in range(2, TILES):
            sp.wait_ge(s("xs_ready"), t - 1)
            load_x(xin[t % 2], t)
            if t == 3:
                load_w(1)
        sp.wait_ge(s("xn_ready"), TILES)
        dma(wsp, a["w_spatial"][0].rearrange("g t s -> t g s")).then_inc(s("gate_in"), 16)
        dma(bsr[0:1, :, :], a["b_spatial"]).then_inc(s("gate_in"), 16)
        dma(gvb, a["v_norm_g"][0].partition_broadcast(P)).then_inc(s("gate_in"), 16)
        sp.wait_ge(s("zrow_ready"), 1)
        dma(y_d[NE * P:, :].rearrange("(p j) (a c) -> p (j a) c", p=P, c=512), zrow.unsqueeze(1).to_broadcast([P, 2 * OVER, 512]))\
            .then_inc(s("y_zero"), 16)
        for n in range(2, NWIN):
            load_w(n)
            if n == 12:
                for g in range(NG):
                    w = DIL[g][0]
                    drop = PKEEP[g] + NS - SKEEP[g]
                    for kv in "kv":
                        dma(o[f"sample_{kv}_w{w}"][0, :, 0:PKEEP[g] - drop], a[f"cache_{kv}_w{w}"][0, :, drop:PKEEP[g]])\
                            .then_inc(s("cache_out"), 16)

        for j in range(4):
            sp.wait_ge(s(f"v_st{j}"), 16 * vst_n[-1][j])
            sp.wait_ge(s(f"k_st{j}"), 16 * kst[-1][j])
            sp.wait_ge(s(f"sg_st{j}"), 16 * 12)
        sp.wait_ge(s("qk_T"), 2 * NG * TILES)
        sp.wait_ge(s("y_zero"), 16)
        for n in range(NG * NTILE):
            g, j = divmod(n, NTILE)
            if n >= 2:
                sp.wait_ge(s("attn_pv"), n - 1)
            for i, (rows, k) in enumerate(value_rows(g, j)):
                dst = vg[n % 2][:, k, :]
                if g == 2:
                    dst = vg[n % 2][64 * i:64 * i + 64, 0, :]
                dma(dst, rows(v_d[NSAMP:T, g * GW:(g + 1) * GW])).then_inc(s(f"vg_in{n % 2}"), 16)
        dma(vnew[0:NS, :, :], v_d[0:NSAMP, :].rearrange("(b t) c -> t b c", t=NS)).then_inc(s("vnew_in"), 16)
        for n in range(NG * NB):
            g, b = divmod(n, NB)
            if n >= 2:
                sp.wait_ge(s("sattn_pv"), n - 1)
            for kv, dst in (("k", kc), ("v", vc)):
                src = a[f"cache_{kv}_w{DIL[g][0]}"][0, b].rearrange("n h d -> n (h d)")
                for i in range(SKT[g]):
                    if g == 2:
                        rows = src.rearrange("(m r) c -> m r c", r=16)[16 * i:16 * i + 16, 0:NS, :]
                        dma(dst[n % 2][:, i, :], rows).then_inc(s(f"cache_in{n % 2}"), 16)
                    else:
                        dma(dst[n % 2][:, i, :], src[P * i:P * i + P, :]).then_inc(s(f"cache_in{n % 2}"), 16)
        for j in range(4):
            sp.wait_ge(s(f"attn_st{j}"), 16 * attn_n[-1][j])
        sp.wait_ge(s("sattn_stored"), 16 * sattn_stores)
        for t in range(TILES):
            if t >= 2:
                sp.wait_ge(s("comb"), t - 1)
            dma(co[t % 2], ao_d[col0(t):col0(t) + P].rearrange("t g h c -> t (g h) c")).then_inc(s(f"comb_in{t % 2}"), 16)
        load_w(NWIN)
        for j in range(3):
            sp.wait_ge(s(f"a_st{j}"), 16 * AG)
        for i in range(AG * 3):
            g, c = divmod(i, 3)
            c0, w = CHUNK[c]
            if i >= 2:
                sp.wait_ge(s("a_split"), i - 1)
            dma(sga[i % 2][:, 0:w], a_d[g, :, c0:c0 + w]).then_inc(s(f"a_in{i % 2}"), 16)
        for m in range(KT * 3):
            dt, c = divmod(m, 3)
            c0, w = CHUNK[c]
            if m >= 2:
                sp.wait_ge(s("merge"), m - 1)
            else:
                sp.wait_ge(s("a_split"), AG * 3)
            dma(sga[m % 2][:, 0:w], sg_d[0, dt, :, c0:c0 + w]).then_inc(s(f"sg_in{m % 2}"), 16)
            dma(sgb[m % 2][:, 0:w], sg_d[1, dt, :, c0:c0 + w]).then_inc(s(f"sg_in{m % 2}"), 16)
            if m % 6 == 0 and m // 6 < NPROJ - 1:
                load_w(NWIN + 1 + m // 6)
        for j in range(4):
            load_w(NWIN + NPROJ + j)
        sp.wait_ge(s("proj_mm"), KT * 3)
        sp.wait_ge(s("merge"), KT * 3)
        dma(g2b, a["norm2_g"][0].partition_broadcast(P)).then_inc(s("rout_in"), 16)
        dma(wr[:, :, 0:NEG], a["w_group_router"][0].rearrange("(k p) c -> p k c", p=P)).then_inc(s("rout_in"), 16)
        dma(wr[:, :, NEG:RW], a["w_expert_router"][0].rearrange("(k p) g e -> p k (g e)", p=P)).then_inc(s("rout_in"), 16)
        dma(rbias[:, 0:NEG], a["b_group_router"][0].partition_broadcast(P)).then_inc(s("rout_in"), 16)
        dma(rbias[:, NEG:RW], a["b_expert_router"][0].rearrange("g e -> (g e)").partition_broadcast(P)).then_inc(s("rout_in"), 16)
        for t in range(TILES):
            if t >= 2:
                sp.wait_ge(s("h_ready"), t - 1)
            dst = xr[t % 2]
            if t == ST:
                dma(dst[0:NSAMP, :], a["x_sample"].rearrange("b s d -> (b s) d")).then_inc(s(f"xr_in{t % 2}"), 16)
                dma(dst[NSAMP:P, :], a["x_prompt"][0, 0:P - NSAMP, :]).then_inc(s(f"xr_in{t % 2}"), 16)
            else:
                dma(dst[:, :], a["x_prompt"][0, P * t:P * t + P, :]).then_inc(s(f"xr_in{t % 2}"), 16)

        sp.wait_ge(s("out_mm"), TILES)

        def load_chunk(kind, j, expert, slot6):
            if kind == "gu":
                w = a["w_gate" if j % 2 == 0 else "w_up"][0, bass.ds(expert, 1), :, :]
                src = w.rearrange("a (p k) f -> p (a k) f", k=KT)[:, 4 * (j // 2):4 * (j // 2) + 4, :]
                dst = eraw[:, slot6, :].rearrange("p (k f) -> p k f", f=DE)
            else:
                w = a["w_down"][0, bass.ds(expert, 1), :, :]
                src = w.rearrange("a (p k) f -> p (a k) f", k=4)[:, 2 * j:2 * j + 2, :]
                dst = eraw[:, slot6, :].rearrange("p (k f) -> p k f", f=D)
            dma(dst, src).then_inc(s(f"e_in{slot6}"), 16)

        def load_chunks(plan, b):
            for kind, j, off, expert in plan:
                if not isinstance(b, int) or 6 * b + off >= NRAW:
                    sp.wait_ge(s("e_split"), b * 6 + (off - NRAW + 1))
                load_chunk(kind, j, expert, off % NRAW)

        load_chunks(first_chunks(), 0)
        load_chunks(loop_chunks(1), 1)
        with sp.Fori(2, NE) as b:
            load_chunks(loop_chunks(b), b)
        load_chunks(last_chunks(), NE - 1)
        sp.wait_ge(s("table_ready"), 1)
        nover = sp.value_load(obe[0:1, OVER:OVER + 1], min_val=0, max_val=OVER)
        with sp.Fori(0, OVER) as j2:
            with sp.If(j2 < nover):
                eo = sp.value_load(obe[0:1, bass.ds(j2, 1)], min_val=0, max_val=NE - 1)
                load_chunks(over_chunks(eo), j2 + NE)
        for t in range(TILES):
            sp.wait_ge(s("yo_ready"), t + 1)
            if t == ST:
                dma(o["y_sample"].rearrange("b s d -> (b s) d"), yo[t % 2][0:NSAMP, :]).then_inc(s(f"y_out{t % 2}"), 16)
            else:
                dma(o["y_prompt"][0, P * t:P * t + P, :], yo[t % 2]).then_inc(s(f"y_out{t % 2}"), 16)
        sp.wait_ge(s("cache_out"), 16 * 2 * NG)
        for j in range(4):
            sp.wait_ge(s(f"k_st{j}"), 16 * kst[-1][j])
            sp.wait_ge(s(f"v_st{j}"), 16 * vst_n[-1][j])
        sp.wait_ge(s("vn_out"), 16)
        for j in range(2):
            sp.wait_ge(s(f"y_out{j}"), 16 * len(range(j, TILES, 2)))
    @block.tensor
    def _(pe):
        mm, tr = nc.tensor.matmul, nc.tensor.transpose
        unit = [0]

        def claim():
            if unit[0] >= 4:
                eng, count = readers[unit[0] - 4]
                pe.wait_ge(s(f"freed_{eng}"), count)
            unit[0] += 1
            return (unit[0] - 1) % 4

        def three(out, lhs, rhs, n):
            for k in range(n):
                mm(out, lhs[0](k), rhs[0](k), start=(k == 0), stop=False)
                mm(out, lhs[0](k), rhs[1](k), start=False, stop=False)
                last = mm(out, lhs[1](k), rhs[0](k), start=False, stop=(k == n - 1))
            return last

        def x_transposes(t):
            pe.wait_ge(s("xs_ready"), t + 1)
            if t >= 2:
                pe.wait_ge(s("xf_ready"), t - 1)
            else:
                pe.wait_ge(s("const_in"), 32)
            dst = pair(4 + 2 * (t % 2))
            for k in range(KT):
                last = tr(dst[:, k, :], xs[t % 2][:, P * k:P * k + P], ident)
            last.then_inc(s("x_T"), 1)

        def tok_unit(n, t):
            _, hi, lo = wslot(n)
            if t == 0:
                pe.wait_ge(s("w_split"), n + 1)
            b = claim()
            c0 = col0(t)
            three(bank(b, WB), [lambda k, v=v: v[:, k, c0:c0 + P] for v in xT],
                  [lambda k, v=v: v[:, k, :] for v in (hi, lo)], KT).then_inc(s("unit_mm"), 1)

        def feat_unit(n, ct, c, src=None, dst=None, nk=KT, k0=0):
            _, hi, lo = wslot(n)
            if ct == 0 and c == 0:
                pe.wait_ge(s("w_split"), n + 1)
            c0, w = CHUNK[c]
            src = src or xT
            out = dst if dst is not None else bank(claim(), w)
            return three(out, [lambda k, v=v: v[:, k0 + k, P * ct:P * ct + P] for v in (hi, lo)],
                         [lambda k, v=v: v[:, k, c0:c0 + w] for v in src], nk)

        x_transposes(0)
        for t in range(TILES):
            if t + 1 < TILES:
                x_transposes(t + 1)
            pe.wait_ge(s("xn_ready"), t + 1)
            tok_unit(0, t)
        for n in range(1, 7):
            for t in range(TILES):
                tok_unit(n, t)
        pe.wait_ge(s("gate_in"), 48)
        for g in range(AG):
            last = tr(pair(4)[:, g, :], wsp[:, g, :], ident)
        last.then_inc(s("ws_T"), 1)
        pe.wait_ge(s("wm_ready"), 1)
        mm(ps[0:NSAMP, 6, 0:AG * NS].rearrange("p (g t) -> p g t", t=NS), cst[0:NS, CREP:CREP + NSAMP],
           wmT[0:NS, :, 0:NS], start=True, stop=True).then_inc(s("ws_rep"), 1)

        gate_n = [0]

        def gate_unit(m):
            g, c = divmod(m, 3)
            b = 4 + m % 4
            if m == 0:
                pe.wait_ge(s("vn_ready"), TILES)
                pe.wait_ge(s("wms_ready"), 1)
            if m >= 4:
                pe.wait_ge(s("a_ready"), m - 3)
            c0, w = CHUNK[c]
            one = cst[0:1, CONE:CONE + P]
            if c < 2:
                out = ps[:, b, :].rearrange("p (n t) -> p n t", t=P)
                mm(out, one, bsr[0:1, g:g + 1, :].to_broadcast([1, 4, P]), start=True, stop=True)
                for i in range(4):
                    last = mm(out[:, i, :], vn[:, 4 * c + i, P * g:P * g + P], wmT[:, g, :], start=False, stop=True,
                              skip_group_check=True)
            else:
                out = ps[:, b, 0:NSAMP]
                mm(out.rearrange("p (n t) -> p n t", t=NS), one, bsr[0:1, g:g + 1, 0:NS].to_broadcast([1, NB, NS]),
                   start=True, stop=True)
                last = mm(out, vn[0:NSAMP, ST, P * g:P * g + P], wmS[0:NSAMP, g, :], start=False, stop=True,
                          skip_group_check=True)
            last.then_inc(s("gate_mm2"), 1)

        m = 0
        for n in range(7, 11):
            for ct in range(2):
                for c in range(3):
                    feat_unit(n, ct, c).then_inc(s("unit_mm"), 1)
                    if m:
                        gate_unit(m - 1)
                    m += 1
        gate_unit(m - 1)

        qk = [(n, t) for n in range(11, 17) for t in range(TILES)]

        def qk_transposes(i):
            pe.wait_ge(s("qn_ready"), i + 1)
            if i >= 2:
                pe.wait_ge(s("qk_T"), i - 1)
            else:
                pe.wait_ge(s("a_ready"), 24)
            for j in range(2):
                last = tr(ps[:, 4 + i % 2, P * j:P * j + P], qn[i % 4][:, P * j:P * j + P], ident)
            last.then_inc(s("qk_tr"), 1)

        for i, (n, t) in enumerate(qk):
            tok_unit(n, t)
            if i >= 3:
                qk_transposes(i - 3)
        for i in range(len(qk) - 3, len(qk)):
            qk_transposes(i)
        for n in range(17, 25):
            for ct in range(2):
                for c in range(3):
                    feat_unit(n, ct, c).then_inc(s("unit_mm"), 1)
        for eng, count in readers[-4:]:
            pe.wait_ge(s(f"freed_{eng}"), count)

        def scores(n):
            g, j = divmod(n, NTILE)
            nb = nblk(n)
            if n >= 2:
                pe.wait_ge(s("attn_exp"), n - 1)
            if n == 0:
                pe.wait_ge(s("qk_T"), 54)
            sc = ps[:, 2 * (n % 2):2 * (n % 2) + 2, 0:2 * nb * P].rearrange("p b (h k) -> p b h k", k=nb * P)
            mask = cbf[:, BPAIR:BPAIR + P] if g == 2 else cbf[:, BPO + (2 - nb) * P:BPO + 2 * P]
            for b in range(2):
                mm(ps[:, 2 * (n % 2) + b, 0:2 * nb * P].rearrange("p (h k) -> p h k", k=nb * P), identb,
                   mask.unsqueeze(1).to_broadcast([P, 2, nb * P]), start=True, stop=True)
            for b in range(2):
                for i in range(2):
                    pr = 2 * g + i
                    q = qT[64 * b:64 * b + 64, pr, :]
                    k = kT[64 * b:64 * b + 64, pr, :]
                    out = sc[:, b, i, :]
                    if g == 2:
                        for half in range(2):
                            r = 2 * j + half
                            rows = slice(64 * half, 64 * half + 64)
                            last = mm(out[rows, 64 * half:64 * half + 64], q[:, r:NPROMPT:16], k[:, r:NPROMPT:16],
                                      start=False, stop=True, skip_group_check=True)
                    else:
                        qa = qcols(q, g, j, 0)
                        for kb in range(nb):
                            last = mm(out[:, kb * P:kb * P + P], qa, qcols(k, g, j, kb - nb + 1), start=False,
                                      stop=True, skip_group_check=True)
            last.then_inc(s("attn_s"), 1)

        def p_transposes(n):
            nb = nblk(n)
            pe.wait_ge(s("attn_exp"), n + 1)
            if n >= 1:
                pe.wait_ge(s("attn_pt"), n)
            for i in range(NH * nb):
                last = tr(pair(4)[:, i, :], Eb[n % 2][:, i // nb, (i % nb) * P:(i % nb) * P + P], ident)
            last.then_inc(s("attn_tr"), 1)

        def pv(n):
            g, j = divmod(n, NTILE)
            nb = nblk(n)
            pe.wait_ge(s("attn_pt"), n + 1)
            pe.wait_ge(s(f"vg_in{n % 2}"), vg_count(n))
            if n >= 2:
                pe.wait_ge(s("attn_o"), n - 1)
            for sl in range(NH):
                head = 2 * (sl % 2) + sl // 2
                for kb in range(nb):
                    k = 0 if g == 2 else 2 - nb + kb
                    last = mm(ps[:, 6 + n % 2, HD * head:HD * head + HD], Pt[n % 2][:, nb * sl + kb, :],
                              vg[n % 2][:, k, HD * head:HD * head + HD], start=(kb == 0), stop=(kb == nb - 1))
            last.then_inc(s("attn_pv"), 1)

        NU = NG * NTILE
        for n in range(NU + 2):
            if n < NU:
                scores(n)
            if 1 <= n <= NU:
                p_transposes(n - 1)
            if n >= 2:
                pv(n - 2)
        pe.wait_ge(s("attn_o"), NU)
        pe.wait_ge(s("qpad_ready"), 2)
        offs = (BS0, BS1, BS2)

        def k_transposes(n):
            g, b = divmod(n, NB)
            pe.wait_ge(s(f"cache_in{n % 2}"), cache_count(n))
            if n >= 1:
                pe.wait_ge(s("sk_T"), n)
            for hp in range(2):
                for i in range(SKT[g]):
                    last = tr(ps[:, 4 + hp, P * i:P * i + P], kc[n % 2][:, i, P * hp:P * hp + P], ident)
            last.then_inc(s("sk_tr"), 1)

        def s_scores(n):
            g, b = divmod(n, NB)
            pe.wait_ge(s("sk_T"), n + 1)
            if n >= 2:
                pe.wait_ge(s("sattn_exp"), n - 1)
            nk = P * SKT[g]
            bk = 2 * (n % 2)
            parts = [(0, nk, ps[:, bk, 0:nk])]
            parts.append((nk, NS, ps[:, bk + (nk // 512), nk % 512:nk % 512 + NS]))
            for i, (k0, w, out) in enumerate(parts):
                mm(out, identb, cbf[:, offs[g] + k0:offs[g] + k0 + w], start=(i == 0 or nk == 512), stop=True,
                   skip_group_check=True)
            for hd in range(NH):
                q = qpad[:, 2 * g + hd // 2, (hd % 2) * NB + b, :]
                for i, (k0, w, out) in enumerate(parts):
                    rhs = KTs[n % 2][:, hd // 2, 0:nk] if i == 0 else kTs[:, 2 * g + hd // 2, NS * b:NS * b + NS]
                    last = mm(out[32 * hd:32 * hd + 32, :], q, rhs, start=False, stop=True,
                              skip_group_check=True)
            last.then_inc(s("sattn_s"), 1)

        def s_tail(n):
            g, b = divmod(n, NB)
            pe.wait_ge(s("sattn_exp"), n + 1)
            if n >= 1:
                pe.wait_ge(s("sattn_pt"), n)
                pe.wait_ge(s("sattn_o"), n)
            for i in range(SKT[g]):
                tr(ps[:, 6, P * i:P * i + P], Es[n % 2][:, P * i:P * i + P], ident)
            nk = P * SKT[g]
            tr(ps[0:NS, 7, 0:P], Es[n % 2][:, nk:nk + NS], ident).then_inc(s("sattn_tr"), 1)

        def s_pv(n):
            g, b = divmod(n, NB)
            pe.wait_ge(s("sattn_pt"), n + 1)
            if n == 0:
                pe.wait_ge(s("vnew_in"), 16)
            for hd in range(NH):
                out = ps[32 * hd:32 * hd + 32, 7, 256:256 + HD]
                for i in range(SKT[g]):
                    mm(out, PTs[n % 2][:, i, 32 * hd:32 * hd + 32], vc[n % 2][:, i, HD * hd:HD * hd + HD],
                       start=(i == 0), stop=False)
                last = mm(out, PTs[n % 2][0:NS, 4, 32 * hd:32 * hd + 32],
                          vnew[0:NS, b, g * GW + HD * hd:g * GW + HD * hd + HD], start=False, stop=True)
            last.then_inc(s("sattn_pv"), 1)

        NSU = NG * NB
        for n in range(NSU + 1):
            if n < NSU:
                k_transposes(n)
                s_scores(n)
            if n >= 1:
                s_tail(n - 1)
                s_pv(n - 1)
        for t in range(TILES):
            pe.wait_ge(s("comb"), t + 1)
            if t >= 2:
                pe.wait_ge(s("bT_ready"), t - 1)
            else:
                pe.wait_ge(s("sattn_o"), NSU)
            for j in range(2):
                last = tr(ps[:, 4 + t % 2, P * j:P * j + P], cb[t % 2][:, 0, P * j:P * j + P], ident)
            last.then_inc(s("bT_tr"), 1)
        pe.wait_ge(s("bT_ready"), TILES)
        pe.wait_ge(s("a_split"), AG * 3)
        for n in range(NPROJ):
            for ct in range(2):
                for c in range(3):
                    mi = (n * 2 + ct) * 3 + c
                    if mi >= 4:
                        pe.wait_ge(s("merge"), mi - 3)
                    w = CHUNK[c][1]
                    feat_unit(NWIN + n, ct, c, src=aT, dst=bank(mi % 4, w))
                    feat_unit(NWIN + n, ct, c, src=bT, dst=bank(4 + mi % 4, w), nk=2, k0=KT).then_inc(s("proj_mm"), 1)
        pe.wait_ge(s("w_split"), NSPLIT)
        pe.wait_ge(s("merge"), KT * 3)

        def router(t):
            pe.wait_ge(s("x2_ready"), t + 1)
            if t >= 1:
                pe.wait_ge(s("x2T_ready"), t)
            for k in range(KT):
                last = tr(pair(4)[:, k, :], x2[t % 2][:, P * k:P * k + P], ident)
            last.then_inc(s("x2_tr"), 1)
            pe.wait_ge(s("x2T_ready"), t + 1)
            if t == 0:
                pe.wait_ge(s("rout_in"), 80)
            if t >= 1:
                pe.wait_ge(s("route_in"), t)
            for k in range(KT):
                last = mm(bank(6, RW), x2T[t % 2][:, k, :], wr[:, k, :], start=(k == 0), stop=(k == KT - 1))
            last.then_inc(s("rout_mm"), 1)

        for t in range(TILES):
            pe.wait_ge(s("m_split"), t + 1)
            if t >= 2:
                pe.wait_ge(s("h_ready"), t - 1)
            for half in range(2):
                last = three(bank(2 * (t % 2) + half), [lambda k, v=v: v[t % 2][:, k, :] for v in (mh, ml)],
                             [lambda k, v=v: v[:, k, 512 * half:512 * half + 512] for v in wo], KT)
            last.then_inc(s("out_mm"), 1)
            if t >= 1:
                router(t - 1)
        router(TILES - 1)
        pe.wait_ge(s("assign"), 1)
        pe.wait_ge(s("route_in"), TILES)
        ones = cbf[:, BONE:BONE + P]
        for t in range(TILES):
            out = ps[:, 0, NE * t:NE * t + NE]
            order = [ST] + list(range(NTILE))
            before = order[:order.index(t)]
            for b4 in before:
                mm(out, ones, Abf[:, b4, :], start=(b4 == before[0]), stop=False)
            last = mm(out, cbf[:, BLT:BLT + P], Abf[:, t, :], start=not before, stop=True)
        for t in range(TILES):
            last = mm(ps[0:NE, 1, 0:1], Abf[:, t, :], cbf[:, BONE:BONE + 1], start=(t == 0), stop=(t == TILES - 1))
        last.then_inc(s("count_mm"), 1)
        pe.wait_ge(s("over_cnt"), 1)
        mm(ps[:, 2, 0:NE], nbb[0:NE, 0:P], cbf[0:NE, BLS:BLS + NE], start=True, stop=True)
        mm(ps[:, 2, NE:2 * NE], nbb[0:NE, 0:P], cbf[0:NE, BLI:BLI + NE], start=True, stop=True).then_inc(s("over_mm"), 1)
        pe.wait_ge(s("table_ready"), 1)

        def x_tr(b):
            pe.wait_ge(s("xg_in"), b * 16 + 16)
            for k in range(KT):
                last = tr(pair(0)[:, k, :], xg[:, k:D:KT], ident)
            last.then_inc(s("xg_tr"), 1)

        def gate_up(b, plan, cb_):
            pe.wait_ge(s("xgT"), b + 1)
            for kind, j, off, _ in plan:
                if kind == "gu":
                    pe.wait_ge(s("e_split"), cb_ * 6 + (off + 1))
                    hi, lo = (v[:, off % NSPL, :].rearrange("p (k f) -> p k f", f=DE) for v in (ehi, elo))
                    for k in range(4):
                        kk = 4 * (j // 2) + k
                        mm(bank(2 + j % 2), xgh[:, kk, :], hi[:, k, :], start=(kk == 0), stop=False)
                        mm(bank(2 + j % 2), xgh[:, kk, :], lo[:, k, :], start=False, stop=False)
                        last = mm(bank(2 + j % 2), xgl[:, kk, :], hi[:, k, :], start=False, stop=(kk == KT - 1))
                    last.then_inc(s("e_used"), 1)

        def h_tr(b):
            pe.wait_ge(s("hid"), b + 1)
            for k in range(4):
                last = tr(ps[:, 4, P * k:P * k + P], hid[:, k:DE:4], ident)
            last.then_inc(s("hid_tr"), 1)

        def down(b, plan, cb_, first=False):
            pe.wait_ge(s("hidT"), b + 1)
            if not first:
                pe.wait_ge(s("y_read"), b)
            for kind, j, off, _ in plan:
                if kind == "down":
                    pe.wait_ge(s("e_split"), cb_ * 6 + (off + 1))
                    hi, lo = (v[:, off % NSPL, :].rearrange("p (k f) -> p k f", f=D) for v in (ehi, elo))
                    for k in range(2):
                        for half in range(2):
                            kk, cols = 2 * j + k, slice(512 * half, 512 * half + 512)
                            mm(bank(5 + half), hTh[:, kk, :], hi[:, k, cols], start=(kk == 0), stop=False)
                            mm(bank(5 + half), hTh[:, kk, :], lo[:, k, cols], start=False, stop=False)
                            last = mm(bank(5 + half), hTl[:, kk, :], hi[:, k, cols], start=False, stop=(kk == 3))
                    last.then_inc(s("e_used"), 1)

        x_tr(0)
        gate_up(0, first_chunks(), 0)
        x_tr(1)
        h_tr(0)
        gate_up(1, loop_chunks(1), 1)
        x_tr(2)
        down(0, loop_chunks(1), 1, first=True)
        h_tr(1)
        with pe.Fori(2, NE - 1) as b:
            gate_up(b, loop_chunks(b), b)
            x_tr(b + 1)
            down(b - 1, loop_chunks(b), b)
            h_tr(b)
        gate_up(NE - 1, loop_chunks(NE - 1), NE - 1)
        down(NE - 2, loop_chunks(NE - 1), NE - 1)
        h_tr(NE - 1)
        down(NE - 1, last_chunks(), NE - 1)
        nover = pe.value_load(obe[0:1, OVER:OVER + 1], min_val=0, max_val=OVER)
        with pe.Fori(0, OVER) as j2:
            with pe.If(j2 < nover):
                b = j2 + NE
                x_tr(b)
                gate_up(b, over_chunks(0), b)
                h_tr(b)
                down(b, over_chunks(0), b)

    @block.scalar
    def _(act):
        act_ = nc.scalar.activation
        own = Steps(act, s("act_own"))

        def w_hi(n):
            raw, hi, _ = wslot(n)
            act.wait_ge(s("w_in"), w_in_count(n))
            if n >= NWIN + NPROJ:
                act.wait_ge(s("proj_mm"), 6 * NPROJ)
            elif n - 2 >= NWIN:
                act.wait_ge(s("proj_mm"), 6 * (n - 2 - NWIN + 1))
            elif n >= 2:
                act.wait_ge(s("unit_mm"), last_unit[n - 2])
            act_(hi, raw, ACT.Copy).then_inc(s("w_hi"), 1)

        def norm1(t):
            act.wait_ge(s(f"x_in{t % 2}"), 16 * (t // 2 + 1 + (t == ST)))
            own.then_wait(act_(junk1, xin[t % 2], ACT.Square, accum_out=small[:, 0, t:t + 1]))
            act_(small[:, 1, t:t + 1], small[:, 0, t:t + 1], ACT.Sqrt, bias=eps, scale=1.0 / D).then_inc(s("sd1"), 1)

        def x_hi(t):
            act.wait_ge(s("xf_ready"), t + 1)
            w = NSAMP if t == ST else P
            act_(xT[0][:, :, col0(t):col0(t) + w], xfull[:, :, 0:w], ACT.Copy).then_inc(s("xh_ready"), 1)

        act.wait_ge(s("const_in"), 32)
        norm1(0)
        w_hi(0)
        seen = {"va": 0, "u": 0, "qk": 0, "g": 0}

        def qk_evac(k):
            act.wait_ge(s("qk_tr"), k + 1)
            g, t = divmod(k, TILES)
            src = ps[:, 4 + k % 2, 0:GW].rearrange("p (a b) -> p a b", b=P)
            full, samp = (qT, qTs) if g < NG else (kT, kTs)
            g %= NG
            if t == ST:
                act_(samp[:, 2 * g:2 * g + 2, :], src[:, :, 0:NSAMP], ACT.Copy).then_inc(s("qk_T"), 1)
            else:
                act_(full[:, 2 * g:2 * g + 2, P * t:P * t + P], src, ACT.Copy).then_inc(s("qk_T"), 1)

        def evac(i):
            un = units[i]
            n, kind = un[0], blocks[un[0]][0]
            if kind == "ga" and seen["g"] == 0:
                for j in range(6 * TILES - 3, 6 * TILES):
                    qk_evac(j)
            act.wait_ge(s("unit_mm"), i + 1)
            if kind == "v":
                act_(vn[:, un[1], WB * n:WB * n + WB], bank(i % 4, WB), ACT.Gelu_apprx_tanh).then_inc(s("freed_act"), 1)
            elif kind == "va":
                k = seen["va"]
                seen["va"] += 1
                if k >= 4:
                    act.wait_ge(s(f"v_st{k % 4}"), 16 * vst_n[k - 4][k % 4])
                act_(vst[k % 4], bank(i % 4, WB), ACT.Copy).then_inc(s("freed_act"), 1)
                if k < TILES:
                    act.wait_ge(s("vss"), k + 1)
                    act_(small[:, 4, k:k + 1], small[:, 3, k:k + 1], ACT.Sqrt, bias=eps, scale=1.0 / D).then_inc(s("vsd"), 1)
            elif kind == "u":
                m, w = seen["u"], CHUNK[un[2]][1]
                seen["u"] += 1
                if m >= 3:
                    act.wait_ge(s("a_ready"), m - 2)
                act_(ug[m % 3][:, 0:w], bank(i % 4, w), ACT.Gelu_apprx_tanh).then_inc(s("freed_act"), 1)
            elif kind in ("q", "k"):
                k = seen["qk"]
                seen["qk"] += 1
                if k == 0:
                    act.wait_ge(s("a_ready"), 3 * AG)
                if k >= 2:
                    act.wait_ge(s("ss_ready"), k - 1)
                act_(sq[k % 2], bank(i % 4, WB), ACT.Square).then_inc(s("sq_ready"), 1)
                act.wait_ge(s("ss_ready"), k + 1)
                act_(stat[:, 2 + k % 2, :], stat[:, k % 2, :], ACT.Sqrt, bias=eps, scale=1.0 / HD).then_inc(s("sd_ready"), 1)
                if k >= 3:
                    qk_evac(k - 3)
            else:
                k, w = seen["g"], CHUNK[un[2]][1]
                seen["g"] += 1
                if k >= 4:
                    act.wait_ge(s(f"sg_st{k % 4}"), 16 * (k // 4))
                act_(sgs[k % 4][:, 0:w], bank(i % 4, w), ACT.Sigmoid).then_inc(s("freed_act"), 1)

        def mid(n):
            return 4 if blocks[n][0] in ("v", "va", "q", "k") else 2

        at = 0
        for i, un in enumerate(units):
            if i and units[i - 1][0] != un[0]:
                at = i
            if un[0] == 0:
                if i + 1 < TILES:
                    norm1(i + 1)
                x_hi(i)
                if i:
                    evac(i - 1)
            else:
                if i == TILES:
                    evac(i - 1)
                evac(i)
            if i - at == mid(un[0]) and un[0] + 1 < NWIN:
                w_hi(un[0] + 1)
        for j in range(4):
            act.wait_ge(s(f"sg_st{j}"), 16 * 12)
        for n in range(NG * NTILE):
            nk = nblk(n) * P
            act.wait_ge(s("nm_ready"), n + 1)
            if n >= 2:
                act.wait_ge(s("attn_tr"), n - 1)
            for sl in range(NH):
                head = 2 * (sl % 2) + sl // 2
                last = act_(Eb[n % 2][:, sl, 0:nk], ps[:, 2 * (n % 2) + sl // 2, nk * (sl % 2):nk * (sl % 2) + nk], ACT.Exp,
                            bias=nm[:, n % 2, sl:sl + 1], scale=SCALE, accum_out=ob[n % 4][:, head, HD:HD + 1])
            last.then_inc(s("attn_exp"), 1)
        for n in range(NG * NB):
            g, b = divmod(n, NB)
            nk = P * SKT[g]
            act.wait_ge(s("sk_tr"), n + 1)
            if n >= 2:
                act.wait_ge(s("sattn_s"), n - 1)
            act_(KTs[n % 2][:, :, 0:nk], ps[:, 4:6, 0:nk], ACT.Copy).then_inc(s("sk_T"), 1)
            act.wait_ge(s("snm_ready"), n + 1)
            if n >= 2:
                act.wait_ge(s("sattn_tr"), n - 1)
            act_(Es[n % 2][:, 0:nk + NS], flat(2 * (n % 2))[:, 0:nk + NS], ACT.Exp, bias=snm[:, n % 2:n % 2 + 1], scale=SCALE,
                 accum_out=osb[:, b * NG + g, HD:HD + 1]).then_inc(s("sattn_exp"), 1)
        for t in range(TILES):
            act.wait_ge(s("cd_ready"), t + 1)
            act_(cs[t % 2][:, 1:4, :], cs[t % 2][:, 1:4, :], ACT.Exp).then_inc(s("ce_ready"), 1)
            act.wait_ge(s("bT_tr"), t + 1)
            w = NSAMP if t == ST else P
            act_(bT[0][:, :, col0(t):col0(t) + w], ps[:, 4 + t % 2, 0:2 * P].rearrange("p (a b) -> p a b", b=P)[:, :, 0:w],
                 ACT.Copy).then_inc(s("bh_ready"), 1)
        w_hi(NWIN)
        for i in range(3 * AG):
            g, c = divmod(i, 3)
            c0, w = CHUNK[c]
            act.wait_ge(s(f"a_in{i % 2}"), 16 * (i // 2 + 1))
            act_(aT[0][:, g, c0:c0 + w], sga[i % 2][:, 0:w], ACT.Copy).then_inc(s("a_hi"), 1)
        for n in range(NWIN + 1, NSPLIT):
            w_hi(n)

        def m_hi(t):
            if t == 0:
                act.wait_ge(s("merge"), 3 * KT)
            if t >= 2:
                act.wait_ge(s("out_mm"), t - 1)
            act_(mh[t % 2], mT[:, :, col0(t):col0(t) + P], ACT.Copy).then_inc(s("m_hi"), 1)

        def x2T_evac(t):
            act.wait_ge(s("x2_tr"), t + 1)
            if t >= 2:
                act.wait_ge(s("rout_mm"), t - 1)
            act_(x2T[t % 2], pair(4), ACT.Copy).then_inc(s("x2T_ready"), 1)

        m_hi(0)
        for t in range(TILES):
            if t + 1 < TILES:
                m_hi(t + 1)
            act.wait_ge(s("h_ready"), t + 1)
            own.then_wait(act_(junk3, hbuf[:, t, :], ACT.Square, accum_out=small[:, 0, t:t + 1]))
            act_(small[:, 1, t:t + 1], small[:, 0, t:t + 1], ACT.Sqrt, bias=eps, scale=1.0 / D).then_inc(s("sd2"), 1)
            if t >= 1:
                x2T_evac(t - 1)
        x2T_evac(TILES - 1)
        act.wait_ge(s("rt_d4"), 1)
        act_(R["d4"], R["d4"], ACT.Exp).then_inc(s("rt_e4"), 1)
        act.wait_ge(s("rt_dd"), 1)
        act_(R["ex"], R["ex"], ACT.Exp).then_inc(s("rt_ex"), 1)

        def c_hi(b, off, first=False):
            act.wait_ge(s(f"e_in{off % NRAW}"), b * 16 + 16 * chunk_uses(off))
            if not first:
                act.wait_ge(s("e_used"), b * 6 + (off - NSPL + 1))
            act_(ehi[:, off % NSPL, :], eraw[:, off % NRAW, :], ACT.Copy).then_inc(s("e_hi"), 1)

        def xg_hi(b):
            act.wait_ge(s("xg_tr"), b + 1)
            act_(xgh, pair(0), ACT.Copy).then_inc(s("xg_hi"), 1)

        def silu(b, used):
            act.wait_ge(s("e_used"), used)
            act_(sil, bank(2), ACT.Silu).then_inc(s("silu"), 1)

        def hid_hi(b):
            act.wait_ge(s("hid_tr"), b + 1)
            act_(hTh, ps[:, 4, :].rearrange("p (k n) -> p k n", n=P), ACT.Copy).then_inc(s("hid_hi"), 1)

        def y_evac(b, used, first=False):
            act.wait_ge(s("e_used"), used)
            if not first:
                act.wait_ge(s("y_st"), b * 16)
            act_(yb, flat(5)[:, 0:D], ACT.Copy).then_inc(s("y_read"), 1)
            act.wait_ge(s("y_read"), b + 1)
            act.dma_start(y_d.rearrange("(b p) d -> b p d", p=P)[bass.ds(b, 1), :, :].rearrange("a p d -> p (a d)"), yb)\
                .then_inc(s("y_st"), 16)

        act.wait_ge(s("table_ready"), 1)
        act.wait_ge(s("x2_st0"), 16 * 5)
        act.wait_ge(s("x2_st1"), 16 * 4)
        for off in range(3):
            c_hi(0, off, first=True)
        xg_hi(0)
        c_hi(0, 3)
        c_hi(0, 4)
        silu(0, 4)
        xg_hi(1)
        c_hi(0, 5)
        c_hi(0, 6)
        hid_hi(0)

        def turn(b, bn, last=False):
            for off in (1, 2, 3, 4):
                c_hi(b, off)
            silu(b, b * 6 + 2)
            if not last:
                xg_hi(b + 1)
            c_hi(b, 5)
            if not last:
                c_hi(b, 6)
            y_evac(b - 1, b * 6 + 4, first=(bn == 1))
            hid_hi(b)

        turn(1, 1)
        with act.Fori(2, NE - 1) as b:
            turn(b, None)
        turn(NE - 1, None, last=True)
        y_evac(NE - 1, 6 * NE)
        nover = act.value_load(obe[0:1, OVER:OVER + 1], min_val=0, max_val=OVER)
        with act.Fori(0, OVER) as j2:
            with act.If(j2 < nover):
                b = j2 + NE
                xg_hi(b)
                for off in range(6):
                    c_hi(b, off)
                silu(b, b * 6 + 4)
                hid_hi(b)
                y_evac(b, b * 6 + 6)

    @block.vector
    def _(dve):
        v = nc.vector
        tt, stt, tsc, cp = v.tensor_tensor, v.scalar_tensor_tensor, v.tensor_scalar, v.tensor_copy
        own = Steps(dve, s("dve_own"))

        def w_lo(n):
            raw, hi, lo = wslot(n)
            dve.wait_ge(s("w_hi"), n + 1)
            tt(lo, raw, hi.bitcast(F32), ALU.subtract).then_inc(s("w_split"), 1)

        def scale_x(t):
            dve.wait_ge(s("sd1"), t + 1)
            own.then_wait(v.reciprocal(small[:, 2, t:t + 1], small[:, 1, t:t + 1]))
            if t >= 2:
                dve.wait_ge(s("x_T"), t - 1)
            tsc(xs[t % 2], xin[t % 2], small[:, 2, t:t + 1], None, ALU.mult).then_inc(s("xs_ready"), 1)

        def x_full(t):
            dve.wait_ge(s("x_T"), t + 1)
            if t >= 1:
                dve.wait_ge(s("xn_ready"), t)
            tt(xfull, pair(4 + 2 * (t % 2)), g1T[:, :].unsqueeze(2).to_broadcast([P, KT, P]), ALU.mult)\
                .then_inc(s("xf_ready"), 1)
            dve.wait_ge(s("xh_ready"), t + 1)
            w = NSAMP if t == ST else P
            cols = slice(col0(t), col0(t) + w)
            tt(xT[1][:, :, cols], xfull[:, :, 0:w], xT[0][:, :, cols].bitcast(F32), ALU.subtract).then_inc(s("xn_ready"), 1)

        def vnorm_sum(t):
            dve.wait_ge(s("freed_act"), 3 * TILES + t + 1)
            if t == 0:
                dve.wait_ge(s("gate_in"), 48)
            else:
                dve.wait_ge(s("vss"), t)
            v.tensor_tensor_reduce(junk2, vn[:, t, :], vn[:, t, :], 1.0, 0.0, ALU.mult, ALU.add,
                                   small[:, 3, t:t + 1]).then_inc(s("vss"), 1)

        def vnorm(t):
            dve.wait_ge(s("vsd"), t + 1)
            own.then_wait(v.reciprocal(small[:, 5, t:t + 1], small[:, 4, t:t + 1]))
            stt(vn[:, t, :], vn[:, t, :], small[:, 5, t:t + 1], gvb, ALU.mult, ALU.mult).then_inc(s("vn_ready"), 1)

        def gate(m):
            w = CHUNK[m % 3][1]
            dve.wait_ge(s("gate_mm2"), m + 1)
            dve.wait_ge(s("freed_act"), freed_u0 + m + 1)
            if m >= 3:
                dve.wait_ge(s(f"a_st{m % 3}"), 16 * (m // 3))
            tt(ast[m % 3][:, 0:w], ps[:, 4 + m % 4, 0:w], ug[m % 3][:, 0:w], ALU.mult).then_inc(s("a_ready"), 1)

        def qk_sum(k):
            dve.wait_ge(s("sq_ready"), k + 1)
            v.tensor_reduce(stat[:, k % 2, :], sq[k % 2].rearrange("p (h d) -> p h d", d=HD), AX.X, ALU.add)\
                .then_inc(s("ss_ready"), 1)

        def qk_norm(k, i):
            t = k % TILES
            out = qn[k % 4].rearrange("p (h d) -> p h d", d=HD)
            dve.wait_ge(s("sd_ready"), k + 1)
            own.then_wait(v.reciprocal(stat[:, 4 + k % 2, :], stat[:, 2 + k % 2, :]))
            if k >= 4:
                dve.wait_ge(s("qk_tr"), k - 3)
                if kst[k - 4][k % 4]:
                    dve.wait_ge(s(f"k_st{k % 4}"), 16 * kst[k - 4][k % 4])
            ins = tt(out, bank(i % 4, WB).rearrange("p (h d) -> p h d", d=HD),
                     stat[:, 4 + k % 2, :].unsqueeze(2).to_broadcast([P, NH, HD]), ALU.mult).then_inc(s("freed_dve"), 1)
            dve.wait_ge(s("freed_dve"), k + 1)
            own.then_wait(tt(out, out, qg[:, k // (3 * TILES):k // (3 * TILES) + 1, :].to_broadcast([P, NH, HD]), ALU.mult))
            a_, b_ = rt[k % 2]
            ct = cst[:, CROPEC + 16 * t:CROPEC + 16 * t + 16].unsqueeze(1).to_broadcast([P, NH, 16])
            st = cst[:, CROPES + 16 * t:CROPES + 16 * t + 16].unsqueeze(1).to_broadcast([P, NH, 16])
            own.done(tt(a_, out[:, :, 0:16], ct, ALU.mult))
            own.then_wait(tt(b_, out[:, :, 0:16], st, ALU.mult))
            own.then_wait(tt(out[:, :, 0:8], a_[:, :, 0:8], b_[:, :, 8:16], ALU.add))
            tt(out[:, :, 8:16], a_[:, :, 8:16], b_[:, :, 0:8], ALU.add).then_inc(s("qn_ready"), 1)

        dve.wait_ge(s("const_in"), 32)
        scale_x(0)
        w_lo(0)
        at, m, k = 0, 0, 0
        for i, un in enumerate(units):
            kind = blocks[un[0]][0]
            if i and units[i - 1][0] != un[0]:
                at = i
            if un[0] == 0:
                if i + 1 < TILES:
                    scale_x(i + 1)
                x_full(i)
            elif un[0] == 4:
                vnorm_sum(un[1])
                if un[1]:
                    vnorm(un[1] - 1)
            elif un[0] == 5 and un[1] == 0:
                vnorm(TILES - 1)
                dve.wait_ge(s("const2_in"), 48)
                dve.wait_ge(s("masks_in"), 16)
            elif kind == "u":
                if m == 0:
                    dve.wait_ge(s("ws_T"), 1)
                    tt(wmT, pair(4), cst[:, CTRIL:CTRIL + P].unsqueeze(1).to_broadcast([P, AG, P]), ALU.mult)\
                        .then_inc(s("wm_ready"), 1)
                    dve.wait_ge(s("ws_rep"), 1)
                    tt(wmS[0:NSAMP, :, :].rearrange("p g (b t) -> p g b t", t=NS),
                       ps[0:NSAMP, 6, 0:AG * NS].rearrange("p (g t) -> p g t", t=NS).unsqueeze(2).to_broadcast([NSAMP, AG, NB, NS]),
                       cst[0:NSAMP, CBD:CBD + NB].unsqueeze(1).unsqueeze(3).to_broadcast([NSAMP, AG, NB, NS]), ALU.mult)\
                        .then_inc(s("wms_ready"), 1)
                else:
                    gate(m - 1)
                m += 1
            elif kind in ("q", "k"):
                if k == 0:
                    gate(m - 1)
                qk_sum(k)
                if k:
                    qk_norm(k - 1, i - 1)
                k += 1
            elif kind == "ga" and at == i and un[0] == 17:
                qk_norm(k - 1, i - 1)
            if i - at == (4 if kind in ("v", "va", "q", "k") else 2) and un[0] + 1 < NWIN:
                w_lo(un[0] + 1)
        for j in range(4):
            dve.wait_ge(s(f"sg_st{j}"), 16 * 12)
        NU = NG * NTILE
        for n in range(NU + 2):
            if n < NU:
                nk = nblk(n) * P
                dve.wait_ge(s("attn_s"), n + 1)
                if n:
                    dve.wait_ge(s("nm_ready"), n)
                own.then_wait(v.tensor_reduce(stat[:, 0, :].rearrange("p (b i) -> p b i", i=2),
                                              ps[:, 2 * (n % 2):2 * (n % 2) + 2, 0:2 * nk].rearrange("p b (i k) -> p b i k", k=nk),
                                              AX.X, ALU.max))
                if n >= 4:
                    dve.wait_ge(s(f"attn_st{n % 4}"), 16 * attn_n[n - 4][n % 4])
                own.done(tsc(ob[n % 4][:, :, HD + 1].rearrange("p (i b) -> p b i", b=2),
                             stat[:, 0, :].rearrange("p (b i) -> p b i", i=2), SCALE, None, ALU.mult))
                if n >= 2:
                    dve.wait_ge(s("attn_exp"), n - 1)
                tsc(nm[:, n % 2, :], stat[:, 0, :], -SCALE, None, ALU.mult).then_inc(s("nm_ready"), 1)
            if 1 <= n <= NU:
                j = n - 1
                dve.wait_ge(s("attn_tr"), j + 1)
                if j >= 2:
                    dve.wait_ge(s("attn_pv"), j - 1)
                cp(Pt[j % 2][:, 0:NH * nblk(j), :], pair(4)[:, 0:NH * nblk(j), :]).then_inc(s("attn_pt"), 1)
            if n >= 2:
                j = n - 2
                dve.wait_ge(s("attn_pv"), j + 1)
                if j >= 4:
                    dve.wait_ge(s(f"attn_st{j % 4}"), 16 * attn_n[j - 4][j % 4])
                cp(ob[j % 4][:, :, 0:HD], ps[:, 6 + j % 2, 0:GW].rearrange("p (h d) -> p h d", d=HD)).then_inc(s("attn_o"), 1)
        dve.wait_ge(s("qpad_zero"), 1)
        for half in range(2):
            rows = slice(64 * half, 64 * half + 64)
            cp(qpad[rows, :, NB * half:NB * half + NB, 0:NS], qTs[rows, :, :].rearrange("p a (b t) -> p a b t", t=NS))\
                .then_inc(s("qpad_ready"), 1)
        NSU = NG * NB
        for n in range(NSU + 1):
            if n < NSU:
                g, b = divmod(n, NB)
                nk = P * SKT[g]
                dve.wait_ge(s("sattn_s"), n + 1)
                if n:
                    dve.wait_ge(s("snm_ready"), n)
                own.then_wait(v.tensor_reduce(stat[:, 1, 0:1], flat(2 * (n % 2))[:, 0:nk + NS], AX.X, ALU.max))
                own.done(tsc(osb[:, b * NG + g, HD + 1:HD + 2], stat[:, 1, 0:1], SCALE, None, ALU.mult))
                if n >= 2:
                    dve.wait_ge(s("sattn_exp"), n - 1)
                tsc(snm[:, n % 2:n % 2 + 1], stat[:, 1, 0:1], -SCALE, None, ALU.mult).then_inc(s("snm_ready"), 1)
            if n >= 1:
                j = n - 1
                g, b = divmod(j, NB)
                dve.wait_ge(s("sattn_tr"), j + 1)
                if j >= 2:
                    dve.wait_ge(s("sattn_pv"), j - 1)
                own.done(cp(PTs[j % 2][:, 0:SKT[g], :], ps[:, 6, 0:P * SKT[g]].rearrange("p (a b) -> p a b", b=P)))
                cp(PTs[j % 2][0:NS, 4, :], ps[0:NS, 7, 0:P]).then_inc(s("sattn_pt"), 1)
                dve.wait_ge(s("sattn_pv"), j + 1)
                cp(osb[:, b * NG + g, 0:HD], ps[:, 7, 256:256 + HD]).then_inc(s("sattn_o"), 1)

        def b_lo(t):
            dve.wait_ge(s("bh_ready"), t + 1)
            w = NSAMP if t == ST else P
            cols = slice(col0(t), col0(t) + w)
            tt(bT[1][:, :, cols], ps[:, 4 + t % 2, 0:2 * P].rearrange("p (a b) -> p a b", b=P)[:, :, 0:w],
               bT[0][:, :, cols].bitcast(F32), ALU.subtract).then_inc(s("bT_ready"), 1)

        for t in range(TILES):
            dve.wait_ge(s(f"comb_in{t % 2}"), 16 * (t // 2 + 1))
            c_ = cs[t % 2]
            den, mx = (co[t % 2][:, :, HD + j].rearrange("p (g h) -> p g h", h=NH) for j in range(2))
            own.then_wait(v.tensor_reduce(c_[:, 0, :], mx.rearrange("p g h -> p h g"), AX.X, ALU.max))
            tt(c_[:, 1:4, :], mx, c_[:, 0:1, :].to_broadcast([P, NG, NH]), ALU.subtract).then_inc(s("cd_ready"), 1)
            dve.wait_ge(s("ce_ready"), t + 1)
            own.then_wait(tt(c_[:, 4:7, :], c_[:, 1:4, :], den, ALU.mult))
            own.then_wait(v.tensor_reduce(c_[:, 0, :], c_[:, 4:7, :].rearrange("p g h -> p h g"), AX.X, ALU.add))
            own.then_wait(v.reciprocal(c_[:, 7, :], c_[:, 0, :]))
            own.then_wait(tt(c_[:, 1:4, :], c_[:, 1:4, :], c_[:, 7:8, :].to_broadcast([P, NG, NH]), ALU.mult))
            if t >= 2:
                dve.wait_ge(s("bT_tr"), t - 1)
            x4 = lambda y: y.rearrange("p g (h d) -> p g h d", d=HD)
            own.then_wait(tt(x4(cb[t % 2]), co[t % 2][:, :, 0:HD].rearrange("p (g h) d -> p g h d", h=NH), c_[:, 1:4, :].unsqueeze(3).to_broadcast([P, NG, NH, HD]), ALU.mult))
            own.then_wait(tt(cb[t % 2][:, 0, :], cb[t % 2][:, 0, :], cb[t % 2][:, 1, :], ALU.add))
            tt(cb[t % 2][:, 0, :], cb[t % 2][:, 0, :], cb[t % 2][:, 2, :], ALU.add).then_inc(s("comb"), 1)
            if t:
                b_lo(t - 1)
        b_lo(TILES - 1)
        w_lo(NWIN)
        for i in range(3 * AG):
            g, c = divmod(i, 3)
            c0, w = CHUNK[c]
            dve.wait_ge(s("a_hi"), i + 1)
            tt(aT[1][:, g, c0:c0 + w], sga[i % 2][:, 0:w], aT[0][:, g, c0:c0 + w].bitcast(F32), ALU.subtract)\
                .then_inc(s("a_split"), 1)
        for m in range(3 * KT):
            dt, c = divmod(m, 3)
            c0, w = CHUNK[c]
            dve.wait_ge(s(f"sg_in{m % 2}"), 32 * (m // 2 + 1))
            dve.wait_ge(s("proj_mm"), m + 1)
            ga, gb = sga[m % 2][:, 0:w], sgb[m % 2][:, 0:w]
            own.done(tt(ga, ga, bank(m % 4, w), ALU.mult))
            own.then_wait(tt(gb, gb, bank(4 + m % 4, w), ALU.mult))
            tt(mT[:, dt, c0:c0 + w], ga, gb, ALU.add).then_inc(s("merge"), 1)
            if m % 6 == 2 and m // 6 < NPROJ - 1:
                w_lo(NWIN + 1 + m // 6)
        for n in range(NWIN + NPROJ, NSPLIT):
            w_lo(n)

        def m_lo(t):
            dve.wait_ge(s("m_hi"), t + 1)
            tt(ml[t % 2], mT[:, :, col0(t):col0(t) + P], mh[t % 2].bitcast(F32), ALU.subtract).then_inc(s("m_split"), 1)

        def logits(t):
            dve.wait_ge(s("rout_mm"), t + 1)
            tt(lgt[:, t, :], bank(6, RW), rbias, ALU.add).then_inc(s("route_in"), 1)

        m_lo(0)
        dve.wait_ge(s("rout_in"), 80)
        for t in range(TILES):
            if t + 1 < TILES:
                m_lo(t + 1)
            dve.wait_ge(s("out_mm"), t + 1)
            dve.wait_ge(s(f"xr_in{t % 2}"), 16 * (t // 2 + 1 + (t == ST)))
            tt(hbuf[:, t, :], flat(2 * (t % 2)), xr[t % 2], ALU.add).then_inc(s("h_ready"), 1)
            dve.wait_ge(s("sd2"), t + 1)
            own.then_wait(v.reciprocal(small[:, 2, t:t + 1], small[:, 1, t:t + 1]))
            if t >= 2:
                dve.wait_ge(s("x2_tr"), t - 1)
                dve.wait_ge(s(f"x2_st{t % 2}"), 16 * (t // 2))
            stt(x2[t % 2], hbuf[:, t, :], small[:, 2, t:t + 1], g2b, ALU.mult, ALU.mult).then_inc(s("x2_ready"), 1)
            if t >= 1:
                logits(t - 1)
        logits(TILES - 1)

        dve.wait_ge(s("route_in"), TILES)
        step = own.then_wait
        bc = lambda x, w: x.to_broadcast([P, TILES, w])
        lg, le = lgt[:, :, 0:NEG], lgt[:, :, NEG:RW].rearrange("p t (g e) -> p t g e", e=EGE)
        code4 = cst[:, CCODE4:CCODE4 + NEG].unsqueeze(1).to_broadcast([P, TILES, NEG])
        code8 = cst[:, CCODE8:CCODE8 + EGE].unsqueeze(1).to_broadcast([P, TILES, EGE])
        red = lambda out, x, op: step(v.tensor_reduce(out[:, :, 0] if len(out.shape) == 3 and out.shape[2] == 1 else out, x, AX.X, op))

        def first_of(x, best, code, tmp, top, onehot, w):
            red(best, x, ALU.max)
            step(tt(tmp, x, bc(best, w), ALU.is_equal))
            step(tt(tmp, tmp, code, ALU.mult))
            red(top, tmp, ALU.max)
            step(tt(onehot, tmp, bc(top, w), ALU.is_equal))

        first_of(lg, R["m4"], code4, R["eq4"], R["c4"], R["oh4"], NEG)
        tt(R["d4"], lg, bc(R["m4"], NEG), ALU.subtract).then_inc(s("rt_d4"), 1)
        step(tt(prod48, le, R["oh4"].unsqueeze(3).to_broadcast([P, TILES, NEG, EGE]), ALU.mult))
        red(R["sel"], prod48.rearrange("p t g e -> p t e g"), ALU.add)
        first_of(R["sel"], R["m1"], code8, R["t8"], R["c8"], R["oh1"], EGE)
        step(stt(R["le2"], R["oh1"], -BIG, R["sel"], ALU.mult, ALU.add))
        first_of(R["le2"], R["m2"], code8, R["t8"], R["c8"], R["oh2"], EGE)
        tt(R["ex"], R["m2"], R["m1"], ALU.subtract).then_inc(s("rt_dd"), 1)
        for n, oh in (("E1", "oh1"), ("E2", "oh2")):
            step(tt(R[n].rearrange("p t (g e) -> p t g e", e=EGE), R["oh4"].unsqueeze(3).to_broadcast([P, TILES, NEG, EGE]),
                    R[oh].unsqueeze(2).to_broadcast([P, TILES, NEG, EGE]), ALU.mult))
        step(tt(R["A"], R["E1"], R["E2"], ALU.add))
        valid = cst[:, CVALID:CVALID + TILES].unsqueeze(2).to_broadcast([P, TILES, NE])
        tt(Abf, R["A"], valid, ALU.mult).then_inc(s("assign"), 1)
        dve.wait_ge(s("rt_e4"), 1)
        red(R["s4"], R["d4"], ALU.add)
        step(v.reciprocal(R["pg"], R["s4"]))
        dve.wait_ge(s("rt_ex"), 1)
        step(tsc(R["dn"], R["ex"], 1.0, None, ALU.add))
        step(v.reciprocal(R["dn"], R["dn"]))
        step(tt(wts[:, :, 0:1], R["pg"], R["dn"], ALU.mult))
        step(tt(wts[:, :, 1:2], wts[:, :, 0:1], R["ex"], ALU.mult))
        dve.wait_ge(s("count_mm"), 1)
        step(cp(cnt[0:NE, 0:1], ps[0:NE, 1, 0:1]))
        step(tt(nbt[0:NE, :], cst[0:NE, CTHR:CTHR + 8], cnt[0:NE, 0:1].to_broadcast([NE, 8]), ALU.is_lt))
        step(v.tensor_reduce(cnt[0:NE, 1:2], nbt[0:NE, :], AX.X, ALU.add))
        cp(nbb[0:NE, :], cnt[0:NE, 1:2].to_broadcast([NE, P])).then_inc(s("over_cnt"), 1)
        step(cp(R["rank"], ps[:, 0, 0:TILES * NE].rearrange("p (t e) -> p t e", e=NE)))
        step(tsc(R["over"], R["rank"], float(P), None, ALU.is_ge))
        dve.wait_ge(s("over_mm"), 1)
        step(cp(ovl, ps[:, 2, 0:2 * NE].rearrange("p (a e) -> p a e", e=NE)))
        e128 = cst[:, CE128:CE128 + NE]
        step(tsc(obase, ovl[:, 0, :], float(P), float((NE - 1) * P), ALU.mult, ALU.add))
        step(tt(obase, obase, e128, ALU.subtract))
        over_b = obase.unsqueeze(1).to_broadcast([P, TILES, NE])
        step(tt(R["pos"], R["over"], over_b, ALU.mult))
        step(tt(R["pos"], R["pos"], R["rank"], ALU.add))
        step(tt(R["pos"], R["pos"], e128.unsqueeze(1).to_broadcast([P, TILES, NE]), ALU.add))
        for j, n in enumerate(("E1", "E2")):
            step(tt(R["pr"], R[n], R["pos"], ALU.mult))
            step(v.tensor_reduce(R["sl"][:, :, j], R["pr"], AX.X, ALU.add))
        step(cp(slot[:, :, :], R["sl"]))
        step(tsc(rowi, slot[:, :, :], P - 1, None, ALU.bitwise_and))
        step(tsc(blki, slot[:, :, :], 7, None, ALU.logical_shift_right))
        step(cp(R["rowf"], rowi))
        step(cp(R["blkf"], blki))
        step(stt(R["rowf"], R["rowf"], float(SLOTB), R["blkf"], ALU.mult, ALU.add))
        cp(addr, R["rowf"]).then_inc(s("addr_ready"), 1)
        step(tt(cmpo, ovl[:, 1:2, :].to_broadcast([P, OVER, NE]),
                cst[:, CBLK:CBLK + OVER].unsqueeze(2).to_broadcast([P, OVER, NE]), ALU.is_lt))
        step(v.tensor_reduce(obf[:, 0:OVER], cmpo, AX.X, ALU.add))
        step(tsc(obf[:, 0:OVER], obf[:, 0:OVER], float(NE - 1), None, ALU.min))
        step(cp(obf[:, OVER:OVER + 1], ovl[:, 1, NE - 1:NE]))
        cp(obe[:, 0:OVER + 1], obf[:, 0:OVER + 1]).then_inc(s("table_ready"), 1)

        def c_lo(b, off):
            dve.wait_ge(s("e_hi"), b * 6 + (off + 1))
            tt(elo[:, off % NSPL, :], eraw[:, off % NRAW, :], ehi[:, off % NSPL, :].bitcast(F32), ALU.subtract)\
                .then_inc(s("e_split"), 1)

        def xg_lo(b):
            dve.wait_ge(s("xg_hi"), b + 1)
            tt(xgl, pair(0), xgh.bitcast(F32), ALU.subtract).then_inc(s("xgT"), 1)

        def hidden(b):
            dve.wait_ge(s("silu"), b + 1)
            tt(hid, sil, bank(3), ALU.mult).then_inc(s("hid"), 1)

        def hid_lo(b):
            dve.wait_ge(s("hid_hi"), b + 1)
            tt(hTl, ps[:, 4, :].rearrange("p (k n) -> p k n", n=P), hTh.bitcast(F32), ALU.subtract).then_inc(s("hidT"), 1)

        dve.wait_ge(s("x2_st0"), 16 * 5)
        dve.wait_ge(s("x2_st1"), 16 * 4)
        for off in range(3):
            c_lo(0, off)
        xg_lo(0)
        c_lo(0, 3)
        c_lo(0, 4)
        hidden(0)
        xg_lo(1)
        c_lo(0, 5)
        c_lo(0, 6)
        hid_lo(0)

        def turn(b, last=False):
            for off in (1, 2, 3, 4):
                c_lo(b, off)
            hidden(b)
            if not last:
                xg_lo(b + 1)
            c_lo(b, 5)
            if not last:
                c_lo(b, 6)
            hid_lo(b)

        with dve.Fori(1, NE - 1) as b:
            turn(b)
        turn(NE - 1, last=True)
        nover = dve.value_load(obe[0:1, OVER:OVER + 1], min_val=0, max_val=OVER)
        with dve.Fori(0, OVER) as j2:
            with dve.If(j2 < nover):
                b = j2 + NE
                xg_lo(b)
                for off in range(6):
                    c_lo(b, off)
                hidden(b)
                hid_lo(b)
        for t in range(TILES):
            dve.wait_ge(s(f"yg_in{t % 2}"), 32 * (t // 2 + 1))
            if t >= 2:
                dve.wait_ge(s(f"y_out{t % 2}"), 16 * (t // 2))
            own.then_wait(stt(yo[t % 2], y1[t % 2], wts[:, t, 0:1], hbuf[:, t, :], ALU.mult, ALU.add))
            stt(yo[t % 2], y2[t % 2], wts[:, t, 1:2], yo[t % 2], ALU.mult, ALU.add).then_inc(s("yo_ready"), 1)

    @block.gpsimd
    def _(pool):
        dma = nc.gpsimd.dma_start
        dma(cbf[:, :], a["c_bf16"]).then_inc(s("masks_in"), 16)
        nc.gpsimd.memset(tabs[:, :], 0).then_inc(s("tabs_zero"), 1)
        nc.gpsimd.memset(zrow, 0.0).then_inc(s("zrow_ready"), 1)
        pool.wait_ge(s("tabs_zero"), 1)
        dma(tok_d.rearrange("(p b) o -> p (b o)", b=SLOTB), tabs[:, :]).then_inc(s("tok_zero"), 16)

        def window_store(kv, g, t, src, sm):
            w = DIL[g][0]
            if t == ST:
                keep = SKEEP[g]
                dst = o[f"sample_{kv}_w{w}"][0, :, keep - NS:keep].rearrange("b t h d -> b t (h d)")
                dma(dst, src[0:NSAMP, :]).then_inc(s(sm), 16)
            elif kept(g, t):
                r = P * t - (NPROMPT - KEEP[g])
                dma(o[f"prompt_{kv}_w{w}"][0, 0, r:r + P].rearrange("t h d -> t (h d)"), src).then_inc(s(sm), 16)

        va0 = 4 * TILES
        for k in range(NG * TILES):
            g, t = divmod(k, TILES)
            pool.wait_ge(s("freed_act"), va0 + k + 1)
            w = NSAMP if t == ST else P
            dma(v_d[col0(t):col0(t) + w, g * GW:(g + 1) * GW], vst[k % 4][0:w, :]).then_inc(s(f"v_st{k % 4}"), 16)
            window_store("v", g, t, vst[k % 4], f"v_st{k % 4}")
        pool.wait_ge(s("vn_ready"), TILES)
        dma(o["state_sgu_v_sample"][0].rearrange("b t c -> (b t) c"), vn[0:NSAMP, ST, :]).then_inc(s("vn_out"), 16)
        for m in range(3 * AG):
            g, c = divmod(m, 3)
            c0, w = CHUNK[c]
            pool.wait_ge(s("a_ready"), m + 1)
            dma(a_d[g, :, c0:c0 + w], ast[m % 3][:, 0:w]).then_inc(s(f"a_st{m % 3}"), 16)
        for k in range(NG * TILES, 2 * NG * TILES):
            g, t = k // TILES - NG, k % TILES
            if kept(g, t):
                pool.wait_ge(s("qn_ready"), k + 1)
                window_store("k", g, t, qn[k % 4], f"k_st{k % 4}")
        for k in range(48):
            i, c = divmod(k, 3)
            c0, w = CHUNK[c]
            pool.wait_ge(s("freed_act"), freed_g0 + k + 1)
            dma(sg_d[i // KT, i % KT, :, c0:c0 + w], sgs[k % 4][:, 0:w]).then_inc(s(f"sg_st{k % 4}"), 16)
        pool.wait_ge(s("unit_mm"), len(units))
        nc.gpsimd.memset(qpad, 0.0).then_inc(s("qpad_zero"), 1)
        for n in range(NG * NTILE):
            g, j = divmod(n, NTILE)
            pool.wait_ge(s("attn_o"), n + 1)
            rows = value_rows(g, j)
            rows = rows if g == 2 else rows[-1:]
            for i, (f, _) in enumerate(rows):
                part = slice(64 * i, 64 * i + 64) if g == 2 else slice(0, P)
                dma(f(ao_d[NSAMP:T, g].rearrange("t h c -> t (h c)")), ob[n % 4][part].rearrange("p h c -> p (h c)"))\
                    .then_inc(s(f"attn_st{n % 4}"), 16)
        pool.wait_ge(s("sattn_o"), NG * NB)
        for hd in range(NH):
            src = osb[32 * hd:32 * hd + NS, :, :].rearrange("p (b g) c -> p b g c", g=NG)
            for g in range(NG):
                dst = ao_d[0:NSAMP, g, hd, :].rearrange("(b t) c -> t b c", t=NS)
                dma(dst, src[:, :, g, :]).then_inc(s("sattn_stored"), 16)
        for t in range(TILES):
            pool.wait_ge(s("x2_ready"), t + 1)
            w = NSAMP if t == ST else P
            dma(xn_d[col0(t):col0(t) + w, :], x2[t % 2][0:w, :]).then_inc(s(f"x2_st{t % 2}"), 16)
        pool.wait_ge(s("tok_zero"), 16)
        pool.wait_ge(s("addr_ready"), 1)
        for t in range(TILES):
            w = NSAMP if t == ST else P
            for j in range(2):
                pool.indirect_dma_start(tok_d, bass.IndirectOffsetOnAxis(ap=addr[0:w, t, j:j + 1], axis=0), ids[0:w, t:t + 1], None)\
                    .then_inc(s("scattered"), 16)
        pool.wait_ge(s("scattered"), 32 * TILES)
        dma(tabs[:, :], tok_d.rearrange("(p b) o -> p (b o)", b=SLOTB)).then_inc(s("tabs_in"), 16)
        pool.wait_ge(s("tabs_in"), 16)
        pool.wait_ge(s("x2_st0"), 16 * 5)
        pool.wait_ge(s("x2_st1"), 16 * 4)
        pool.wait_ge(s("table_ready"), 1)

        def gather(b):
            nc.gpsimd.tensor_copy(idxc[:, 0:1], tabs[:, bass.ds(b, 1)]).then_inc(s("idx_ready"), 1)
            pool.wait_ge(s("idx_ready"), b + 1)
            pool.sem_inc(s("gathers"), 1)
            pool.indirect_dma_start(xg, None, xn_d, bass.IndirectOffsetOnAxis(ap=idxc[:, 0:1], axis=0)).then_inc(s("xg_in"), 16)

        gather(0)
        with pool.Fori(1, NE) as b:
            pool.wait_ge(s("xg_tr"), b)
            gather(b)
        nover = pool.value_load(obe[0:1, OVER:OVER + 1], min_val=0, max_val=OVER)
        with pool.Fori(0, OVER) as j2:
            with pool.If(j2 < nover):
                pool.wait_ge(s("xg_tr"), j2 + NE)
                gather(j2 + NE)
                pool.wait_ge(s("y_st"), j2 * 16 + 16 * (NE + 1))
        pool.wait_ge(s("y_zero"), 16)
        pool.wait_ge(s("y_st"), 16 * NE)
        for t in range(TILES):
            if t >= 2:
                pool.wait_ge(s("yo_ready"), t - 1)
            for j, dst in enumerate((y1[t % 2], y2[t % 2])):
                pool.indirect_dma_start(dst, None, y_d, bass.IndirectOffsetOnAxis(ap=slot[:, t, j:j + 1], axis=0))\
                    .then_inc(s(f"yg_in{t % 2}"), 16)


_INS = ["x_prompt", "x_sample", "cache_k_w128", "cache_v_w128", "cache_k_w512", "cache_v_w512", "cache_k_w2048",
        "cache_v_w2048", "norm1_g", "w_in", "v_norm_g", "w_spatial", "b_spatial", "q_norm_g", "k_norm_g", "w_proj_a",
        "w_proj_b", "w_out", "norm2_g", "w_group_router", "b_group_router", "w_expert_router", "b_expert_router",
        "w_gate", "w_up", "w_down"]
_OUTS = [("y_prompt", (1, NPROMPT, D)), ("y_sample", (NB, NS, D))]
_OUTS += [(f"prompt_{kv}_w{DIL[g][0]}", (1, 1, KEEP[g], NH, HD)) for g in range(NG) for kv in "kv"]
_OUTS += [(f"sample_{kv}_w{DIL[g][0]}", (1, NB, SKEEP[g], NH, HD)) for g in range(NG) for kv in "kv"]
_OUTS += [("state_sgu_v_sample", (1, NB, NS, D))]


def kernel(**inputs):
    import concourse.bacc as bacc
    from concourse.bass_utils import run_bass_kernel_spmd

    nc = bacc.Bacc("TRN2", target_bir_lowering=False, num_devices=1)
    arrays, a, o = {}, {}, {}
    given = {n: np.ascontiguousarray(inputs[n]) for n in _INS}
    given.update(constants())
    for n, x in given.items():
        arrays[n] = x
        a[n] = nc.dram_tensor(n, x.shape, mybir.dt.from_np(x.dtype), kind="ExternalInput").ap()
    for n, shape in _OUTS:
        o[n] = nc.dram_tensor("out_" + n, shape, F32, kind="ExternalOutput").ap()
    build(nc, a, o)
    r = run_bass_kernel_spmd(nc, [arrays], core_ids=[0])
    return tuple(r.results[0]["out_" + n] for n, _ in _OUTS)
```

```python
from contextlib import ExitStack

import numpy as np
import concourse.bass as bass
from concourse import mybir

F32 = mybir.dt.float32
F32R = mybir.dt.float32r
BF16 = mybir.dt.bfloat16
I32 = mybir.dt.int32
ALU = mybir.AluOpType
ACT = mybir.ActivationFunctionType
AX = mybir.AxisListType

P = 128
D = 1024
KT = D // P
NPROMPT, NB, NS, PAST = 1024, 8, 8, 512
NSAMP = NB * NS
T = NPROMPT + NSAMP
NTILE = NPROMPT // P
TILES = NTILE + 1
ST = NTILE
HD, NH = 64, 4
GW = HD * NH
DIL = ((128, 1), (512, 4), (2048, 16))
NG = len(DIL)
KEEP = [min(w, NPROMPT) for w, _ in DIL]
PKEEP = [min(w, PAST) for w, _ in DIL]
SKEEP = [min(w, PAST + NS) for w, _ in DIL]
AG = 8
C_U, C_V, C_Q = 0, D, 2 * D
C_K, C_VA = C_Q + NG * GW, C_Q + 2 * NG * GW
C_GA = C_Q + 3 * NG * GW
C_GB = C_GA + D
WB = 256
NEG, EGE = 4, 8
NE = NEG * EGE
DE = D // 2
RW = NEG + NE
OVER = 16
SLOTB = NE + OVER
EMPTY = 4096
EPS = 1e-6
SCALE = HD ** -0.5
BIG = 1e30
SKT = [1, 4, 2]
SNK = [P * k + NS for k in SKT]
CHUNK = [(NSAMP + 2 * P, 3 * P), (NSAMP + 5 * P, 3 * P), (0, NSAMP + 2 * P)]
CHUNK_T = [(2, 3, 4), (5, 6, 7), (0, 1)]

(CI, CROPEC, CROPES, CBD, CREP, CTRIL, CCODE4, CCODE8, CE128, CTHR, CBLK, CVALID, CEPS, CONE, CIOTA, CID, CEND) = np.cumsum(
    [0, P, TILES * 16, TILES * 16, NB, NSAMP, P, NEG, EGE, NE, 8, OVER, TILES, 1, P, P, 2 * TILES]).tolist()
(BI, BPO, BPAIR, BS0, BS1, BS2, BLT, BONE, BLS, BLI, BEND) = np.cumsum(
    [0, P, 2 * P, P, SNK[0], SNK[1], SNK[2], P, P, NE, NE]).tolist()


def col0(t):
    return 0 if t == ST else NSAMP + P * t


def constants():
    c = np.zeros((P, CEND), np.float32)
    p = np.arange(P)
    c[:, CI:CI + P] = np.eye(P)
    inv = np.float32(500000.0) ** (-np.arange(8, dtype=np.float32) * np.float32(2.0) / np.float32(16))
    for t in range(TILES):
        pos = (PAST + p % NS if t == ST else P * t + p).astype(np.float32)
        ang = (pos[:, None] * inv[None, :]).astype(np.float32)
        co, si = np.cos(ang), np.sin(ang)
        c[:, CROPEC + 16 * t:CROPEC + 16 * t + 16] = np.concatenate([co, co], 1)
        c[:, CROPES + 16 * t:CROPES + 16 * t + 16] = np.concatenate([si, -si], 1)
    c[:NSAMP, CBD:CBD + NB] = (p[:NSAMP, None] // NS == np.arange(NB)[None])
    c[:NS, CREP:CREP + NSAMP] = (p[:NS, None] == np.arange(NSAMP)[None] % NS)
    c[:, CTRIL:CTRIL + P] = (p[None, :] >= p[:, None])
    c[:, CCODE4:CCODE4 + NEG] = NEG - np.arange(NEG)
    c[:, CCODE8:CCODE8 + EGE] = EGE - np.arange(EGE)
    c[:, CE128:CE128 + NE] = P * np.arange(NE)
    c[:, CTHR:CTHR + 8] = P * (1 + np.arange(8)) + 0.5
    c[:, CBLK:CBLK + OVER] = np.arange(OVER) + 0.5
    c[:, CVALID:CVALID + TILES] = 1
    c[NSAMP:, CVALID + ST] = 0
    c[:, CEPS] = EPS
    c[:, CONE:CONE + P] = 1
    c[:, CIOTA:CIOTA + P] = np.arange(P)
    for t in range(TILES):
        c[:NSAMP if t == ST else P, CID + 2 * t] = (2 * (col0(t) + p) - EMPTY)[:NSAMP if t == ST else P]
        c[:NSAMP if t == ST else P, CID + 2 * t + 1] = (2 * (col0(t) + p) + 1 - EMPTY)[:NSAMP if t == ST else P]
    b = np.zeros((P, BEND), np.float32)
    b[:, BI:BI + P] = np.eye(P)
    b[:, BPO:BPO + P] = np.where(p[None, :] >= p[:, None], 0, -BIG)
    b[:, BPO + P:BPO + 2 * P] = np.where(p[None, :] <= p[:, None], 0, -BIG)
    same = p[None, :] // 64 == p[:, None] // 64
    b[:, BPAIR:BPAIR + P] = np.where(same & (p[None, :] <= p[:, None]), 0, -BIG)
    step = (p % 32) % NS
    for g, off in enumerate((BS0, BS1, BS2)):
        win, dil = DIL[g]
        nc_ = P * SKT[g]
        n = np.arange(nc_)
        key = (n // NS) * 16 + n % NS if g == 2 else n
        key = np.concatenate([key, PKEEP[g] + np.arange(NS)])
        dist = PKEEP[g] + step[:, None] - key[None, :]
        ok = (dist >= 0) & (dist <= win) & (dist % dil == 0)
        b[:, off:off + SNK[g]] = np.where(ok, 0, -BIG)
    b[:, BLT:BLT + P] = (p[:, None] < p[None, :])
    b[:, BONE:BONE + P] = 1
    e = np.arange(NE)
    b[:NE, BLS:BLS + NE] = e[:, None] < e[None, :]
    b[:NE, BLI:BLI + NE] = e[:, None] <= e[None, :]
    return {"c_f32": c, "c_bf16": b}


class Steps:

    def __init__(self, eng, sem):
        self.eng, self.sem, self.n = eng, sem, 0

    def done(self, ins):
        ins.then_inc(self.sem, 1)
        self.n += 1
        return self.n

    def then_wait(self, ins):
        self.eng.wait_ge(self.sem, self.done(ins))


def build(nc, a, o):
    ctx = ExitStack()
    with ctx:
        _build(nc, ctx, a, o)


def _build(nc, ctx, a, o):
    def sb(name, shape, dt=F32):
        return ctx.enter_context(nc.sbuf_tensor(name, shape, dt))

    def sem(name):
        return ctx.enter_context(nc.semaphore(name))

    def dram(name, shape, dt=F32):
        return nc.dram_tensor(name, shape, dt).ap()

    a_d = dram("a_scratch", [AG, P, T])
    sg_d = dram("gate_scratch", [2, KT, P, T])
    v_d = dram("v_scratch", [T, NG * GW])
    ao_d = dram("attn_scratch", [T, NG, NH, HD + 2])
    xn_d = dram("xn2_scratch", [T, D])
    y_d = dram("expert_out_scratch", [2 * T, D])

    cst = sb("cst", [P, CEND])
    cbf = sb("cbf", [P, BEND], BF16)
    ident = cst[:, CI:CI + P]
    identb = cbf[:, BI:BI + P]
    eps = cst[:, CEPS:CEPS + 1]
    g1T = sb("g1T", [P, KT])
    qg = sb("qg", [P, 2, HD])

    NA = 50600
    ARENA = nc.sbuf_base
    arena = sb("arena", [P, NA])
    assert nc.sbuf_base - ARENA == 4 * NA
    parts = []

    class Lay:
        def __init__(self, at):
            self.at = at

        def take(self, *shape, dt=F32):
            n = int(np.prod(shape))
            parts.append(self.at)
            v = nc.alloc_sbuf_tensor_at(f"part{len(parts)}", [P, n], dt, offset=ARENA + 4 * self.at)[:, :]
            self.at += -(-n // 8) * 8
            assert self.at <= NA, self.at
            if len(shape) == 2:
                v = v.rearrange("p (a b) -> p a b", b=shape[1])
            elif len(shape) == 3:
                v = v.rearrange("p (a b c) -> p a b c", b=shape[1], c=shape[2])
            return v

    lay = Lay(0)
    xT = [lay.take(KT, T, dt=F32R), lay.take(KT, T, dt=F32R)]
    WSLOT = 10 * WB
    wraw = lay.take(WSLOT)
    SLOT0 = lay.at
    whi, wlo = zip(*[[lay.take(WSLOT, dt=F32R) for _ in range(2)] for _ in range(2)])
    AFTER_W = lay.at
    l1 = Lay(AFTER_W)
    xin = [l1.take(D) for _ in range(2)]
    xs = [l1.take(D) for _ in range(2)]
    xfull = l1.take(KT, P)
    junk1 = l1.take(D)
    l2 = Lay(l1.at)
    vn = l2.take(TILES, D)
    l2b = Lay(AFTER_W)
    gvb = l2b.take(D)
    bsr = l2b.take(AG, P)
    junk2 = l2b.take(D)
    wsp = l2b.take(AG, P)
    wmT = l2b.take(AG, P)
    wmS = l2b.take(AG, NSAMP)
    assert l2b.at <= l1.at
    ug = [l2.take(512) for _ in range(3)]
    ast = [l2.take(512) for _ in range(3)]
    vst = [l2.take(GW) for _ in range(4)]
    l3 = Lay(AFTER_W)
    qTs = l3.take(6, NSAMP)
    kTs = l3.take(6, NSAMP)
    AFTER_S = l3.at
    qT = l3.take(6, NPROMPT)
    kT = l3.take(6, NPROMPT)
    AFTER_QK = l3.at
    qn = [l3.take(GW) for _ in range(4)]
    sq = [l3.take(GW) for _ in range(2)]
    rt = [[l3.take(NH, 16) for _ in range(2)] for _ in range(2)]
    sgs = [l3.take(512) for _ in range(4)]
    la = Lay(AFTER_QK)
    ob = [la.take(NH, HD + 2) for _ in range(4)]
    vg = [la.take(2, GW) for _ in range(2)]
    Eb = [la.take(NH, 2 * P) for _ in range(2)]
    Pt = [la.take(NH * 2, P) for _ in range(2)]
    lc = Lay(AFTER_QK)
    co = [lc.take(NG * NH, HD + 2) for _ in range(2)]
    cb = [lc.take(NG, GW) for _ in range(2)]
    sga = [lc.take(512) for _ in range(2)]
    sgb = [lc.take(512) for _ in range(2)]
    ls = Lay(SLOT0)
    qpad = ls.take(6 * NB, 2, 32)
    kc = [ls.take(4, GW) for _ in range(2)]
    assert ls.at <= SLOT0 + 2 * WSLOT
    ls = Lay(AFTER_S)
    vc = [ls.take(5, GW) for _ in range(3)]
    KTs = [ls.take(2, 512) for _ in range(2)]
    PTs = [ls.take(5, P) for _ in range(2)]
    Es = [ls.take(528)]
    cs = [ls.take(8, NH) for _ in range(2)]
    assert ls.at <= AFTER_W + KT * T
    Es.append(lc.take(528))
    osb = lc.take(NB * NG, HD + 2)
    lm = Lay(AFTER_W)
    mT = lm.take(KT, T)
    bT = [lm.take(2, T, dt=F32R), lm.take(2, T, dt=F32R)]
    assert lm.at <= AFTER_QK
    aT = xT
    lw = Lay(0)
    wo = [lw.take(KT, D, dt=F32R), lw.take(KT, D, dt=F32R)]
    assert lw.at <= 2 * KT * T
    wo_raw = [Lay(at).take(KT, WB) for at in (2 * KT * T, SLOT0 + 2 * WSLOT, SLOT0 + 2 * WSLOT + KT * WB, AFTER_QK)]
    AFTER_M = AFTER_W + KT * T
    lh = Lay(AFTER_M)
    hbuf = lh.take(TILES, D)
    AFTER_H = lh.at
    xr = [lh.take(D) for _ in range(2)]
    wr = lh.take(KT, RW)
    rbias = lh.take(RW)
    lh2 = Lay(2 * KT * T + WSLOT)
    mh = [lh2.take(KT, P, dt=F32R) for _ in range(2)]
    ml = [lh2.take(KT, P, dt=F32R) for _ in range(2)]
    x2 = [lh2.take(D) for _ in range(2)]
    x2T = [lh2.take(KT, P) for _ in range(2)]
    junk3 = lh2.take(D)
    g2b = lh2.take(D)
    assert lh2.at <= AFTER_W
    lgt = sb("lgt", [P, TILES, RW])
    wts = sb("wts", [P, TILES, 2])
    small = sb("small", [P, 8, TILES])
    tabs = sb("tabs", [P, SLOTB], I32)
    obe = sb("obe", [P, 24], I32)
    tabt = sb("tabt", [P, SLOTB], I32)
    idxc = sb("idxc", [P, 1], I32)
    idxy = sb("idxy", [P, 1], I32)
    stat = sb("stat", [P, 8, NH])
    nm = sb("nm", [P, 2, NH])
    snm = sb("snm", [P, 2])
    lr = Lay(AFTER_W)
    R = {n: lr.take(TILES, w) for n, w in (
        ("m4", 1), ("d4", NEG), ("s4", 1), ("eq4", NEG), ("oh4", NEG), ("c4", 1), ("pg", 1),
        ("sel", EGE), ("t8", EGE), ("m1", 1), ("c8", 1), ("oh1", EGE), ("le2", EGE), ("m2", 1),
        ("oh2", EGE), ("ex", 1), ("dn", 1), ("E1", NE), ("E2", NE), ("A", NE), ("rank", NE),
        ("over", NE), ("pos", NE), ("pr", NE), ("sl", 2), ("rowf", 2), ("blkf", 2))}
    prod48 = lr.take(TILES * NEG, EGE)[:, :, :].rearrange("p (t g) e -> p t g e", g=NEG)
    Abf = lr.take(TILES * NE)[:, :].bitcast(BF16)[:, 0:TILES * NE].rearrange("p (a b) -> p a b", b=NE)
    cnt = lr.take(8)
    nbt = lr.take(8)
    nbb = lr.take(P).bitcast(BF16)[:, 0:P]
    ovl = lr.take(2, NE)
    obase = lr.take(NE)
    cmpo = lr.take(OVER, NE)
    obf = lr.take(24)
    sloti = lr.take(TILES * 2, dt=I32).rearrange("p (a b) -> p a b", b=2)
    rowi = lr.take(TILES * 2, dt=I32).rearrange("p (a b) -> p a b", b=2)
    blki = lr.take(TILES * 2, dt=I32).rearrange("p (a b) -> p a b", b=2)
    in_row = lr.take(2 * TILES, P, dt=F32R)
    in_col = lr.take(2 * TILES, SLOTB)
    num_col = lr.take(2 * TILES, SLOTB, dt=F32R)
    assert lr.at <= AFTER_M
    NRAW, NSPL = 6, 3
    CW = 2048
    le_ = Lay(0)
    eraw = le_.take(NRAW, CW)
    ehi = le_.take(NSPL, CW, dt=F32R)
    elo = le_.take(NSPL, CW, dt=F32R)
    xg = le_.take(D)
    xgh = le_.take(KT, P, dt=F32R)
    xgl = le_.take(KT, P, dt=F32R)
    sil = le_.take(DE)
    hid = le_.take(DE)
    hTh = le_.take(4, P, dt=F32R)
    hTl = le_.take(4, P, dt=F32R)
    assert le_.at <= AFTER_W
    yb = Lay(AFTER_H).take(D)
    lf = Lay(0)
    yy = [lf.take(2, D) for _ in range(3)]
    yo = [lf.take(D) for _ in range(2)]

    ps = ctx.enter_context(nc.psum_tensor("ps", [P, 8, 512], F32))

    def bank(b, n=512):
        return ps[:, b, 0:n]

    def pair(b):
        return ps[:, b:b + 2, :].rearrange("p b (c n) -> p (b c) n", n=P)

    def flat(b):
        return ps[:, b:b + 2, :].rearrange("p b n -> p (b n)")

    S = {}

    def s(name):
        if name not in S:
            S[name] = sem(name)
        return S[name]

    blocks = [("va", C_VA)] + [("v", C_V + WB * i) for i in range(4)] + [("va", C_VA + GW * g) for g in range(1, NG)]
    blocks += [("u", C_U + WB * i) for i in range(4)]
    blocks += [("q", C_Q + GW * g) for g in range(NG)] + [("k", C_K + GW * g) for g in range(NG)]
    blocks += [("ga", C_GA + WB * i) for i in range(4)] + [("gb", C_GB + WB * i) for i in range(4)]
    NWIN = len(blocks)
    assert NWIN == 25
    NPROJ = 4
    NSPLIT = NWIN + NPROJ + 4
    w_in_v = a["w_in"][0].rearrange("(k p) c -> p k c", p=P)
    wpa_v = a["w_proj_a"][0].rearrange("(k p) c -> p k c", p=P)
    wpb_v = a["w_proj_b"][0].rearrange("(k p) c -> p k c", p=P)
    wout_v = a["w_out"][0].rearrange("(k p) c -> p k c", p=P)

    def wslot(n):
        k = 10 if NWIN <= n < NWIN + NPROJ else KT
        if n >= NWIN + NPROJ:
            j = n - NWIN - NPROJ
            return (wo_raw[j],) + tuple(w[:, :, WB * j:WB * (j + 1)] for w in wo)
        hi, lo = (w[n % 2][:, 0:k * WB].rearrange("p (k c) -> p k c", c=WB) for w in (whi, wlo))
        return wraw[:, 0:k * WB].rearrange("p (k c) -> p k c", c=WB), hi, lo

    units = []
    for n, (kind, _) in enumerate(blocks):
        if kind in ("v", "va", "q", "k"):
            units += [(n, t) for t in range(TILES)]
        else:
            units += [(n, ct, c) for ct in range(2) for c in range(3)]
    readers, freed = [], {"act": 0, "dve": 0}
    for un in units:
        eng_ = "dve" if blocks[un[0]][0] in ("q", "k") else "act"
        freed[eng_] += 1
        readers.append((eng_, freed[eng_]))
    freed_u0 = 7 * TILES
    freed_g0 = 7 * TILES + 3 * AG
    last_unit = {un[0]: i + 1 for i, un in enumerate(units)}


    def first_chunks():
        return [("gu", j, j, 0) for j in range(4)]

    def loop_chunks(b):
        return [("gu", j, j - 2, b) for j in range(4)] + [("down", j, 2 + j, b - 1) for j in range(2)]

    def last_chunks():
        return [("down", j, 4 + j, NE - 1) for j in range(2)]

    def over_chunks(expert):
        return [("gu", j, j, expert) for j in range(4)] + [("down", j, 4 + j, expert) for j in range(2)]

    merges = [(n, ct, c) for n in range(NPROJ) for ct, c in ((0, 0), (0, 1), (1, 0), (1, 1), (0, 2), (1, 2))]

    def combine(n):
        return [(i, (n - 2 - i) // 3) for i in range(4) if n >= 2 + i and (n - 2 - i) % 3 == 0 and (n - 2 - i) // 3 < NTILE]

    def store_counts(n, ring, stores):
        seen, out = [0] * ring, []
        for i in range(n):
            seen[i % ring] += stores(i)
            out.append(list(seen))
        return out

    def kept(g, t):
        return t == ST or P * t >= NPROMPT - KEEP[g]

    vst_n = store_counts(NG * TILES, 4, lambda i: 1 + kept(i // TILES, i % TILES))
    kst = store_counts(2 * NG * TILES, 4, lambda i: int(i >= NG * TILES and kept(i // TILES - NG, i % TILES)))

    def value_rows(g, j):
        dil = DIL[g][1]
        if g == 0:
            lst = ([(lambda v, i=j - 1: v[P * i:P * i + P, :], 0)] if j else []) + [(lambda v, i=j: v[P * i:P * i + P, :], 1)]
        elif g == 1:
            r, n = j // 2, j % 2
            f = lambda v, i: v.rearrange("(n q r) c -> r n q c", r=dil, q=P)[r, i, :, :]
            lst = ([(lambda v: f(v, n - 1), 0)] if n else []) + [(lambda v: f(v, n), 1)]
        else:
            lst = [(lambda v, r=2 * j + i: v.rearrange("(q r) c -> r q c", r=dil)[r, :, :], 0) for i in range(2)]
        return lst

    def qcols(x, g, j, which):
        dil = DIL[g][1]
        if g == 0:
            i = j + which
            return x[:, P * i:P * i + P]
        if g == 1:
            r, n = j // 2, j % 2 + which
            return x[:, P * dil * n + r:P * dil * (n + 1):dil]
        raise AssertionError

    attn_n = store_counts(NG * NTILE, 4, lambda n: 2 if n // NTILE == 2 else 1)
    sattn_stores = NH * NG
    NSU = NG * NB

    def nblk(n):
        g, j = divmod(n, NTILE)
        return 1 if g == 2 or (g == 0 and j == 0) or (g == 1 and j % 2 == 0) else 2

    def vg_count(n):
        return 16 * sum(len(value_rows(*divmod(m, NTILE))) for m in range(n % 2, n + 1, 2))

    def cache_count(n, ring, extra):
        return 16 * sum((1, 1, SKT[2])[m // NB] + extra for m in range(n % ring, n + 1, ring))

    def w_in_count(n):
        return 16 * (n + 1 + max(0, min(n - NWIN + 1, NPROJ)))

    def chunk_uses(off):
        return off // NRAW + 1

    block = ctx.enter_context(nc.Block())

    @block.sync
    def _(sp):
        dma = nc.sync.dma_start

        def load_x(dst, t):
            if t == ST:
                dma(dst[0:NSAMP, :], a["x_sample"].rearrange("b s d -> (b s) d")).then_inc(s(f"x_in{t % 2}"), 16)
                dma(dst[NSAMP:P, :], a["x_prompt"][0, 0:P - NSAMP, :]).then_inc(s(f"x_in{t % 2}"), 16)
            else:
                dma(dst[:, :], a["x_prompt"][0, P * t:P * t + P, :]).then_inc(s(f"x_in{t % 2}"), 16)

        def load_w(n):
            if n >= 1:
                sp.wait_ge(s("w_split"), n)
            raw = wslot(n)[0]
            if n < NWIN:
                c = blocks[n][1]
                dma(raw, w_in_v[:, :, c:c + WB]).then_inc(s("w_in"), 16)
            elif n < NWIN + NPROJ:
                c = WB * (n - NWIN)
                dma(raw[:, 0:KT, :], wpa_v[:, :, c:c + WB]).then_inc(s("w_in"), 16)
                dma(raw[:, KT:10, :], wpb_v[:, :, c:c + WB]).then_inc(s("w_in"), 16)

        def load_wout(j):
            dma(wo_raw[j], wout_v[:, :, WB * j:WB * (j + 1)]).then_inc(s(f"wout_in{j // 2}"), 16)

        load_x(xin[0], 0)
        dma(cst[:, :], a["c_f32"]).then_inc(s("const_in"), 16)
        dma(g1T[:, :], a["norm1_g"][0].rearrange("(k p) -> p k", p=P), allow_slow_non_contiguous=True).then_inc(s("const_in"), 16)
        load_w(0)
        load_x(xin[1], 1)
        for j, n in enumerate(("q_norm_g", "k_norm_g")):
            dma(qg[:, j, :], a[n][0].partition_broadcast(P)).then_inc(s("const2_in"), 16)
        for t in range(2, TILES):
            sp.wait_ge(s("xs_ready"), t - 1)
            load_x(xin[t % 2], t)
            if t == 3:
                load_w(1)
        sp.wait_ge(s("xn_ready"), TILES)
        dma(wsp, a["w_spatial"][0].rearrange("g t s -> t g s")).then_inc(s("gate_in"), 16)
        dma(bsr[0:1, :, :], a["b_spatial"]).then_inc(s("gate_in"), 16)
        dma(gvb, a["v_norm_g"][0].partition_broadcast(P)).then_inc(s("gate_in"), 16)
        pieces = []
        for g in range(NG):
            pieces += [(g, kv, b) for kv in "kv" for b in ([slice(0, NB)] if g == 0 else [slice(i, i + 1) for i in range(NB)])]
        assert len(pieces) <= 2 * (NWIN - 3)
        for n in range(2, NWIN):
            load_w(n)
            for g, kv, b in (pieces[2 * (n - 3):2 * (n - 2)] if n >= 3 else []):
                w = DIL[g][0]
                drop = PKEEP[g] + NS - SKEEP[g]
                dma(o[f"sample_{kv}_w{w}"][0, b, 0:PKEEP[g] - drop], a[f"cache_{kv}_w{w}"][0, b, drop:PKEEP[g]])\
                    .then_inc(s("cache_out"), 16)

        for j in range(4):
            sp.wait_ge(s(f"v_st{j}"), 16 * vst_n[-1][j])
            sp.wait_ge(s(f"k_st{j}"), 16 * kst[-1][j])
            sp.wait_ge(s(f"sg_st{j}"), 16 * 12)
        sp.wait_ge(s("qk_T"), 2 * NG * TILES)
        for n in range(NG * NTILE):
            g, j = divmod(n, NTILE)
            if n >= 2:
                sp.wait_ge(s("attn_pv"), n - 1)
            for i, (rows, k) in enumerate(value_rows(g, j)):
                dst = vg[n % 2][:, k, :]
                if g == 2:
                    dst = vg[n % 2][64 * i:64 * i + 64, 0, :]
                dma(dst, rows(v_d[NSAMP:T, g * GW:(g + 1) * GW])).then_inc(s(f"vg_in{n % 2}"), 16)
        def load_cache(kv, n, dst):
            g, b = divmod(n, NB)
            src = a[f"cache_{kv}_w{DIL[g][0]}"][0, b].rearrange("n h d -> n (h d)")
            done = s(f"{kv}c_in{n % (2 if kv == 'k' else 3)}")
            if g < 2:
                dma(dst[:, 0:SKT[g], :], src[0:P * SKT[g], :].rearrange("(i p) c -> p i c", p=P)).then_inc(done, 16)
            else:
                for i in range(SKT[g]):
                    dma(dst[:, i, :], src.rearrange("(m r) c -> m r c", r=16)[16 * i:16 * i + 16, 0:NS, :]).then_inc(done, 16)

        def load_combined(t):
            dma(co[t % 2], ao_d[col0(t):col0(t) + P].rearrange("t g h c -> t (g h) c")).then_inc(s(f"comb_in{t % 2}"), 16)

        load_w(NWIN)
        load_cache("k", 0, kc[0])
        sp.wait_ge(s("attn_s"), NG * NTILE)
        for n in range(NSU):
            g, b = divmod(n, NB)
            if n + 1 < NSU:
                if n >= 1:
                    sp.wait_ge(s("sk_tr"), n)
                load_cache("k", n + 1, kc[(n + 1) % 2])
            if n >= 3:
                sp.wait_ge(s("sattn_pv"), n - 2)
            load_cache("v", n, vc[n % 3])
            dma(vc[n % 3][0:NS, 4, :], v_d[NS * b:NS * b + NS, g * GW:(g + 1) * GW]).then_inc(s(f"vc_in{n % 3}"), 16)
            if n == 0:
                for j in range(4):
                    sp.wait_ge(s(f"attn_st{j}"), 16 * attn_n[-1][j])
                for j in range(3):
                    sp.wait_ge(s(f"a_st{j}"), 16 * AG)
                sp.wait_ge(s("attn_o"), NG * NTILE)
            if n % 3 == 0:
                t = n // 3
                if t >= 2:
                    sp.wait_ge(s("comb"), t - 1)
                load_combined(t)
            ga, c = divmod(n, 3)
            c0, w = CHUNK[c]
            if n >= 2:
                sp.wait_ge(s("a_split"), n - 1)
            dma(sga[n % 2][:, 0:w], a_d[ga, :, c0:c0 + w]).then_inc(s(f"a_in{n % 2}"), 16)
            if n == 4:
                load_w(NWIN + 1)
        for m, (n, ct, c) in enumerate(merges):
            c0, w = CHUNK[c]
            if m >= 2:
                sp.wait_ge(s("merge"), m - 1)
            else:
                sp.wait_ge(s("a_split"), AG * 3)
            dma(sga[m % 2][:, 0:w], sg_d[0, 2 * n + ct, :, c0:c0 + w]).then_inc(s(f"sg_in{m % 2}"), 16)
            dma(sgb[m % 2][:, 0:w], sg_d[1, 2 * n + ct, :, c0:c0 + w]).then_inc(s(f"sg_in{m % 2}"), 16)
            if m == 1:
                sp.wait_ge(s("sattn_stored"), 16 * sattn_stores)
                load_combined(ST)
            if m % 6 == 1 and m // 6 < NPROJ - 2:
                load_w(NWIN + 2 + m // 6)
            if m == 14:
                sp.wait_ge(s("w_split"), NWIN + NPROJ)
                load_wout(0)
                sp.wait_ge(s("bT_ready"), TILES)
                load_wout(3)
            if m == 20:
                sp.wait_ge(s("proj_mm"), 6 * 3)
                load_wout(1)
                load_wout(2)
        sp.wait_ge(s("proj_mm"), KT * 3)
        sp.wait_ge(s("merge"), KT * 3)
        dma(g2b, a["norm2_g"][0].partition_broadcast(P)).then_inc(s("rout_in"), 16)
        dma(wr[:, :, 0:NEG], a["w_group_router"][0].rearrange("(k p) c -> p k c", p=P)).then_inc(s("rout_in"), 16)
        dma(wr[:, :, NEG:RW], a["w_expert_router"][0].rearrange("(k p) g e -> p k (g e)", p=P)).then_inc(s("rout_in"), 16)
        dma(rbias[:, 0:NEG], a["b_group_router"][0].partition_broadcast(P)).then_inc(s("rout_in"), 16)
        dma(rbias[:, NEG:RW], a["b_expert_router"][0].rearrange("g e -> (g e)").partition_broadcast(P)).then_inc(s("rout_in"), 16)
        for t in range(TILES):
            if t >= 2:
                sp.wait_ge(s("h_ready"), t - 1)
            dst = xr[t % 2]
            if t == ST:
                dma(dst[0:NSAMP, :], a["x_sample"].rearrange("b s d -> (b s) d")).then_inc(s(f"xr_in{t % 2}"), 16)
                dma(dst[NSAMP:P, :], a["x_prompt"][0, 0:P - NSAMP, :]).then_inc(s(f"xr_in{t % 2}"), 16)
            else:
                dma(dst[:, :], a["x_prompt"][0, P * t:P * t + P, :]).then_inc(s(f"xr_in{t % 2}"), 16)

        sp.wait_ge(s("out_mm"), TILES)

        def load_chunk(kind, j, expert, slot6):
            if kind == "gu":
                w = a["w_gate" if j % 2 == 0 else "w_up"][0, bass.ds(expert, 1), :, :]
                src = w.rearrange("a (p k) f -> p (a k) f", k=KT)[:, 4 * (j // 2):4 * (j // 2) + 4, :]
                dst = eraw[:, slot6, :].rearrange("p (k f) -> p k f", f=DE)
            else:
                w = a["w_down"][0, bass.ds(expert, 1), :, :]
                src = w.rearrange("a (p k) f -> p (a k) f", k=4)[:, 2 * j:2 * j + 2, :]
                dst = eraw[:, slot6, :].rearrange("p (k f) -> p k f", f=D)
            dma(dst, src).then_inc(s(f"e_in{slot6}"), 16)

        def load_chunks(plan, b):
            for kind, j, off, expert in plan:
                if not isinstance(b, int) or 6 * b + off >= NRAW:
                    sp.wait_ge(s("e_split"), b * 6 + (off - NRAW + 1))
                load_chunk(kind, j, expert, off % NRAW)

        load_chunks(first_chunks(), 0)
        load_chunks(loop_chunks(1), 1)
        with sp.Fori(2, NE) as b:
            load_chunks(loop_chunks(b), b)
        load_chunks(last_chunks(), NE - 1)
        sp.wait_ge(s("table_ready"), 1)
        nover = sp.value_load(obe[0:1, OVER:OVER + 1], min_val=0, max_val=OVER)
        with sp.If(nover > 0):
            with sp.Fori(0, OVER) as j2:
                with sp.If(j2 < nover):
                    eo = sp.value_load(obe[0:1, bass.ds(j2, 1)], min_val=0, max_val=NE - 1)
                    load_chunks(over_chunks(eo), j2 + NE)
        sp.wait_ge(s("all_stored"), 1)
        for t in range(TILES):
            w = NSAMP if t == ST else P
            if t >= 3:
                sp.wait_ge(s("yo_ready"), t - 2)
            dma(yy[t % 3][0:w, :, :], y_d.rearrange("(t j) d -> t j d", j=2)[col0(t):col0(t) + w]).then_inc(s(f"yg_in{t % 3}"), 16)
        sp.wait_ge(s("cache_out"), 16 * len(pieces))
        for j in range(4):
            sp.wait_ge(s(f"k_st{j}"), 16 * kst[-1][j])
            sp.wait_ge(s(f"v_st{j}"), 16 * vst_n[-1][j])
        sp.wait_ge(s("vn_out"), 16)
        for j in range(2):
            sp.wait_ge(s(f"y_out{j}"), 16 * len(range(j, TILES, 2)))
    @block.tensor
    def _(pe):
        mm, tr = nc.tensor.matmul, nc.tensor.transpose
        unit = [0]

        def claim():
            if unit[0] >= 4:
                eng, count = readers[unit[0] - 4]
                pe.wait_ge(s(f"freed_{eng}"), count)
            unit[0] += 1
            return (unit[0] - 1) % 4

        def three(out, lhs, rhs, n):
            for k in range(n):
                mm(out, lhs[0](k), rhs[0](k), start=(k == 0), stop=False)
                mm(out, lhs[0](k), rhs[1](k), start=False, stop=False)
                last = mm(out, lhs[1](k), rhs[0](k), start=False, stop=(k == n - 1))
            return last

        def x_transposes(t):
            pe.wait_ge(s("xs_ready"), t + 1)
            if t >= 2:
                pe.wait_ge(s("xf_ready"), t - 1)
            else:
                pe.wait_ge(s("const_in"), 32)
            dst = pair(4 + 2 * (t % 2))
            for k in range(KT):
                last = tr(dst[:, k, :], xs[t % 2][:, P * k:P * k + P], ident)
            last.then_inc(s("x_T"), 1)

        def tok_unit(n, t):
            _, hi, lo = wslot(n)
            if t == 0:
                pe.wait_ge(s("w_split"), n + 1)
            b = claim()
            c0 = col0(t)
            three(bank(b, WB), [lambda k, v=v: v[:, k, c0:c0 + P] for v in xT],
                  [lambda k, v=v: v[:, k, :] for v in (hi, lo)], KT).then_inc(s("unit_mm"), 1)

        def feat_unit(n, ct, c, src=None, dst=None, nk=KT, k0=0):
            _, hi, lo = wslot(n)
            if ct == 0 and c == 0:
                pe.wait_ge(s("w_split"), n + 1)
            c0, w = CHUNK[c]
            src = src or xT
            out = dst if dst is not None else bank(claim(), w)
            return three(out, [lambda k, v=v: v[:, k0 + k, P * ct:P * ct + P] for v in (hi, lo)],
                         [lambda k, v=v: v[:, k, c0:c0 + w] for v in src], nk)

        x_transposes(0)
        for t in range(TILES):
            if t + 1 < TILES:
                x_transposes(t + 1)
            pe.wait_ge(s("xn_ready"), t + 1)
            tok_unit(0, t)
        for n in range(1, 7):
            for t in range(TILES):
                tok_unit(n, t)
        pe.wait_ge(s("gate_in"), 48)
        for g in range(AG):
            last = tr(pair(4)[:, g, :], wsp[:, g, :], ident)
        last.then_inc(s("ws_T"), 1)
        pe.wait_ge(s("spatial_ready"), 1)
        mm(ps[0:NSAMP, 6, 0:AG * NS].rearrange("p (g t) -> p g t", t=NS), cst[0:NS, CREP:CREP + NSAMP],
           wmT[0:NS, :, 0:NS], start=True, stop=True).then_inc(s("ws_rep"), 1)

        gate_n = [0]

        def gate_unit(m):
            g, c = divmod(m, 3)
            b = 4 + m % 4
            if m == 0:
                pe.wait_ge(s("vn_ready"), TILES)
                pe.wait_ge(s("spatial_ready"), 2)
            if m >= 4:
                pe.wait_ge(s("a_ready"), m - 3)
            c0, w = CHUNK[c]
            one = cst[0:1, CONE:CONE + P]
            tiles = CHUNK_T[c]
            at = col0(tiles[0]) - c0
            out = ps[:, b, at:w].rearrange("p (n t) -> p n t", t=P)
            mm(out, one, bsr[0:1, g:g + 1, :].to_broadcast([1, len(tiles), P]), start=True, stop=True)
            for i, t in enumerate(tiles):
                last = mm(out[:, i, :], vn[:, t, P * g:P * g + P], wmT[:, g, :], start=False, stop=True,
                          skip_group_check=True)
            if c == 2:
                out = ps[:, b, 0:NSAMP]
                mm(out.rearrange("p (n t) -> p n t", t=NS), one, bsr[0:1, g:g + 1, 0:NS].to_broadcast([1, NB, NS]),
                   start=True, stop=True)
                last = mm(out, vn[0:NSAMP, ST, P * g:P * g + P], wmS[0:NSAMP, g, :], start=False, stop=True,
                          skip_group_check=True)
            last.then_inc(s("gate_mm2"), 1)

        m = 0
        for n in range(7, 11):
            for ct in range(2):
                for c in range(3):
                    feat_unit(n, ct, c).then_inc(s("unit_mm"), 1)
                    if m:
                        gate_unit(m - 1)
                    m += 1
        gate_unit(m - 1)

        qk = [(n, t) for n in range(11, 17) for t in range(TILES)]

        def qk_transposes(i):
            pe.wait_ge(s("qn_ready"), i + 1)
            if i >= 2:
                pe.wait_ge(s("qk_T"), i - 1)
            else:
                pe.wait_ge(s("a_ready"), 24)
            for j in range(2):
                last = tr(ps[:, 4 + i % 2, P * j:P * j + P], qn[i % 4][:, P * j:P * j + P], ident)
            last.then_inc(s("qk_tr"), 1)

        for i, (n, t) in enumerate(qk):
            tok_unit(n, t)
            if i >= 3:
                qk_transposes(i - 3)
        for i in range(len(qk) - 3, len(qk)):
            qk_transposes(i)
        for n in range(17, 25):
            for ct in range(2):
                for c in range(3):
                    feat_unit(n, ct, c).then_inc(s("unit_mm"), 1)
        for eng, count in readers[-4:]:
            pe.wait_ge(s(f"freed_{eng}"), count)

        def scores(n):
            g, j = divmod(n, NTILE)
            nb = nblk(n)
            if n >= 2:
                pe.wait_ge(s("attn_exp"), n - 1)
            if n == 0:
                pe.wait_ge(s("qk_T"), 54)
            sc = ps[:, 2 * (n % 2):2 * (n % 2) + 2, 0:2 * nb * P].rearrange("p b (h k) -> p b h k", k=nb * P)
            mask = cbf[:, BPAIR:BPAIR + P] if g == 2 else cbf[:, BPO + (2 - nb) * P:BPO + 2 * P]
            for b in range(2):
                mm(ps[:, 2 * (n % 2) + b, 0:2 * nb * P].rearrange("p (h k) -> p h k", k=nb * P), identb,
                   mask.unsqueeze(1).to_broadcast([P, 2, nb * P]), start=True, stop=True)
            for b in range(2):
                for i in range(2):
                    pr = 2 * g + i
                    q = qT[64 * b:64 * b + 64, pr, :]
                    k = kT[64 * b:64 * b + 64, pr, :]
                    out = sc[:, b, i, :]
                    if g == 2:
                        for half in range(2):
                            r = 2 * j + half
                            rows = slice(64 * half, 64 * half + 64)
                            last = mm(out[rows, 64 * half:64 * half + 64], q[:, r:NPROMPT:16], k[:, r:NPROMPT:16],
                                      start=False, stop=True, skip_group_check=True)
                    else:
                        qa = qcols(q, g, j, 0)
                        for kb in range(nb):
                            last = mm(out[:, kb * P:kb * P + P], qa, qcols(k, g, j, kb - nb + 1), start=False,
                                      stop=True, skip_group_check=True)
            last.then_inc(s("attn_s"), 1)

        def p_transposes(n):
            nb = nblk(n)
            pe.wait_ge(s("attn_exp"), n + 1)
            if n >= 1:
                pe.wait_ge(s("attn_pt"), n)
            for i in range(NH * nb):
                last = tr(pair(4)[:, i, :], Eb[n % 2][:, i // nb, (i % nb) * P:(i % nb) * P + P], ident)
            last.then_inc(s("attn_tr"), 1)

        def pv(n):
            g, j = divmod(n, NTILE)
            nb = nblk(n)
            pe.wait_ge(s("attn_pt"), n + 1)
            pe.wait_ge(s(f"vg_in{n % 2}"), vg_count(n))
            if n >= 2:
                pe.wait_ge(s("attn_o"), n - 1)
            for sl in range(NH):
                head = 2 * (sl % 2) + sl // 2
                for kb in range(nb):
                    k = 0 if g == 2 else 2 - nb + kb
                    last = mm(ps[:, 6 + n % 2, HD * head:HD * head + HD], Pt[n % 2][:, nb * sl + kb, :],
                              vg[n % 2][:, k, HD * head:HD * head + HD], start=(kb == 0), stop=(kb == nb - 1))
            last.then_inc(s("attn_pv"), 1)

        NU = NG * NTILE
        for n in range(NU + 2):
            if n < NU:
                scores(n)
            if 1 <= n <= NU:
                p_transposes(n - 1)
            if n >= 2:
                pv(n - 2)
        pe.wait_ge(s("attn_o"), NU)
        offs = (BS0, BS1, BS2)

        def k_transposes(n):
            g, b = divmod(n, NB)
            pe.wait_ge(s(f"kc_in{n % 2}"), cache_count(n, 2, 0))
            if n >= 1:
                pe.wait_ge(s("sk_T"), n)
            for hp in range(2):
                for i in range(SKT[g]):
                    last = tr(ps[:, 4 + hp, P * i:P * i + P], kc[n % 2][:, i, P * hp:P * hp + P], ident)
            last.then_inc(s("sk_tr"), 1)

        def s_scores(n):
            g, b = divmod(n, NB)
            pe.wait_ge(s("sk_T"), n + 1)
            if n >= 2:
                pe.wait_ge(s("sattn_exp"), n - 1)
            nk = P * SKT[g]
            bk = 2 * (n % 2)
            parts = [(0, nk, ps[:, bk, 0:nk])]
            parts.append((nk, NS, ps[:, bk + (nk // 512), nk % 512:nk % 512 + NS]))
            for i, (k0, w, out) in enumerate(parts):
                mm(out, identb, cbf[:, offs[g] + k0:offs[g] + k0 + w], start=(i == 0 or nk == 512), stop=True,
                   skip_group_check=True)
            for hp in range(2):
                q = qpad[:, NB * (2 * g + hp) + b, :, :].rearrange("p a b -> p (a b)")
                for i, (k0, w, out) in enumerate(parts):
                    rhs = KTs[n % 2][:, hp, 0:nk] if i == 0 else kTs[:, 2 * g + hp, NS * b:NS * b + NS]
                    last = mm(out[64 * hp:64 * hp + 64, :], q, rhs, start=False, stop=True,
                              skip_group_check=True)
            last.then_inc(s("sattn_s"), 1)

        def s_tail(n):
            g, b = divmod(n, NB)
            pe.wait_ge(s("sattn_exp"), n + 1)
            if n >= 1:
                pe.wait_ge(s("sattn_pt"), n)
            for i in range(SKT[g]):
                tr(ps[:, 6, P * i:P * i + P], Es[n % 2][:, P * i:P * i + P], ident)
            nk = P * SKT[g]
            tr(ps[0:NS, 7, 0:P], Es[n % 2][:, nk:nk + NS], ident).then_inc(s("sattn_tr"), 1)

        def s_pv(n):
            g, b = divmod(n, NB)
            pe.wait_ge(s("sattn_pt"), n + 1)
            pe.wait_ge(s(f"vc_in{n % 3}"), cache_count(n, 3, 1))
            if n >= 1:
                pe.wait_ge(s("sattn_o"), n)
            for hd in range(NH):
                out = ps[32 * hd:32 * hd + 32, 7, P:P + HD]
                for i in range(SKT[g]):
                    mm(out, PTs[n % 2][:, i, 32 * hd:32 * hd + 32], vc[n % 3][:, i, HD * hd:HD * hd + HD],
                       start=(i == 0), stop=False)
                last = mm(out, PTs[n % 2][0:NS, 4, 32 * hd:32 * hd + 32], vc[n % 3][0:NS, 4, HD * hd:HD * hd + HD],
                          start=False, stop=True)
            last.then_inc(s("sattn_pv"), 1)

        def b_transposes(t):
            pe.wait_ge(s("comb"), t + 1)
            for j in range(2):
                last = tr(ps[:, 7, P * (j + 2):P * (j + 2) + P], cb[t % 2][:, 0, P * j:P * j + P], ident)
            last.then_inc(s("bT_tr"), 1)

        k_transposes(0)
        pe.wait_ge(s("qpad_ready"), 2)
        for n in range(NSU + 3):
            if n + 1 < NSU:
                k_transposes(n + 1)
            if n < NSU:
                s_scores(n)
            if 2 <= n < NSU + 2:
                s_pv(n - 2)
            for step, t in combine(n):
                if step == 2:
                    b_transposes(t)
            if 1 <= n <= NSU:
                s_tail(n - 1)
        pe.wait_ge(s("bT_ready"), NTILE)
        pe.wait_ge(s("a_split"), AG * 3)
        pe.wait_ge(s("sattn_o"), NSU)
        for m, (n, ct, c) in enumerate(merges):
            if m == 3:
                b_transposes(ST)
                pe.wait_ge(s("bT_ready"), TILES)
            if m >= 4:
                pe.wait_ge(s("merge"), m - 3)
            w = CHUNK[c][1]
            feat_unit(NWIN + n, ct, c, src=aT, dst=bank(m % 4, w))
            feat_unit(NWIN + n, ct, c, src=bT, dst=bank(4 + m % 4, w), nk=2, k0=KT).then_inc(s("proj_mm"), 1)
        def x2_transposes(t):
            pe.wait_ge(s("x2_ready"), t + 1)
            if t >= 1:
                pe.wait_ge(s("x2T_ready"), t)
            for k in range(KT):
                last = tr(pair(4)[:, k, :], x2[t % 2][:, P * k:P * k + P], ident)
            last.then_inc(s("x2_tr"), 1)

        def router(t):
            pe.wait_ge(s("x2T_ready"), t + 1)
            if t == 0:
                pe.wait_ge(s("rout_in"), 80)
            if t >= 1:
                pe.wait_ge(s("route_in"), t)
            for k in range(KT):
                last = mm(bank(6, RW), x2T[t % 2][:, k, :], wr[:, k, :], start=(k == 0), stop=(k == KT - 1))
            last.then_inc(s("rout_mm"), 1)

        for t in range(TILES):
            pe.wait_ge(s("m_split"), t + 1)
            if t >= 2:
                pe.wait_ge(s("h_ready"), t - 1)
            for half in range(2):
                if t == 0:
                    pe.wait_ge(s("w_split"), NSPLIT - 2 + 2 * half)
                last = three(bank(2 * (t % 2) + half), [lambda k, v=v: v[t % 2][:, k, :] for v in (mh, ml)],
                             [lambda k, v=v: v[:, k, 512 * half:512 * half + 512] for v in wo], KT)
            last.then_inc(s("out_mm"), 1)
            if t >= 1:
                x2_transposes(t - 1)
            if t >= 2:
                router(t - 2)
        router(TILES - 2)
        x2_transposes(TILES - 1)
        router(TILES - 1)
        pe.wait_ge(s("assign"), 1)
        pe.wait_ge(s("route_in"), TILES)
        ones = cbf[:, BONE:BONE + P]
        for t in range(TILES):
            out = ps[:, 0, NE * t:NE * t + NE]
            order = [ST] + list(range(NTILE))
            before = order[:order.index(t)]
            for b4 in before:
                mm(out, ones, Abf[:, b4, :], start=(b4 == before[0]), stop=False)
            last = mm(out, cbf[:, BLT:BLT + P], Abf[:, t, :], start=not before, stop=True)
        for t in range(TILES):
            last = mm(ps[0:NE, 1, 0:1], Abf[:, t, :], cbf[:, BONE:BONE + 1], start=(t == 0), stop=(t == TILES - 1))
        last.then_inc(s("count_mm"), 1)
        pe.wait_ge(s("over_cnt"), 1)
        mm(ps[:, 2, 0:NE], nbb[0:NE, 0:P], cbf[0:NE, BLS:BLS + NE], start=True, stop=True)
        mm(ps[:, 2, NE:2 * NE], nbb[0:NE, 0:P], cbf[0:NE, BLI:BLI + NE], start=True, stop=True).then_inc(s("over_mm"), 1)
        pe.wait_ge(s("onehot"), 1)
        for i in range(2 * TILES):
            last = mm(ps[:, 3, 0:SLOTB], in_row[:, i, :], num_col[:, i, :], start=(i == 0), stop=(i == 2 * TILES - 1))
        last.then_inc(s("tab_mm"), 1)
        pe.wait_ge(s("table_ready"), 1)

        def x_tr(b):
            pe.wait_ge(s("xg_in"), b * 16 + 16)
            for k in range(KT):
                last = tr(pair(0)[:, k, :], xg[:, k:D:KT], ident)
            last.then_inc(s("xg_tr"), 1)

        def gate_up(b, plan, cb_):
            pe.wait_ge(s("xgT"), b + 1)
            for kind, j, off, _ in plan:
                if kind == "gu":
                    pe.wait_ge(s("e_split"), cb_ * 6 + (off + 1))
                    hi, lo = (v[:, off % NSPL, :].rearrange("p (k f) -> p k f", f=DE) for v in (ehi, elo))
                    for k in range(4):
                        kk = 4 * (j // 2) + k
                        mm(bank(2 + j % 2), xgh[:, kk, :], hi[:, k, :], start=(kk == 0), stop=False)
                        mm(bank(2 + j % 2), xgh[:, kk, :], lo[:, k, :], start=False, stop=False)
                        last = mm(bank(2 + j % 2), xgl[:, kk, :], hi[:, k, :], start=False, stop=(kk == KT - 1))
                    last.then_inc(s("e_used"), 1)

        def h_tr(b):
            pe.wait_ge(s("hid"), b + 1)
            for k in range(4):
                last = tr(ps[:, 4, P * k:P * k + P], hid[:, k:DE:4], ident)
            last.then_inc(s("hid_tr"), 1)

        def down(b, plan, cb_, first=False):
            pe.wait_ge(s("hidT"), b + 1)
            if not first:
                pe.wait_ge(s("y_read"), b)
            for kind, j, off, _ in plan:
                if kind == "down":
                    pe.wait_ge(s("e_split"), cb_ * 6 + (off + 1))
                    hi, lo = (v[:, off % NSPL, :].rearrange("p (k f) -> p k f", f=D) for v in (ehi, elo))
                    for k in range(2):
                        for half in range(2):
                            kk, cols = 2 * j + k, slice(512 * half, 512 * half + 512)
                            mm(bank(5 + half), hTh[:, kk, :], hi[:, k, cols], start=(kk == 0), stop=False)
                            mm(bank(5 + half), hTh[:, kk, :], lo[:, k, cols], start=False, stop=False)
                            last = mm(bank(5 + half), hTl[:, kk, :], hi[:, k, cols], start=False, stop=(kk == 3))
                    last.then_inc(s("e_used"), 1)

        x_tr(0)
        gate_up(0, first_chunks(), 0)
        x_tr(1)
        h_tr(0)
        gate_up(1, loop_chunks(1), 1)
        x_tr(2)
        down(0, loop_chunks(1), 1, first=True)
        h_tr(1)
        with pe.Fori(2, NE - 1) as b:
            gate_up(b, loop_chunks(b), b)
            x_tr(b + 1)
            down(b - 1, loop_chunks(b), b)
            h_tr(b)
        gate_up(NE - 1, loop_chunks(NE - 1), NE - 1)
        down(NE - 2, loop_chunks(NE - 1), NE - 1)
        h_tr(NE - 1)
        down(NE - 1, last_chunks(), NE - 1)
        nover = pe.value_load(obe[0:1, OVER:OVER + 1], min_val=0, max_val=OVER)
        with pe.If(nover > 0):
            with pe.Fori(0, OVER) as j2:
                with pe.If(j2 < nover):
                    b = j2 + NE
                    x_tr(b)
                    gate_up(b, over_chunks(0), b)
                    h_tr(b)
                    down(b, over_chunks(0), b)

    @block.scalar
    def _(act):
        act_ = nc.scalar.activation
        own = Steps(act, s("act_own"))

        def w_hi(n):
            raw, hi, _ = wslot(n)
            if n < NWIN + NPROJ:
                act.wait_ge(s("w_in"), w_in_count(n))
            else:
                act.wait_ge(s(f"wout_in{(n - NWIN - NPROJ) // 2}"), 32)
            if n >= NWIN + NPROJ:
                act.wait_ge(s("proj_mm"), 6 * NPROJ)
            elif n - 2 >= NWIN:
                act.wait_ge(s("proj_mm"), 6 * (n - 2 - NWIN + 1))
            elif n >= 2:
                act.wait_ge(s("unit_mm"), last_unit[n - 2])
            act_(hi, raw, ACT.Copy).then_inc(s("w_hi"), 1)

        def norm1(t):
            act.wait_ge(s(f"x_in{t % 2}"), 16 * (t // 2 + 1 + (t == ST)))
            own.then_wait(act_(junk1, xin[t % 2], ACT.Square, accum_out=small[:, 0, t:t + 1]))
            if t == 0:
                act.wait_ge(s("const_in"), 32)
            act_(small[:, 1, t:t + 1], small[:, 0, t:t + 1], ACT.Sqrt, bias=eps, scale=1.0 / D).then_inc(s("sd1"), 1)

        def x_hi(t):
            act.wait_ge(s("xf_ready"), t + 1)
            w = NSAMP if t == ST else P
            act_(xT[0][:, :, col0(t):col0(t) + w], xfull[:, :, 0:w], ACT.Copy).then_inc(s("xh_ready"), 1)

        norm1(0)
        w_hi(0)
        seen = {"va": 0, "u": 0, "qk": 0, "g": 0}

        def qk_evac(k):
            act.wait_ge(s("qk_tr"), k + 1)
            g, t = divmod(k, TILES)
            src = ps[:, 4 + k % 2, 0:GW].rearrange("p (a b) -> p a b", b=P)
            full, samp = (qT, qTs) if g < NG else (kT, kTs)
            g %= NG
            if t == ST:
                act_(samp[:, 2 * g:2 * g + 2, :], src[:, :, 0:NSAMP], ACT.Copy).then_inc(s("qk_T"), 1)
            else:
                act_(full[:, 2 * g:2 * g + 2, P * t:P * t + P], src, ACT.Copy).then_inc(s("qk_T"), 1)

        def evac(i):
            un = units[i]
            n, kind = un[0], blocks[un[0]][0]
            if kind == "ga" and seen["g"] == 0:
                for j in range(6 * TILES - 3, 6 * TILES):
                    qk_evac(j)
            act.wait_ge(s("unit_mm"), i + 1)
            if kind == "v":
                act_(vn[:, un[1], WB * (n - 1):WB * n], bank(i % 4, WB), ACT.Gelu_apprx_tanh).then_inc(s("freed_act"), 1)
            elif kind == "va":
                k = seen["va"]
                seen["va"] += 1
                if k >= 4:
                    act.wait_ge(s(f"v_st{k % 4}"), 16 * vst_n[k - 4][k % 4])
                act_(vst[k % 4], bank(i % 4, WB), ACT.Copy).then_inc(s("freed_act"), 1)
                if n == 5:
                    t = un[1]
                    act.wait_ge(s("vss"), t + 1)
                    act_(small[:, 4, t:t + 1], small[:, 3, t:t + 1], ACT.Sqrt, bias=eps, scale=1.0 / D).then_inc(s("vsd"), 1)
            elif kind == "u":
                m, w = seen["u"], CHUNK[un[2]][1]
                seen["u"] += 1
                if m >= 3:
                    act.wait_ge(s("a_ready"), m - 2)
                act_(ug[m % 3][:, 0:w], bank(i % 4, w), ACT.Gelu_apprx_tanh).then_inc(s("freed_act"), 1)
            elif kind in ("q", "k"):
                k = seen["qk"]
                seen["qk"] += 1
                if k == 0:
                    act.wait_ge(s("a_ready"), 3 * AG)
                if k >= 2:
                    act.wait_ge(s("ss_ready"), k - 1)
                act_(sq[k % 2], bank(i % 4, WB), ACT.Square).then_inc(s("sq_ready"), 1)
                act.wait_ge(s("ss_ready"), k + 1)
                act_(stat[:, 2 + k % 2, :], stat[:, k % 2, :], ACT.Sqrt, bias=eps, scale=1.0 / HD).then_inc(s("sd_ready"), 1)
                if k >= 3:
                    qk_evac(k - 3)
            else:
                k, w = seen["g"], CHUNK[un[2]][1]
                seen["g"] += 1
                if k >= 4:
                    act.wait_ge(s(f"sg_st{k % 4}"), 16 * (k // 4))
                act_(sgs[k % 4][:, 0:w], bank(i % 4, w), ACT.Sigmoid).then_inc(s("freed_act"), 1)

        def mid(n):
            return 4 if blocks[n][0] in ("v", "va", "q", "k") else 2

        at = 0
        for i, un in enumerate(units):
            if i and units[i - 1][0] != un[0]:
                at = i
            if un[0] == 0:
                if i + 1 < TILES:
                    norm1(i + 1)
                x_hi(i)
                if i:
                    evac(i - 1)
            else:
                if i == TILES:
                    evac(i - 1)
                evac(i)
            if i - at == mid(un[0]) and un[0] + 1 < NWIN:
                w_hi(un[0] + 1)
        for j in range(4):
            act.wait_ge(s(f"sg_st{j}"), 16 * 12)
        for n in range(NG * NTILE):
            nk = nblk(n) * P
            act.wait_ge(s("nm_ready"), n + 1)
            if n >= 2:
                act.wait_ge(s("attn_tr"), n - 1)
            for sl in range(NH):
                head = 2 * (sl % 2) + sl // 2
                last = act_(Eb[n % 2][:, sl, 0:nk], ps[:, 2 * (n % 2) + sl // 2, nk * (sl % 2):nk * (sl % 2) + nk], ACT.Exp,
                            bias=nm[:, n % 2, sl:sl + 1], scale=SCALE, accum_out=ob[n % 4][:, head, HD:HD + 1])
            last.then_inc(s("attn_exp"), 1)
        def keys_T(n):
            nk = P * SKT[n // NB]
            act.wait_ge(s("sk_tr"), n + 1)
            if n >= 2:
                act.wait_ge(s("sattn_s"), n - 1)
            else:
                act.wait_ge(s("attn_s"), NG * NTILE)
            act_(KTs[n % 2][:, :, 0:nk], ps[:, 4:6, 0:nk], ACT.Copy).then_inc(s("sk_T"), 1)

        def group_weights(t):
            act.wait_ge(s("cd_ready"), t + 1)
            act_(cs[t % 2][:, 1:4, :], cs[t % 2][:, 1:4, :], ACT.Exp).then_inc(s("ce_ready"), 1)

        def b_hi(t):
            act.wait_ge(s("b_ready"), t + 1)
            w = NSAMP if t == ST else P
            act_(bT[0][:, :, col0(t):col0(t) + w], cb[t % 2][:, 1, :].rearrange("p (a b) -> p a b", b=P)[:, :, 0:w],
                 ACT.Copy).then_inc(s("bh_ready"), 1)

        keys_T(0)
        w_hi(NWIN)
        act.wait_ge(s("attn_pv"), NG * NTILE)
        for n in range(NSU + 3):
            if n + 1 < NSU:
                keys_T(n + 1)
            for step, t in combine(n):
                if step == 1:
                    group_weights(t)
                elif step == 3:
                    b_hi(t)
            if n < NSU:
                g, b = divmod(n, NB)
                nk = P * SKT[g]
                act.wait_ge(s("snm_ready"), n + 1)
                if n >= 2:
                    act.wait_ge(s("sattn_tr"), n - 1)
                act_(Es[n % 2][:, 0:nk + NS], flat(2 * (n % 2))[:, 0:nk + NS], ACT.Exp, bias=snm[:, n % 2:n % 2 + 1], scale=SCALE,
                     accum_out=osb[:, b * NG + g, HD:HD + 1]).then_inc(s("sattn_exp"), 1)
                ga, c = divmod(n, 3)
                c0, w = CHUNK[c]
                act.wait_ge(s(f"a_in{n % 2}"), 16 * (n // 2 + 1))
                act_(aT[0][:, ga, c0:c0 + w], sga[n % 2][:, 0:w], ACT.Copy).then_inc(s("a_hi"), 1)
        w_hi(NWIN + 1)
        group_weights(ST)
        b_hi(ST)
        for n in range(NWIN + 2, NSPLIT - 2):
            w_hi(n)

        def m_hi(t):
            if t == 0:
                act.wait_ge(s("merge"), 3 * KT)
            if t >= 2:
                act.wait_ge(s("out_mm"), t - 1)
            act_(mh[t % 2], mT[:, :, col0(t):col0(t) + P], ACT.Copy).then_inc(s("m_hi"), 1)

        def x2T_evac(t):
            act.wait_ge(s("x2_tr"), t + 1)
            if t >= 2:
                act.wait_ge(s("rout_mm"), t - 1)
            act_(x2T[t % 2], pair(4), ACT.Copy).then_inc(s("x2T_ready"), 1)

        m_hi(0)
        w_hi(NSPLIT - 2)
        w_hi(NSPLIT - 1)
        for t in range(TILES):
            if t + 1 < TILES:
                m_hi(t + 1)
            act.wait_ge(s("h_ready"), t + 1)
            own.then_wait(act_(junk3, hbuf[:, t, :], ACT.Square, accum_out=small[:, 0, t:t + 1]))
            act_(small[:, 1, t:t + 1], small[:, 0, t:t + 1], ACT.Sqrt, bias=eps, scale=1.0 / D).then_inc(s("sd2"), 1)
            if t >= 1:
                x2T_evac(t - 1)
        x2T_evac(TILES - 1)
        act.wait_ge(s("rt_diff"), 1)
        act_(R["d4"], R["d4"], ACT.Exp).then_inc(s("rt_exp"), 1)
        act.wait_ge(s("rt_diff"), 2)
        act_(R["ex"], R["ex"], ACT.Exp).then_inc(s("rt_exp"), 1)

        def c_hi(b, off, first=False):
            act.wait_ge(s(f"e_in{off % NRAW}"), b * 16 + 16 * chunk_uses(off))
            if not first:
                act.wait_ge(s("e_used"), b * 6 + (off - NSPL + 1))
            act_(ehi[:, off % NSPL, :], eraw[:, off % NRAW, :], ACT.Copy).then_inc(s("e_hi"), 1)

        def xg_hi(b):
            act.wait_ge(s("xg_tr"), b + 1)
            act_(xgh, pair(0), ACT.Copy).then_inc(s("xg_hi"), 1)

        def silu(b, used):
            act.wait_ge(s("e_used"), used)
            act_(sil, bank(2), ACT.Silu).then_inc(s("silu"), 1)

        def hid_hi(b):
            act.wait_ge(s("hid_tr"), b + 1)
            act_(hTh, ps[:, 4, :].rearrange("p (k n) -> p k n", n=P), ACT.Copy).then_inc(s("hid_hi"), 1)

        def y_evac(b, used, first=False):
            act.wait_ge(s("e_used"), used)
            if not first:
                act.wait_ge(s("y_st"), b * 16)
            act_(yb, flat(5)[:, 0:D], ACT.Copy).then_inc(s("y_read"), 1)

        act.wait_ge(s("x2_st0"), 16 * 5)
        act.wait_ge(s("x2_st1"), 16 * 4)
        for off in range(3):
            c_hi(0, off, first=True)
        xg_hi(0)
        c_hi(0, 3)
        c_hi(0, 4)
        silu(0, 4)
        xg_hi(1)
        c_hi(0, 5)
        c_hi(0, 6)
        hid_hi(0)

        def turn(b, bn, last=False):
            for off in (1, 2, 3, 4):
                c_hi(b, off)
            silu(b, b * 6 + 2)
            if not last:
                xg_hi(b + 1)
            c_hi(b, 5)
            if not last:
                c_hi(b, 6)
            y_evac(b - 1, b * 6 + 4, first=(bn == 1))
            hid_hi(b)

        turn(1, 1)
        with act.Fori(2, NE - 1) as b:
            turn(b, None)
        turn(NE - 1, None, last=True)
        y_evac(NE - 1, 6 * NE)
        act.wait_ge(s("table_ready"), 1)
        nover = act.value_load(obe[0:1, OVER:OVER + 1], min_val=0, max_val=OVER)
        with act.If(nover > 0):
            with act.Fori(0, OVER) as j2:
                with act.If(j2 < nover):
                    b = j2 + NE
                    xg_hi(b)
                    for off in range(6):
                        c_hi(b, off)
                    silu(b, b * 6 + 4)
                    hid_hi(b)
                    y_evac(b, b * 6 + 6)
        for t in range(TILES):
            act.wait_ge(s("yo_ready"), t + 1)
            if t == ST:
                dst, src = o["y_sample"].rearrange("b s d -> (b s) d"), yo[t % 2][0:NSAMP, :]
            else:
                dst, src = o["y_prompt"][0, P * t:P * t + P, :], yo[t % 2]
            act.dma_start(dst, src).then_inc(s(f"y_out{t % 2}"), 16)

    @block.vector
    def _(dve):
        v = nc.vector
        tt, stt, tsc, cp = v.tensor_tensor, v.scalar_tensor_tensor, v.tensor_scalar, v.tensor_copy
        own = Steps(dve, s("dve_own"))

        def w_lo(n):
            raw, hi, lo = wslot(n)
            dve.wait_ge(s("w_hi"), n + 1)
            tt(lo, raw, hi.bitcast(F32), ALU.subtract).then_inc(s("w_split"), 1)

        def scale_x(t):
            dve.wait_ge(s("sd1"), t + 1)
            own.then_wait(v.reciprocal(small[:, 2, t:t + 1], small[:, 1, t:t + 1]))
            if t >= 2:
                dve.wait_ge(s("x_T"), t - 1)
            tsc(xs[t % 2], xin[t % 2], small[:, 2, t:t + 1], None, ALU.mult).then_inc(s("xs_ready"), 1)

        def x_full(t):
            dve.wait_ge(s("x_T"), t + 1)
            if t >= 1:
                dve.wait_ge(s("xn_ready"), t)
            tt(xfull, pair(4 + 2 * (t % 2)), g1T[:, :].unsqueeze(2).to_broadcast([P, KT, P]), ALU.mult)\
                .then_inc(s("xf_ready"), 1)
            dve.wait_ge(s("xh_ready"), t + 1)
            w = NSAMP if t == ST else P
            cols = slice(col0(t), col0(t) + w)
            tt(xT[1][:, :, cols], xfull[:, :, 0:w], xT[0][:, :, cols].bitcast(F32), ALU.subtract).then_inc(s("xn_ready"), 1)

        def vnorm_sum(t):
            dve.wait_ge(s("freed_act"), 4 * TILES + t + 1)
            if t == 0:
                dve.wait_ge(s("gate_in"), 48)
            else:
                dve.wait_ge(s("vss"), t)
            v.tensor_tensor_reduce(junk2, vn[:, t, :], vn[:, t, :], 1.0, 0.0, ALU.mult, ALU.add,
                                   small[:, 3, t:t + 1]).then_inc(s("vss"), 1)

        def vnorm(t):
            dve.wait_ge(s("vsd"), t + 1)
            own.then_wait(v.reciprocal(small[:, 5, t:t + 1], small[:, 4, t:t + 1]))
            stt(vn[:, t, :], vn[:, t, :], small[:, 5, t:t + 1], gvb, ALU.mult, ALU.mult).then_inc(s("vn_ready"), 1)

        def gate(m):
            w = CHUNK[m % 3][1]
            dve.wait_ge(s("gate_mm2"), m + 1)
            dve.wait_ge(s("freed_act"), freed_u0 + m + 1)
            if m >= 3:
                dve.wait_ge(s(f"a_st{m % 3}"), 16 * (m // 3))
            tt(ast[m % 3][:, 0:w], ps[:, 4 + m % 4, 0:w], ug[m % 3][:, 0:w], ALU.mult).then_inc(s("a_ready"), 1)

        def qk_sum(k):
            dve.wait_ge(s("sq_ready"), k + 1)
            v.tensor_reduce(stat[:, k % 2, :], sq[k % 2].rearrange("p (h d) -> p h d", d=HD), AX.X, ALU.add)\
                .then_inc(s("ss_ready"), 1)

        def qk_norm(k, i):
            t = k % TILES
            out = qn[k % 4].rearrange("p (h d) -> p h d", d=HD)
            dve.wait_ge(s("sd_ready"), k + 1)
            own.then_wait(v.reciprocal(stat[:, 4 + k % 2, :], stat[:, 2 + k % 2, :]))
            if k >= 4:
                dve.wait_ge(s("qk_tr"), k - 3)
                if kst[k - 4][k % 4]:
                    dve.wait_ge(s(f"k_st{k % 4}"), 16 * kst[k - 4][k % 4])
            ins = tt(out, bank(i % 4, WB).rearrange("p (h d) -> p h d", d=HD),
                     stat[:, 4 + k % 2, :].unsqueeze(2).to_broadcast([P, NH, HD]), ALU.mult).then_inc(s("freed_dve"), 1)
            dve.wait_ge(s("freed_dve"), k + 1)
            own.then_wait(tt(out, out, qg[:, k // (3 * TILES):k // (3 * TILES) + 1, :].to_broadcast([P, NH, HD]), ALU.mult))
            a_, b_ = rt[k % 2]
            ct = cst[:, CROPEC + 16 * t:CROPEC + 16 * t + 16].unsqueeze(1).to_broadcast([P, NH, 16])
            st = cst[:, CROPES + 16 * t:CROPES + 16 * t + 16].unsqueeze(1).to_broadcast([P, NH, 16])
            own.done(tt(a_, out[:, :, 0:16], ct, ALU.mult))
            own.then_wait(tt(b_, out[:, :, 0:16], st, ALU.mult))
            own.then_wait(tt(out[:, :, 0:8], a_[:, :, 0:8], b_[:, :, 8:16], ALU.add))
            tt(out[:, :, 8:16], a_[:, :, 8:16], b_[:, :, 0:8], ALU.add).then_inc(s("qn_ready"), 1)

        dve.wait_ge(s("const_in"), 32)
        scale_x(0)
        w_lo(0)
        at, m, k = 0, 0, 0
        for i, un in enumerate(units):
            kind = blocks[un[0]][0]
            if i and units[i - 1][0] != un[0]:
                at = i
            if un[0] == 0:
                if i + 1 < TILES:
                    scale_x(i + 1)
                x_full(i)
            elif un[0] == 5:
                vnorm_sum(un[1])
                if un[1]:
                    vnorm(un[1] - 1)
            elif un[0] == 6 and un[1] == 0:
                vnorm(TILES - 1)
                dve.wait_ge(s("const2_in"), 32)
                dve.wait_ge(s("masks_in"), 16)
            elif kind == "u":
                if m == 0:
                    dve.wait_ge(s("ws_T"), 1)
                    tt(wmT, pair(4), cst[:, CTRIL:CTRIL + P].unsqueeze(1).to_broadcast([P, AG, P]), ALU.mult)\
                        .then_inc(s("spatial_ready"), 1)
                    dve.wait_ge(s("ws_rep"), 1)
                    tt(wmS[0:NSAMP, :, :].rearrange("p g (b t) -> p g b t", t=NS),
                       ps[0:NSAMP, 6, 0:AG * NS].rearrange("p (g t) -> p g t", t=NS).unsqueeze(2).to_broadcast([NSAMP, AG, NB, NS]),
                       cst[0:NSAMP, CBD:CBD + NB].unsqueeze(1).unsqueeze(3).to_broadcast([NSAMP, AG, NB, NS]), ALU.mult)\
                        .then_inc(s("spatial_ready"), 1)
                else:
                    gate(m - 1)
                m += 1
            elif kind in ("q", "k"):
                if k == 0:
                    gate(m - 1)
                qk_sum(k)
                if k:
                    qk_norm(k - 1, i - 1)
                k += 1
            elif kind == "ga" and at == i and un[0] == 17:
                qk_norm(k - 1, i - 1)
            if i - at == (4 if kind in ("v", "va", "q", "k") else 2) and un[0] + 1 < NWIN:
                w_lo(un[0] + 1)
        for j in range(4):
            dve.wait_ge(s(f"sg_st{j}"), 16 * 12)
        NU = NG * NTILE
        for n in range(NU + 2):
            if n < NU:
                nk = nblk(n) * P
                dve.wait_ge(s("attn_s"), n + 1)
                if n:
                    dve.wait_ge(s("nm_ready"), n)
                own.then_wait(v.tensor_reduce(stat[:, 0, :].rearrange("p (b i) -> p b i", i=2),
                                              ps[:, 2 * (n % 2):2 * (n % 2) + 2, 0:2 * nk].rearrange("p b (i k) -> p b i k", k=nk),
                                              AX.X, ALU.max))
                if n >= 4:
                    dve.wait_ge(s(f"attn_st{n % 4}"), 16 * attn_n[n - 4][n % 4])
                own.done(tsc(ob[n % 4][:, :, HD + 1].rearrange("p (i b) -> p b i", b=2),
                             stat[:, 0, :].rearrange("p (b i) -> p b i", i=2), SCALE, None, ALU.mult))
                if n >= 2:
                    dve.wait_ge(s("attn_exp"), n - 1)
                tsc(nm[:, n % 2, :], stat[:, 0, :], -SCALE, None, ALU.mult).then_inc(s("nm_ready"), 1)
            if 1 <= n <= NU:
                j = n - 1
                dve.wait_ge(s("attn_tr"), j + 1)
                if j >= 2:
                    dve.wait_ge(s("attn_pv"), j - 1)
                cp(Pt[j % 2][:, 0:NH * nblk(j), :], pair(4)[:, 0:NH * nblk(j), :]).then_inc(s("attn_pt"), 1)
            if n >= 2:
                j = n - 2
                dve.wait_ge(s("attn_pv"), j + 1)
                if j >= 4:
                    dve.wait_ge(s(f"attn_st{j % 4}"), 16 * attn_n[j - 4][j % 4])
                cp(ob[j % 4][:, :, 0:HD], ps[:, 6 + j % 2, 0:GW].rearrange("p (h d) -> p h d", d=HD)).then_inc(s("attn_o"), 1)
        dve.wait_ge(s("zeroed"), 1)
        for half in range(2):
            rows = slice(64 * half, 64 * half + 64)
            cp(qpad[rows, :, half, 0:NS], qTs[rows, :, :].rearrange("p a (b t) -> p (a b) t", t=NS))\
                .then_inc(s("qpad_ready"), 1)
        def weights_1(t):
            dve.wait_ge(s(f"comb_in{t % 2}"), 16 * (t // 2 + 1))
            mx = co[t % 2][:, :, HD + 1].rearrange("p (g h) -> p g h", h=NH)
            c_ = cs[t % 2]
            own.then_wait(v.tensor_reduce(c_[:, 0, :], mx.rearrange("p g h -> p h g"), AX.X, ALU.max))
            tt(c_[:, 1:4, :], mx, c_[:, 0:1, :].to_broadcast([P, NG, NH]), ALU.subtract).then_inc(s("cd_ready"), 1)

        def weights_2(t):
            den = co[t % 2][:, :, HD].rearrange("p (g h) -> p g h", h=NH)
            c_ = cs[t % 2]
            dve.wait_ge(s("ce_ready"), t + 1)
            own.then_wait(tt(c_[:, 4:7, :], c_[:, 1:4, :], den, ALU.mult))
            own.then_wait(v.tensor_reduce(c_[:, 0, :], c_[:, 4:7, :].rearrange("p g h -> p h g"), AX.X, ALU.add))
            own.then_wait(v.reciprocal(c_[:, 7, :], c_[:, 0, :]))
            own.then_wait(tt(c_[:, 1:4, :], c_[:, 1:4, :], c_[:, 7:8, :].to_broadcast([P, NG, NH]), ALU.mult))
            own.then_wait(tt(cb[t % 2].rearrange("p g (h d) -> p g h d", d=HD),
                             co[t % 2][:, :, 0:HD].rearrange("p (g h) d -> p g h d", h=NH),
                             c_[:, 1:4, :].unsqueeze(3).to_broadcast([P, NG, NH, HD]), ALU.mult))
            own.then_wait(tt(cb[t % 2][:, 0, :], cb[t % 2][:, 0, :], cb[t % 2][:, 1, :], ALU.add))
            tt(cb[t % 2][:, 0, :], cb[t % 2][:, 0, :], cb[t % 2][:, 2, :], ALU.add).then_inc(s("comb"), 1)

        def b_copy(t):
            dve.wait_ge(s("bT_tr"), t + 1)
            cp(cb[t % 2][:, 1, :], ps[:, 7, 2 * P:4 * P]).then_inc(s("b_ready"), 1)

        def b_lo(t):
            dve.wait_ge(s("bh_ready"), t + 1)
            w = NSAMP if t == ST else P
            cols = slice(col0(t), col0(t) + w)
            tt(bT[1][:, :, cols], cb[t % 2][:, 1, :].rearrange("p (a b) -> p a b", b=P)[:, :, 0:w],
               bT[0][:, :, cols].bitcast(F32), ALU.subtract).then_inc(s("bT_ready"), 1)

        w_lo(NWIN)
        for n in range(NSU + 3):
            if n < NSU:
                g, b = divmod(n, NB)
                nk = P * SKT[g]
                mx1 = stat[:, 1, n % 2:n % 2 + 1]
                dve.wait_ge(s("sattn_s"), n + 1)
                if n:
                    dve.wait_ge(s("snm_ready"), n)
                own.then_wait(v.tensor_reduce(mx1, flat(2 * (n % 2))[:, 0:nk + NS], AX.X, ALU.max))
                if n >= 2:
                    dve.wait_ge(s("sattn_exp"), n - 1)
                tsc(snm[:, n % 2:n % 2 + 1], mx1, -SCALE, None, ALU.mult).then_inc(s("snm_ready"), 1)
                own.done(tsc(osb[:, b * NG + g, HD + 1:HD + 2], mx1, SCALE, None, ALU.mult))
            if 1 <= n <= NSU:
                j = n - 1
                g, b = divmod(j, NB)
                dve.wait_ge(s("sattn_tr"), j + 1)
                if j >= 2:
                    dve.wait_ge(s("sattn_pv"), j - 1)
                own.done(cp(PTs[j % 2][:, 0:SKT[g], :], ps[:, 6, 0:P * SKT[g]].rearrange("p (a b) -> p a b", b=P)))
                cp(PTs[j % 2][0:NS, 4, :], ps[0:NS, 7, 0:P]).then_inc(s("sattn_pt"), 1)
            if 2 <= n < NSU + 2:
                j = n - 2
                g, b = divmod(j, NB)
                dve.wait_ge(s("sattn_pv"), j + 1)
                for step, t in combine(n):
                    if step == 2:
                        b_copy(t)
                cp(osb[:, b * NG + g, 0:HD], ps[:, 7, P:P + HD]).then_inc(s("sattn_o"), 1)
            if n < NSU:
                ga, c = divmod(n, 3)
                c0, w = CHUNK[c]
                dve.wait_ge(s("a_hi"), n + 1)
                tt(aT[1][:, ga, c0:c0 + w], sga[n % 2][:, 0:w], aT[0][:, ga, c0:c0 + w].bitcast(F32), ALU.subtract)\
                    .then_inc(s("a_split"), 1)
            for step, t in combine(n):
                if step == 0:
                    weights_1(t)
                elif step == 1:
                    weights_2(t)
                elif step == 3:
                    b_lo(t)
        w_lo(NWIN + 1)
        weights_1(ST)
        weights_2(ST)
        b_copy(ST)
        b_lo(ST)
        for m, (n, ct, c) in enumerate(merges):
            c0, w = CHUNK[c]
            dve.wait_ge(s(f"sg_in{m % 2}"), 32 * (m // 2 + 1))
            dve.wait_ge(s("proj_mm"), m + 1)
            ga, gb = sga[m % 2][:, 0:w], sgb[m % 2][:, 0:w]
            own.done(tt(ga, ga, bank(m % 4, w), ALU.mult))
            own.then_wait(tt(gb, gb, bank(4 + m % 4, w), ALU.mult))
            tt(mT[:, 2 * n + ct, c0:c0 + w], ga, gb, ALU.add).then_inc(s("merge"), 1)
            if m % 6 == 5 and n < NPROJ - 2:
                w_lo(NWIN + 2 + n)
        w_lo(NSPLIT - 4)
        w_lo(NSPLIT - 3)

        def m_lo(t):
            dve.wait_ge(s("m_hi"), t + 1)
            tt(ml[t % 2], mT[:, :, col0(t):col0(t) + P], mh[t % 2].bitcast(F32), ALU.subtract).then_inc(s("m_split"), 1)

        def logits(t):
            dve.wait_ge(s("rout_mm"), t + 1)
            tt(lgt[:, t, :], bank(6, RW), rbias, ALU.add).then_inc(s("route_in"), 1)

        m_lo(0)
        w_lo(NSPLIT - 2)
        w_lo(NSPLIT - 1)
        dve.wait_ge(s("rout_in"), 80)
        for t in range(TILES):
            if t + 1 < TILES:
                m_lo(t + 1)
            dve.wait_ge(s("out_mm"), t + 1)
            dve.wait_ge(s(f"xr_in{t % 2}"), 16 * (t // 2 + 1 + (t == ST)))
            tt(hbuf[:, t, :], flat(2 * (t % 2)), xr[t % 2], ALU.add).then_inc(s("h_ready"), 1)
            dve.wait_ge(s("sd2"), t + 1)
            own.then_wait(v.reciprocal(small[:, 2, t:t + 1], small[:, 1, t:t + 1]))
            if t >= 2:
                dve.wait_ge(s("x2_tr"), t - 1)
                dve.wait_ge(s(f"x2_st{t % 2}"), 16 * (t // 2))
            stt(x2[t % 2], hbuf[:, t, :], small[:, 2, t:t + 1], g2b, ALU.mult, ALU.mult).then_inc(s("x2_ready"), 1)
            if t >= 2:
                logits(t - 2)
        logits(TILES - 2)
        logits(TILES - 1)

        dve.wait_ge(s("route_in"), TILES)
        step = own.then_wait
        bc = lambda x, w: x.to_broadcast([P, TILES, w])
        lg, le = lgt[:, :, 0:NEG], lgt[:, :, NEG:RW].rearrange("p t (g e) -> p t g e", e=EGE)
        code4 = cst[:, CCODE4:CCODE4 + NEG].unsqueeze(1).to_broadcast([P, TILES, NEG])
        code8 = cst[:, CCODE8:CCODE8 + EGE].unsqueeze(1).to_broadcast([P, TILES, EGE])
        red = lambda out, x, op: step(v.tensor_reduce(out[:, :, 0] if len(out.shape) == 3 and out.shape[2] == 1 else out, x, AX.X, op))

        def first_of(x, best, code, tmp, top, onehot, w):
            red(best, x, ALU.max)
            step(tt(tmp, x, bc(best, w), ALU.is_equal))
            step(tt(tmp, tmp, code, ALU.mult))
            red(top, tmp, ALU.max)
            step(tt(onehot, tmp, bc(top, w), ALU.is_equal))

        first_of(lg, R["m4"], code4, R["eq4"], R["c4"], R["oh4"], NEG)
        tt(R["d4"], lg, bc(R["m4"], NEG), ALU.subtract).then_inc(s("rt_diff"), 1)
        step(tt(prod48, le, R["oh4"].unsqueeze(3).to_broadcast([P, TILES, NEG, EGE]), ALU.mult))
        red(R["sel"], prod48.rearrange("p t g e -> p t e g"), ALU.add)
        first_of(R["sel"], R["m1"], code8, R["t8"], R["c8"], R["oh1"], EGE)
        step(stt(R["le2"], R["oh1"], -BIG, R["sel"], ALU.mult, ALU.add))
        first_of(R["le2"], R["m2"], code8, R["t8"], R["c8"], R["oh2"], EGE)
        tt(R["ex"], R["m2"], R["m1"], ALU.subtract).then_inc(s("rt_diff"), 1)
        for n, oh in (("E1", "oh1"), ("E2", "oh2")):
            step(tt(R[n].rearrange("p t (g e) -> p t g e", e=EGE), R["oh4"].unsqueeze(3).to_broadcast([P, TILES, NEG, EGE]),
                    R[oh].unsqueeze(2).to_broadcast([P, TILES, NEG, EGE]), ALU.mult))
        step(tt(R["A"], R["E1"], R["E2"], ALU.add))
        valid = cst[:, CVALID:CVALID + TILES].unsqueeze(2).to_broadcast([P, TILES, NE])
        tt(Abf, R["A"], valid, ALU.mult).then_inc(s("assign"), 1)
        dve.wait_ge(s("rt_exp"), 1)
        red(R["s4"], R["d4"], ALU.add)
        step(v.reciprocal(R["pg"], R["s4"]))
        dve.wait_ge(s("rt_exp"), 2)
        step(tsc(R["dn"], R["ex"], 1.0, None, ALU.add))
        step(v.reciprocal(R["dn"], R["dn"]))
        step(tt(wts[:, :, 0:1], R["pg"], R["dn"], ALU.mult))
        step(tt(wts[:, :, 1:2], wts[:, :, 0:1], R["ex"], ALU.mult))
        def c_lo(b, off):
            dve.wait_ge(s("e_hi"), b * 6 + (off + 1))
            tt(elo[:, off % NSPL, :], eraw[:, off % NRAW, :], ehi[:, off % NSPL, :].bitcast(F32), ALU.subtract)\
                .then_inc(s("e_split"), 1)

        dve.wait_ge(s("count_mm"), 1)
        step(cp(cnt[0:NE, 0:1], ps[0:NE, 1, 0:1]))
        step(tt(nbt[0:NE, :], cst[0:NE, CTHR:CTHR + 8], cnt[0:NE, 0:1].to_broadcast([NE, 8]), ALU.is_lt))
        step(v.tensor_reduce(cnt[0:NE, 1:2], nbt[0:NE, :], AX.X, ALU.add))
        cp(nbb[0:NE, :], cnt[0:NE, 1:2].to_broadcast([NE, P])).then_inc(s("over_cnt"), 1)
        step(cp(R["rank"], ps[:, 0, 0:TILES * NE].rearrange("p (t e) -> p t e", e=NE)))
        step(tsc(R["over"], R["rank"], float(P), None, ALU.is_ge))
        dve.wait_ge(s("over_mm"), 1)
        step(cp(ovl, ps[:, 2, 0:2 * NE].rearrange("p (a e) -> p a e", e=NE)))
        e128 = cst[:, CE128:CE128 + NE]
        step(tsc(obase, ovl[:, 0, :], float(P), float((NE - 1) * P), ALU.mult, ALU.add))
        step(tt(obase, obase, e128, ALU.subtract))
        over_b = obase.unsqueeze(1).to_broadcast([P, TILES, NE])
        step(tt(R["pos"], R["over"], over_b, ALU.mult))
        step(tt(R["pos"], R["pos"], R["rank"], ALU.add))
        step(tt(R["pos"], R["pos"], e128.unsqueeze(1).to_broadcast([P, TILES, NE]), ALU.add))
        for j, n in enumerate(("E1", "E2")):
            step(tt(R["pr"], R[n], R["pos"], ALU.mult))
            step(v.tensor_reduce(R["sl"][:, :, j], R["pr"], AX.X, ALU.add))
        step(cp(sloti, R["sl"]))
        step(tsc(rowi, sloti, P - 1, None, ALU.bitwise_and))
        step(tsc(blki, sloti, 7, None, ALU.logical_shift_right))
        step(cp(R["rowf"], rowi))
        step(cp(R["blkf"], blki))
        each = lambda y, w: y.rearrange("p t j -> p (t j)").unsqueeze(2).to_broadcast([P, 2 * TILES, w])
        iota = lambda w: cst[:, CIOTA:CIOTA + w].unsqueeze(1).to_broadcast([P, 2 * TILES, w])
        own.done(tt(in_row, iota(P), each(R["rowf"], P), ALU.is_equal))
        step(tt(in_col, iota(SLOTB), each(R["blkf"], SLOTB), ALU.is_equal))
        tt(num_col, in_col, cst[:, CID:CID + 2 * TILES].unsqueeze(2).to_broadcast([P, 2 * TILES, SLOTB]), ALU.mult)\
            .then_inc(s("onehot"), 1)
        step(tt(cmpo, ovl[:, 1:2, :].to_broadcast([P, OVER, NE]),
                cst[:, CBLK:CBLK + OVER].unsqueeze(2).to_broadcast([P, OVER, NE]), ALU.is_lt))
        step(v.tensor_reduce(obf[:, 0:OVER], cmpo, AX.X, ALU.add))
        step(tsc(obf[:, 0:OVER], obf[:, 0:OVER], float(NE - 1), None, ALU.min))
        step(cp(obf[:, OVER:OVER + 1], ovl[:, 1, NE - 1:NE]))
        dve.wait_ge(s("x2_st0"), 16 * 5)
        dve.wait_ge(s("x2_st1"), 16 * 4)
        c_lo(0, 0)
        dve.wait_ge(s("tab_mm"), 1)
        step(tsc(tabs[:, :], ps[:, 3, 0:SLOTB], float(EMPTY), None, ALU.add))
        step(tsc(tabt[:, :], tabs[:, :], 1, None, ALU.logical_shift_right))
        cp(obe[:, 0:OVER + 1], obf[:, 0:OVER + 1]).then_inc(s("table_ready"), 1)

        def xg_lo(b):
            dve.wait_ge(s("xg_hi"), b + 1)
            tt(xgl, pair(0), xgh.bitcast(F32), ALU.subtract).then_inc(s("xgT"), 1)

        def hidden(b):
            dve.wait_ge(s("silu"), b + 1)
            tt(hid, sil, bank(3), ALU.mult).then_inc(s("hid"), 1)

        def hid_lo(b):
            dve.wait_ge(s("hid_hi"), b + 1)
            tt(hTl, ps[:, 4, :].rearrange("p (k n) -> p k n", n=P), hTh.bitcast(F32), ALU.subtract).then_inc(s("hidT"), 1)

        c_lo(0, 1)
        c_lo(0, 2)
        xg_lo(0)
        c_lo(0, 3)
        c_lo(0, 4)
        hidden(0)
        xg_lo(1)
        c_lo(0, 5)
        c_lo(0, 6)
        hid_lo(0)

        def turn(b, last=False):
            for off in (1, 2, 3, 4):
                c_lo(b, off)
            hidden(b)
            if not last:
                xg_lo(b + 1)
            c_lo(b, 5)
            if not last:
                c_lo(b, 6)
            hid_lo(b)

        with dve.Fori(1, NE - 1) as b:
            turn(b)
        turn(NE - 1, last=True)
        nover = dve.value_load(obe[0:1, OVER:OVER + 1], min_val=0, max_val=OVER)
        with dve.If(nover > 0):
            with dve.Fori(0, OVER) as j2:
                with dve.If(j2 < nover):
                    b = j2 + NE
                    xg_lo(b)
                    for off in range(6):
                        c_lo(b, off)
                    hidden(b)
                    hid_lo(b)
        for t in range(TILES):
            dve.wait_ge(s(f"yg_in{t % 3}"), 16 * (t // 3 + 1))
            if t >= 2:
                dve.wait_ge(s(f"y_out{t % 2}"), 16 * (t // 2))
            w = NSAMP if t == ST else P
            out, (ya, yc) = yo[t % 2][0:w, :], (yy[t % 3][0:w, j, :] for j in range(2))
            own.then_wait(stt(out, ya, wts[0:w, t, 0:1], hbuf[0:w, t, :], ALU.mult, ALU.add))
            stt(out, yc, wts[0:w, t, 1:2], out, ALU.mult, ALU.add).then_inc(s("yo_ready"), 1)

    @block.gpsimd
    def _(pool):
        dma = nc.gpsimd.dma_start
        dma(cbf[:, :], a["c_bf16"]).then_inc(s("masks_in"), 16)

        def window_store(kv, g, t, src, sm):
            w = DIL[g][0]
            if t == ST:
                keep = SKEEP[g]
                dst = o[f"sample_{kv}_w{w}"][0, :, keep - NS:keep].rearrange("b t h d -> b t (h d)")
                dma(dst, src[0:NSAMP, :]).then_inc(s(sm), 16)
            elif kept(g, t):
                r = P * t - (NPROMPT - KEEP[g])
                dma(o[f"prompt_{kv}_w{w}"][0, 0, r:r + P].rearrange("t h d -> t (h d)"), src).then_inc(s(sm), 16)

        for k in range(NG * TILES):
            g, t = divmod(k, TILES)
            pool.wait_ge(s("freed_act"), k + 1 + (4 * TILES if g else 0))
            w = NSAMP if t == ST else P
            dma(v_d[col0(t):col0(t) + w, g * GW:(g + 1) * GW], vst[k % 4][0:w, :]).then_inc(s(f"v_st{k % 4}"), 16)
            window_store("v", g, t, vst[k % 4], f"v_st{k % 4}")
        pool.wait_ge(s("vn_ready"), TILES)
        dma(o["state_sgu_v_sample"][0].rearrange("b t c -> (b t) c"), vn[0:NSAMP, ST, :]).then_inc(s("vn_out"), 16)
        for m in range(3 * AG):
            g, c = divmod(m, 3)
            c0, w = CHUNK[c]
            pool.wait_ge(s("a_ready"), m + 1)
            dma(a_d[g, :, c0:c0 + w], ast[m % 3][:, 0:w]).then_inc(s(f"a_st{m % 3}"), 16)
        for k in range(NG * TILES, 2 * NG * TILES):
            g, t = k // TILES - NG, k % TILES
            if kept(g, t):
                pool.wait_ge(s("qn_ready"), k + 1)
                window_store("k", g, t, qn[k % 4], f"k_st{k % 4}")
        for k in range(48):
            i, c = divmod(k, 3)
            c0, w = CHUNK[c]
            pool.wait_ge(s("freed_act"), freed_g0 + k + 1)
            dma(sg_d[i // KT, i % KT, :, c0:c0 + w], sgs[k % 4][:, 0:w]).then_inc(s(f"sg_st{k % 4}"), 16)
        pool.wait_ge(s("unit_mm"), len(units))
        nc.gpsimd.memset(qpad, 0.0).then_inc(s("zeroed"), 1)
        for n in range(NG * NTILE):
            g, j = divmod(n, NTILE)
            pool.wait_ge(s("attn_o"), n + 1)
            rows = value_rows(g, j)
            rows = rows if g == 2 else rows[-1:]
            for i, (f, _) in enumerate(rows):
                part = slice(64 * i, 64 * i + 64) if g == 2 else slice(0, P)
                dma(f(ao_d[NSAMP:T, g].rearrange("t h c -> t (h c)")), ob[n % 4][part].rearrange("p h c -> p (h c)"))\
                    .then_inc(s(f"attn_st{n % 4}"), 16)
        for g in range(NG):
            pool.wait_ge(s("sattn_o"), (g + 1) * NB)
            for hd in range(NH):
                src = osb[32 * hd:32 * hd + NS, :, :].rearrange("p (b g) c -> p b g c", g=NG)
                dst = ao_d[0:NSAMP, g, hd, :].rearrange("(b t) c -> t b c", t=NS)
                dma(dst, src[:, :, g, :]).then_inc(s("sattn_stored"), 16)
        for t in range(TILES):
            pool.wait_ge(s("x2_ready"), t + 1)
            w = NSAMP if t == ST else P
            dma(xn_d[col0(t):col0(t) + w, :], x2[t % 2][0:w, :]).then_inc(s(f"x2_st{t % 2}"), 16)
        pool.wait_ge(s("x2_st0"), 16 * 5)
        pool.wait_ge(s("x2_st1"), 16 * 4)
        pool.wait_ge(s("route_in"), TILES)
        nc.gpsimd.memset(xg, 0.0).then_inc(s("zeroed"), 1)
        pool.wait_ge(s("zeroed"), 2)
        pool.wait_ge(s("table_ready"), 1)

        def gather(b, k):
            nc.gpsimd.tensor_copy(idxc[:, 0:1], tabt[:, bass.ds(b, 1)]).then_inc(s("idx_ready"), 1)
            pool.wait_ge(s("idx_ready"), k + 1)
            pool.sem_inc(s("index_used"), 1)
            pool.indirect_dma_start(xg, None, xn_d, bass.IndirectOffsetOnAxis(ap=idxc[:, 0:1], axis=0),
                                    bounds_check=T - 1, oob_is_err=False).then_inc(s("xg_in"), 16)

        def store(b, k):
            pool.wait_ge(s("y_read"), b + 1)
            nc.gpsimd.tensor_copy(idxy[:, 0:1], tabs[:, bass.ds(b, 1)]).then_inc(s("idx_ready"), 1)
            pool.wait_ge(s("idx_ready"), k + 1)
            pool.sem_inc(s("index_used"), 1)
            pool.indirect_dma_start(y_d, bass.IndirectOffsetOnAxis(ap=idxy[:, 0:1], axis=0), yb, None,
                                    bounds_check=2 * T - 1, oob_is_err=False).then_inc(s("y_st"), 16)

        gather(0, 0)
        for b in range(1, 3):
            pool.wait_ge(s("xg_tr"), b)
            gather(b, b)
        with pool.Fori(3, NE) as b:
            pool.wait_ge(s("xg_tr"), b)
            gather(b, b * 2 - 3)
            store(b - 3, b * 2 - 2)
        for i in range(3):
            store(NE - 3 + i, 2 * NE - 3 + i)
        nover = pool.value_load(obe[0:1, OVER:OVER + 1], min_val=0, max_val=OVER)
        with pool.If(nover > 0):
            with pool.Fori(0, OVER) as j2:
                with pool.If(j2 < nover):
                    b = j2 + NE
                    pool.wait_ge(s("xg_tr"), b)
                    gather(b, j2 * 2 + 2 * NE)
                    store(b, j2 * 2 + 2 * NE + 1)
                    pool.wait_ge(s("y_st"), j2 * 16 + 16 * (NE + 1))
        pool.wait_ge(s("y_st"), 16 * NE)
        pool.sem_inc(s("all_stored"), 1)


_INS = ["x_prompt", "x_sample", "cache_k_w128", "cache_v_w128", "cache_k_w512", "cache_v_w512", "cache_k_w2048",
        "cache_v_w2048", "norm1_g", "w_in", "v_norm_g", "w_spatial", "b_spatial", "q_norm_g", "k_norm_g", "w_proj_a",
        "w_proj_b", "w_out", "norm2_g", "w_group_router", "b_group_router", "w_expert_router", "b_expert_router",
        "w_gate", "w_up", "w_down"]
_OUTS = [("y_prompt", (1, NPROMPT, D)), ("y_sample", (NB, NS, D))]
_OUTS += [(f"prompt_{kv}_w{DIL[g][0]}", (1, 1, KEEP[g], NH, HD)) for g in range(NG) for kv in "kv"]
_OUTS += [(f"sample_{kv}_w{DIL[g][0]}", (1, NB, SKEEP[g], NH, HD)) for g in range(NG) for kv in "kv"]
_OUTS += [("state_sgu_v_sample", (1, NB, NS, D))]


def kernel(**inputs):
    import concourse.bacc as bacc
    from concourse.bass_utils import run_bass_kernel_spmd

    nc = bacc.Bacc("TRN2", target_bir_lowering=False, num_devices=1)
    arrays, a, o = {}, {}, {}
    given = {n: np.ascontiguousarray(inputs[n]) for n in _INS}
    given.update(constants())
    for n, x in given.items():
        arrays[n] = x
        a[n] = nc.dram_tensor(n, x.shape, mybir.dt.from_np(x.dtype), kind="ExternalInput").ap()
    for n, shape in _OUTS:
        o[n] = nc.dram_tensor("out_" + n, shape, F32, kind="ExternalOutput").ap()
    build(nc, a, o)
    r = run_bass_kernel_spmd(nc, [arrays], core_ids=[0])
    return tuple(r.results[0]["out_" + n] for n, _ in _OUTS)
```
